# Optimizing a Trainium2 kernel written in Bass

```python
import jax, jax.numpy as jnp
from jax import lax
import numpy as np
import math

D_MODEL = 1024
BATCH = 1
SEQ = 512
DEPTH = 2

CHUNK = 64
LN_EPS = 1e-5
GMLP_HEADS = 4
GMLP_WIDTH = D_MODEL
GMLP_HEAD_DIM = GMLP_WIDTH // GMLP_HEADS
GMLP_BLOCK = 128
POOL_WINDOWS = (2, 4, 8, 16)
POOL_GROUPS = len(POOL_WINDOWS)
POOL_WIDTH = D_MODEL
POOL_GROUP_DIM = POOL_WIDTH // POOL_GROUPS
EVEN_IN = 3 * GMLP_WIDTH + 2 * POOL_WIDTH
EVEN_MIX = GMLP_WIDTH + POOL_WIDTH
MLA_HEADS = 16
MLA_NOPE = 128
MLA_ROPE = 64
MLA_V = 128
MLA_Q_RANK = 256
MLA_KV_RANK = 128
MLA_WIDTH = MLA_HEADS * MLA_V
ODD_IN = MLA_Q_RANK + MLA_KV_RANK + MLA_ROPE + MLA_WIDTH
ROPE_THETA = 10000.0
Q_BLOCK = 128
ATTN_SCALE = (MLA_NOPE + MLA_ROPE) ** -0.5
DEEPNORM_ALPHA = (2.0 * DEPTH) ** 0.25
DEEPNORM_BETA = (8.0 * DEPTH) ** -0.25
N_EVEN = (DEPTH + 1) // 2
N_ODD = DEPTH // 2


def layer_norm(x, g, b):
    xf = x.astype(jnp.float32)
    mu = jnp.mean(xf, axis=-1, keepdims=True)
    var = jnp.mean(jnp.square(xf - mu), axis=-1, keepdims=True)
    return ((xf - mu) * lax.rsqrt(var + LN_EPS) * g + b).astype(x.dtype)

def rms_norm(x, g):
    xf = x.astype(jnp.float32)
    ms = jnp.mean(jnp.square(xf), axis=-1, keepdims=True)
    return (xf * lax.rsqrt(ms + LN_EPS) * g).astype(x.dtype)

def rope_cos_sin(positions):
    inv = 1.0 / (ROPE_THETA ** (jnp.arange(0, MLA_ROPE, 2, dtype=jnp.float32) / MLA_ROPE))
    ang = positions.astype(jnp.float32)[..., None] * inv
    return jnp.cos(ang), jnp.sin(ang)

def apply_rope(x, cos, sin):
    half = x.shape[-1] // 2
    x1 = x[..., :half].astype(jnp.float32)
    x2 = x[..., half:].astype(jnp.float32)
    return jnp.concatenate([x1 * cos - x2 * sin, x2 * cos + x1 * sin], axis=-1).astype(x.dtype)

def gmlp_spatial_unit(u, v, norm_g, norm_b, ws, bs):
    B, S, _ = u.shape
    nb = S // GMLP_BLOCK
    v = layer_norm(v.reshape(B, S, GMLP_HEADS, GMLP_HEAD_DIM), norm_g, norm_b)
    v = v.reshape(B, nb, GMLP_BLOCK, GMLP_HEADS, GMLP_HEAD_DIM)
    pos_chunk = jnp.arange(GMLP_BLOCK) // CHUNK
    mask = pos_chunk[None, :] <= pos_chunk[:, None]
    w = jnp.where(mask[None], ws, jnp.zeros_like(ws))
    sv = jnp.einsum('hts,bnshd->bnthd', w, v) + bs.T[:, :, None]
    return u * sv.reshape(B, S, GMLP_WIDTH)

def multiscale_pool(xb, pool_w, pool_b, pool_scale):
    B, S, _ = xb.shape
    xg = xb.reshape(B, S, POOL_GROUPS, POOL_GROUP_DIM).astype(jnp.float32)
    cs = jnp.cumsum(xg, axis=1)
    t = jnp.arange(S)
    means = []
    for g, win in enumerate(POOL_WINDOWS):
        csg = cs[:, :, g]
        lagged = jnp.concatenate([jnp.zeros((B, win, POOL_GROUP_DIM), csg.dtype), csg[:, :S - win]], axis=1)
        cnt = jnp.minimum(t + 1, win).astype(jnp.float32)
        means.append((csg - lagged) / cnt[None, :, None])
    pooled = jnp.stack(means, axis=2) - xg
    y = jnp.einsum('bsgd,gde->bsge', pooled.astype(xb.dtype), pool_w).reshape(B, S, POOL_WIDTH)
    return (y + pool_b) * pool_scale

def even_mixer(h, w_in, gmlp_norm_g, gmlp_norm_b, gmlp_ws, gmlp_bs, pool_w, pool_b, pool_scale, w_out):
    proj = h @ w_in
    u, v, z_a, x_b, z_b = jnp.split(proj, [GMLP_WIDTH, 2 * GMLP_WIDTH, 3 * GMLP_WIDTH,
                                           3 * GMLP_WIDTH + POOL_WIDTH], axis=-1)
    a = gmlp_spatial_unit(u, v, gmlp_norm_g, gmlp_norm_b, gmlp_ws, gmlp_bs) * jax.nn.silu(z_a)
    b = multiscale_pool(x_b, pool_w, pool_b, pool_scale) * jax.nn.silu(z_b)
    return jnp.concatenate([a, b], axis=-1) @ w_out

def mla_mixer(h, positions, w_in, q_norm_g, kv_norm_g, w_uq, w_uk, w_uv, w_out):
    B, S, _ = h.shape
    proj = h @ w_in
    q_c, kv_c, k_r, z = jnp.split(proj, [MLA_Q_RANK, MLA_Q_RANK + MLA_KV_RANK,
                                         MLA_Q_RANK + MLA_KV_RANK + MLA_ROPE], axis=-1)
    q_c = rms_norm(q_c, q_norm_g)
    kv_c = rms_norm(kv_c, kv_norm_g)
    q = jnp.einsum('bsr,rhd->bshd', q_c, w_uq)
    q_nope, q_rope = q[..., :MLA_NOPE], q[..., MLA_NOPE:]
    cos, sin = rope_cos_sin(positions)
    q_rope = apply_rope(q_rope, cos[:, :, None, :], sin[:, :, None, :])
    k_rope = apply_rope(k_r, cos, sin)
    q_lat = jnp.einsum('bshd,rhd->bshr', q_nope, w_uk)
    nb = S // Q_BLOCK
    q_lat_b = q_lat.reshape(B, nb, Q_BLOCK, MLA_HEADS, MLA_KV_RANK).transpose(1, 0, 2, 3, 4)
    q_rope_b = q_rope.reshape(B, nb, Q_BLOCK, MLA_HEADS, MLA_ROPE).transpose(1, 0, 2, 3, 4)
    key_chunk = jnp.arange(S) // CHUNK

    def attend_block(args):
        ql, qr, i = args
        s = jnp.einsum('bqhr,bkr->bhqk', ql, kv_c) + jnp.einsum('bqhd,bkd->bhqk', qr, k_rope)
        s = s.astype(jnp.float32) * ATTN_SCALE
        q_chunk = (i * Q_BLOCK + jnp.arange(Q_BLOCK)) // CHUNK
        mask = key_chunk[None, :] <= q_chunk[:, None]
        p = jax.nn.softmax(jnp.where(mask, s, -jnp.inf), axis=-1).astype(kv_c.dtype)
        return jnp.einsum('bhqk,bkr->bqhr', p, kv_c)

    o_lat = lax.map(attend_block, (q_lat_b, q_rope_b, jnp.arange(nb)))
    o_lat = o_lat.transpose(1, 0, 2, 3, 4).reshape(B, S, MLA_HEADS, MLA_KV_RANK)
    o = jnp.einsum('bshr,rhd->bshd', o_lat, w_uv).reshape(B, S, MLA_WIDTH)
    return (o * jax.nn.silu(z)) @ w_out

def first_inputs(seed: int = 0) -> dict:
    key = jax.random.key(seed)
    ks = jax.random.split(key, 24)
    f32 = jnp.float32

    def nrm(k, shape, s):
        return s * jax.random.normal(k, shape, f32)

    x = nrm(ks[0], (BATCH, SEQ, D_MODEL), 1.0)
    c = nrm(ks[1], (BATCH, D_MODEL), 1.0)
    offs = jax.random.randint(ks[2], (BATCH, 1), 0, 4096, dtype=jnp.int32)
    positions = offs + jnp.arange(SEQ, dtype=jnp.int32)[None, :]
    ada_w = nrm(ks[3], (DEPTH, D_MODEL, 3 * D_MODEL), 0.1 * D_MODEL ** -0.5)
    ada_b = nrm(ks[4], (DEPTH, 3 * D_MODEL), 0.01)
    ln_g = 1.0 + nrm(ks[5], (DEPTH, D_MODEL), 0.02)
    ln_b = nrm(ks[6], (DEPTH, D_MODEL), 0.02)
    e_w_in = nrm(ks[7], (N_EVEN, D_MODEL, EVEN_IN), D_MODEL ** -0.5)
    gmlp_norm_g = 1.0 + nrm(ks[8], (N_EVEN, GMLP_HEAD_DIM), 0.02)
    gmlp_norm_b = nrm(ks[9], (N_EVEN, GMLP_HEAD_DIM), 0.02)
    gmlp_ws = nrm(ks[10], (N_EVEN, GMLP_HEADS, GMLP_BLOCK, GMLP_BLOCK), 0.5 * GMLP_BLOCK ** -0.5)
    gmlp_bs = 1.0 + nrm(ks[11], (N_EVEN, GMLP_HEADS, GMLP_BLOCK), 0.02)
    pool_w = nrm(ks[12], (N_EVEN, POOL_GROUPS, POOL_GROUP_DIM, POOL_GROUP_DIM), POOL_GROUP_DIM ** -0.5)
    pool_b = nrm(ks[13], (N_EVEN, POOL_WIDTH), 0.01)
    pool_scale = 1.0 + nrm(ks[14], (N_EVEN, POOL_WIDTH), 0.1)
    e_w_out = nrm(ks[15], (N_EVEN, EVEN_MIX, D_MODEL), DEEPNORM_BETA * EVEN_MIX ** -0.5)
    o_w_in = nrm(ks[16], (N_ODD, D_MODEL, ODD_IN), D_MODEL ** -0.5)
    mla_q_norm_g = 1.0 + nrm(ks[17], (N_ODD, MLA_Q_RANK), 0.02)
    mla_kv_norm_g = 1.0 + nrm(ks[18], (N_ODD, MLA_KV_RANK), 0.02)
    mla_w_uq = nrm(ks[19], (N_ODD, MLA_Q_RANK, MLA_HEADS, MLA_NOPE + MLA_ROPE), MLA_Q_RANK ** -0.5)
    mla_w_uk = nrm(ks[20], (N_ODD, MLA_KV_RANK, MLA_HEADS, MLA_NOPE), MLA_KV_RANK ** -0.5)
    mla_w_uv = nrm(ks[21], (N_ODD, MLA_KV_RANK, MLA_HEADS, MLA_V), MLA_KV_RANK ** -0.5)
    o_w_out = nrm(ks[22], (N_ODD, MLA_WIDTH, D_MODEL), DEEPNORM_BETA * MLA_WIDTH ** -0.5)
    return {"x": x, "c": c, "positions": positions, "ada_w": ada_w, "ada_b": ada_b,
            "ln_g": ln_g, "ln_b": ln_b, "e_w_in": e_w_in, "gmlp_norm_g": gmlp_norm_g,
            "gmlp_norm_b": gmlp_norm_b, "gmlp_ws": gmlp_ws, "gmlp_bs": gmlp_bs,
            "pool_w": pool_w, "pool_b": pool_b, "pool_scale": pool_scale, "e_w_out": e_w_out,
            "o_w_in": o_w_in, "mla_q_norm_g": mla_q_norm_g, "mla_kv_norm_g": mla_kv_norm_g,
            "mla_w_uq": mla_w_uq, "mla_w_uk": mla_w_uk, "mla_w_uv": mla_w_uv, "o_w_out": o_w_out}

def first_block(x, c, positions, ada_w, ada_b, ln_g, ln_b, e_w_in, gmlp_norm_g, gmlp_norm_b,
              gmlp_ws, gmlp_bs, pool_w, pool_b, pool_scale, e_w_out, o_w_in, mla_q_norm_g,
              mla_kv_norm_g, mla_w_uq, mla_w_uk, mla_w_uv, o_w_out):
    cond = jax.nn.silu(c)
    for l in range(DEPTH):
        mod = cond @ ada_w[l] + ada_b[l]
        shift, scale, gate = jnp.split(mod, 3, axis=-1)
        h = x * (1.0 + scale[:, None, :]) + shift[:, None, :]
        if l % 2 == 0:
            e = l // 2
            y = even_mixer(h, e_w_in[e], gmlp_norm_g[e], gmlp_norm_b[e], gmlp_ws[e], gmlp_bs[e],
                           pool_w[e], pool_b[e], pool_scale[e], e_w_out[e])
        else:
            o = l // 2
            y = mla_mixer(h, positions, o_w_in[o], mla_q_norm_g[o], mla_kv_norm_g[o],
                          mla_w_uq[o], mla_w_uk[o], mla_w_uv[o], o_w_out[o])
        x = layer_norm(DEEPNORM_ALPHA * x + (1.0 + gate[:, None, :]) * y, ln_g[l], ln_b[l])
    return x


N_A = DEPTH // 2
N_B = DEPTH - N_A
CONV_W = 3
HEAD_DIM = 64
N_HEADS = D_MODEL // HEAD_DIM
N_KV_HEADS = 4
GROUP = N_HEADS // N_KV_HEADS
WINDOW = 128
BLOCK = 128
ROT_DIM = HEAD_DIM // 4
ROPE_THETA_2 = 500000.0
D_FF = ((8 * D_MODEL // 3 + 255) // 256) * 256
EPS = 1e-6
NEG = -1e30


def rmsnorm(x, g):
    xf = x.astype(jnp.float32)
    r = lax.rsqrt(jnp.mean(xf * xf, axis=-1, keepdims=True) + EPS)
    return (xf * r).astype(x.dtype) * g

def rope_tables(seq_len, dtype):
    inv_freq = ROPE_THETA_2 ** (-jnp.arange(0, ROT_DIM, 2, dtype=jnp.float32) / ROT_DIM)
    ang = jnp.arange(seq_len, dtype=jnp.float32)[:, None] * inv_freq[None, :]
    return jnp.cos(ang)[:, None, :].astype(dtype), jnp.sin(ang)[:, None, :].astype(dtype)

def partial_rotary(t, cos, sin):
    half = ROT_DIM // 2
    t1, t2, rest = t[..., :half], t[..., half:ROT_DIM], t[..., ROT_DIM:]
    return jnp.concatenate([t1 * cos - t2 * sin, t2 * cos + t1 * sin, rest], axis=-1)

def causal_depthwise_conv3(u, w):
    s = u.shape[1]
    up = jnp.pad(u, ((0, 0), (CONV_W - 1, 0), (0, 0)))
    return up[:, 0:s] * w[0] + up[:, 1:s + 1] * w[1] + up[:, 2:s + 2] * w[2]

def short_conv_mixer(h, w_in, conv_w, w_out):
    bcx = h @ w_in
    b_gate, c_gate, u = jnp.split(bcx, 3, axis=-1)
    y = b_gate * causal_depthwise_conv3(c_gate * u, conv_w)
    return y @ w_out

def swiglu(h, w_gate_up, w_down):
    g, u = jnp.split(h @ w_gate_up, 2, axis=-1)
    return (jax.nn.silu(g) * u) @ w_down

def sliding_window_sink_attention(q, k, v, sinks):
    bsz, s = q.shape[0], q.shape[1]
    nb = s // BLOCK
    qb = q.reshape(bsz, nb, BLOCK, N_KV_HEADS, GROUP, HEAD_DIM)

    def with_prev(t):
        tb = t.reshape(bsz, nb, BLOCK, N_KV_HEADS, HEAD_DIM)
        prev = jnp.concatenate([jnp.zeros_like(tb[:, :1]), tb[:, :-1]], axis=1)
        return jnp.concatenate([prev, tb], axis=2)

    kk, vv = with_prev(k), with_prev(v)
    scale = 1.0 / math.sqrt(HEAD_DIM)
    scores = jnp.einsum('bnqhgd,bnkhd->bnhgqk', qb, kk).astype(jnp.float32) * scale

    qi = jnp.arange(BLOCK)[:, None]
    kj = jnp.arange(2 * BLOCK)[None, :]
    diff = BLOCK + qi - kj
    band = (diff >= 0) & (diff < WINDOW)
    not_pad = (jnp.arange(nb)[:, None, None] > 0) | (kj[None] >= BLOCK)
    valid = band[None] & not_pad
    scores = jnp.where(valid[None, :, None, None], scores, NEG)

    sink = jnp.broadcast_to(
        sinks.astype(jnp.float32).reshape(N_KV_HEADS, GROUP)[None, None, :, :, None, None],
        scores.shape[:-1] + (1,))
    probs = jax.nn.softmax(jnp.concatenate([scores, sink], axis=-1), axis=-1)[..., :-1]
    out = jnp.einsum('bnhgqk,bnkhd->bnqhgd', probs.astype(v.dtype), vv)
    return out.reshape(bsz, s, N_HEADS * HEAD_DIM)

def second_inputs(seed: int = 0) -> dict:
    key = jax.random.key(seed)
    ks = jax.random.split(key, 24)
    f32 = jnp.float32
    D, F = D_MODEL, D_FF
    QD = N_HEADS * HEAD_DIM
    KVD = N_KV_HEADS * HEAD_DIM

    def nrm(k, shape, fan_in):
        return jax.random.normal(k, shape, f32) * (fan_in ** -0.5)

    def gain(k, shape):
        return 1.0 + 0.05 * jax.random.normal(k, shape, f32)

    return {
        "x": jax.random.normal(ks[0], (BATCH, SEQ, D), f32),
        "a_pre_norm": gain(ks[1], (N_A, D)),
        "a_w_in": nrm(ks[2], (N_A, D, 3 * D), D),
        "a_conv_w": nrm(ks[3], (N_A, CONV_W, D), CONV_W),
        "a_w_out": nrm(ks[4], (N_A, D, D), D),
        "a_post_norm": gain(ks[5], (N_A, D)),
        "ffn_pre_norm": gain(ks[6], (DEPTH, D)),
        "ffn_w_gate_up": nrm(ks[7], (DEPTH, D, 2 * F), D),
        "ffn_w_down": nrm(ks[8], (DEPTH, F, D), F),
        "ffn_post_norm": gain(ks[9], (DEPTH, D)),
        "kv_norm": gain(ks[10], (D,)),
        "w_kv": nrm(ks[11], (D, 2 * KVD), D),
        "b_pre_norm": gain(ks[12], (N_B, D)),
        "b_w_q": nrm(ks[13], (N_B, D, QD), D),
        "b_sinks": 0.5 * jax.random.normal(ks[14], (N_B, N_HEADS), f32),
        "b_w_o": nrm(ks[15], (N_B, QD, D), QD),
        "b_post_norm": gain(ks[16], (N_B, D)),
    }

def second_block(x, a_pre_norm, a_w_in, a_conv_w, a_w_out, a_post_norm,
              ffn_pre_norm, ffn_w_gate_up, ffn_w_down, ffn_post_norm,
              kv_norm, w_kv,
              b_pre_norm, b_w_q, b_sinks, b_w_o, b_post_norm):
    bsz, s, _ = x.shape
    cos, sin = rope_tables(s, x.dtype)
    h = x
    for l in range(DEPTH):
        if l < N_A:
            mix = short_conv_mixer(rmsnorm(h, a_pre_norm[l]), a_w_in[l], a_conv_w[l], a_w_out[l])
            h = h + rmsnorm(mix, a_post_norm[l])
        else:
            j = l - N_A
            if j == 0:
                kv = rmsnorm(h, kv_norm) @ w_kv
                k_sh, v_sh = jnp.split(kv, 2, axis=-1)
                k_sh = partial_rotary(k_sh.reshape(bsz, s, N_KV_HEADS, HEAD_DIM), cos, sin)
                v_sh = v_sh.reshape(bsz, s, N_KV_HEADS, HEAD_DIM)
            q = (rmsnorm(h, b_pre_norm[j]) @ b_w_q[j]).reshape(bsz, s, N_HEADS, HEAD_DIM)
            q = partial_rotary(q, cos, sin)
            attn = sliding_window_sink_attention(q, k_sh, v_sh, b_sinks[j]) @ b_w_o[j]
            h = h + rmsnorm(attn, b_post_norm[j])
        ff = swiglu(rmsnorm(h, ffn_pre_norm[l]), ffn_w_gate_up[l], ffn_w_down[l])
        h = h + rmsnorm(ff, ffn_post_norm[l])
    return h


def setup_inputs(seed=0):
    out = dict(first_inputs(seed))
    for name, value in second_inputs(seed + 1).items():
        if name != "x":
            out[name + "_2"] = value
    return out


def reference(
    x, c, positions, ada_w, ada_b, ln_g, ln_b, e_w_in, gmlp_norm_g, gmlp_norm_b, gmlp_ws,
    gmlp_bs, pool_w, pool_b, pool_scale, e_w_out, o_w_in, mla_q_norm_g, mla_kv_norm_g, mla_w_uq,
    mla_w_uk, mla_w_uv, o_w_out, a_pre_norm_2, a_w_in_2, a_conv_w_2, a_w_out_2, a_post_norm_2,
    ffn_pre_norm_2, ffn_w_gate_up_2, ffn_w_down_2, ffn_post_norm_2, kv_norm_2, w_kv_2,
    b_pre_norm_2, b_w_q_2, b_sinks_2, b_w_o_2, b_post_norm_2,
):
    x = first_block(
        x, c, positions, ada_w, ada_b, ln_g, ln_b, e_w_in, gmlp_norm_g, gmlp_norm_b, gmlp_ws,
        gmlp_bs, pool_w, pool_b, pool_scale, e_w_out, o_w_in, mla_q_norm_g, mla_kv_norm_g,
        mla_w_uq, mla_w_uk, mla_w_uv, o_w_out,
    )
    return second_block(
        x, a_pre_norm_2, a_w_in_2, a_conv_w_2, a_w_out_2, a_post_norm_2, ffn_pre_norm_2,
        ffn_w_gate_up_2, ffn_w_down_2, ffn_post_norm_2, kv_norm_2, w_kv_2, b_pre_norm_2,
        b_w_q_2, b_sinks_2, b_w_o_2, b_post_norm_2,
    )


_drawn_inputs = setup_inputs


def setup_inputs(seed=0):
    import zlib

    import numpy as np

    out = dict(_drawn_inputs(seed))
    spreads = {}
    factors = {'ada_b': 5.222,
     'gmlp_norm_g': 8.0,
     'gmlp_norm_b': 8.0,
     'gmlp_bs': 8.0,
     'pool_b': 8.0,
     'mla_q_norm_g': 8.0,
     'mla_kv_norm_g': 8.0,
     'b_sinks_2': 6.557}
    for name, (base, spread) in spreads.items():
        noise = np.random.default_rng([zlib.crc32(name.encode()), seed]).standard_normal(out[name].shape)
        drawn = base * np.exp(spread * noise) if base else spread * noise
        out[name] = __import__('jax').numpy.asarray(drawn.astype(out[name].dtype))
    for name, factor in factors.items():
        out[name] = (out[name] * factor).astype(out[name].dtype)
    return out
```

```python
from contextlib import ExitStack

import numpy as np
import concourse.bass as bass
from concourse import mybir

F32 = mybir.dt.float32
F32R = mybir.dt.float32r
I32 = mybir.dt.int32
ALU = mybir.AluOpType
ACT = mybir.ActivationFunctionType
AX = mybir.AxisListType.X

P = 128
S = 512
T = S // P
D = 1024
K = D // P
CHUNK = 2048
DEPTH = 2

G_HEADS, G_DIM, G_HALF = 4, 256, 64
POOL_WINDOWS = (2, 4, 8, 16)
PAD = 16
MIX = 16
LN_EPS = 1e-5
ALPHA = (2.0 * DEPTH) ** 0.25
HEADS, NOPE, ROPE, QR, KVR = 16, 128, 64, 256, 128
LATENT = QR + KVR + ROPE
MLA_SCALE = (NOPE + ROPE) ** -0.5
MASKED = -1e30
HD, KVH = 64, 4
SW_SCALE = HD ** -0.5
EPS2 = 1e-6
F_TILES = 2816 // P
D_FF = 2816

TWO_PI = 2.0 * np.pi
PI_1 = 6.28125
PI_2 = float(np.float32(np.round((TWO_PI - PI_1) * 2 ** 19) / 2 ** 19))
PI_3 = float(TWO_PI - PI_1 - PI_2)
ROUND = 12582912.0

ROWS = {}
_n = 0
for _name, _count in (("ada_b", 48), ("c", 8), ("pool_b", 8), ("pool_scale", 8), ("q_g", 2), ("kv_g", 1), ("conv", 24)):
    ROWS[_name] = _n
    _n += _count
N_ROWS = _n

RING = [
    ("ada", 12, ("raw", "raw"), (1, 1)),
    ("v", 2, ("split", "split"), (2, 2)),
    ("zu", 4, ("split", "split"), (2, 2)),
    ("xb", 2, ("split", "split"), (2, 2)),
    ("pool", 1, ("raw", "raw"), (1, 1)),
    ("zb", 2, ("split", "split"), (2, 2)),
    ("eout", 4, ("split", "split"), (2, 2)),
    ("lat", 1, ("split", "split"), (2, 2)),
    ("mla", 8, ("split", "raw"), (2, 6)),
    ("oout", 4, ("split", "split"), (2, 2)),
    ("cu", 4, ("split", "split"), (2, 2)),
    ("b", 2, ("split", "split"), (2, 2)),
    ("aout", 2, ("split", "split"), (2, 2)),
    ("gu0", 11, ("split", "split"), (2, 2)),
    ("dn0", 6, ("split", "split"), (2, 2)),
    ("kv", 1, ("split", "split"), (2, 2)),
    ("q", 2, ("split", "split"), (2, 2)),
    ("wo", 2, ("split", "split"), (2, 2)),
    ("gu1", 11, ("split", "split"), (2, 2)),
    ("dn1", 6, ("split", "split"), (2, 2)),
]


class Base:

    def __init__(self, pairs, kinds, dmas, full, use, split):
        self.pairs, self.kinds, self.dmas = pairs, kinds, dmas
        self.full, self.use, self.split = tuple(full), tuple(use), tuple(split)


BASE = {}
_full, _use, _split = [0, 0], [0, 0], [0, 0]
for _name, _pairs, _kinds, _dmas in RING:
    BASE[_name] = Base(_pairs, _kinds, _dmas, _full, _use, _split)
    for _s in range(2):
        _full[_s] += 16 * _dmas[_s] * _pairs
        _use[_s] += _pairs
        _split[_s] += _pairs * (_kinds[_s] == "split")
NAMES = [r[0] for r in RING]

GATED = {}
_n = 0
for _name, _count in (("zu", 8), ("zb", 8), ("b", 8), ("gu0", F_TILES), ("gu1", F_TILES)):
    GATED[_name] = _n
    _n += _count


class Steps:

    def __init__(self, eng, sem):
        self.eng, self.sem, self.n, self.off = eng, sem, 0, 0

    def link(self, ins):
        ins.then_inc(self.sem, 1)
        self.n += 1
        self.eng.wait_ge(self.sem, self.off + self.n)

    def loop(self, i, per):
        self.off, self.first, self.per = i * per, self.n, per

    def done(self, count):
        assert self.n - self.first == self.per, (self.n - self.first, self.per)
        self.n = self.first + self.per * count
        self.off = 0


def constants():
    ident = np.eye(P, dtype=np.float32)
    inv = np.ones((P, len(POOL_WINDOWS) * PAD), np.float32)
    for g, w in enumerate(POOL_WINDOWS):
        for t in range(PAD):
            inv[:, g * PAD + t] = np.float32(1.0) / np.float32(min(t + 1, w))
    r = np.arange(P)
    half = ROPE // 2
    freq = (np.float32(1.0) / (np.float32(10000.0) ** (np.arange(0, ROPE, 2, dtype=np.float32) / np.float32(ROPE)))).astype(np.float32)
    freq_col = freq[r % half][:, None].astype(np.float32)
    turn_m = np.zeros((P, P), np.float32)
    for m in range(P):
        low = (m % ROPE) < half
        turn_m[m + half if low else m - half, m] = -1.0 if low else 1.0
    rot, rh = HD // 4, HD // 8
    inv_freq = (np.float32(500000.0) ** (-np.arange(0, rot, 2, dtype=np.float32) / np.float32(rot))).astype(np.float32)
    ang = (np.arange(S, dtype=np.float32)[:, None] * inv_freq[None, :]).astype(np.float32)
    cos_b, sin_b = np.ones((P, S), np.float32), np.zeros((P, S), np.float32)
    turn_b = np.zeros((P, P), np.float32)
    for m in range(P):
        d = m % HD
        if d < rot:
            cos_b[m], sin_b[m] = np.cos(ang[:, d % rh]), np.sin(ang[:, d % rh])
            turn_b[m + rh if d < rh else m - rh, m] = -1.0 if d < rh else 1.0
    qi, kj = np.arange(P)[:, None], np.arange(2 * P)[None, :]
    diff = P + qi - kj
    window = np.where((diff >= 0) & (diff < P), 0.0, MASKED).astype(np.float32)
    return {
        "k_small": np.concatenate([ident, inv, freq_col], axis=1).astype(np.float32),
        "k_turn_m": turn_m,
        "k_swa": np.concatenate([turn_b, window, cos_b, sin_b], axis=1).astype(np.float32),
    }


N_INV = len(POOL_WINDOWS) * PAD



CREDIT = 1


def program(nc, a, out):
    with ExitStack() as ctx:

        def sem(name):
            return ctx.enter_context(nc.semaphore(name))

        KB = 1024
        arena = ctx.enter_context(nc.sbuf_tensor("arena", [P, 206 * KB // 4], F32))
        start = nc.sbuf_base - 206 * KB

        def at(name, offset, shape, dt=F32):
            return nc.alloc_sbuf_tensor_at(name, shape, dt, offset=start + offset)

        raw = [at(f"w_raw{s}", 8 * KB * s, [P, CHUNK]) for s in range(2)]
        WH = [at(f"w_high{s}", (16 + 8 * s) * KB, [P, CHUNK], F32R) for s in range(2)]
        WL = [at(f"w_low{s}", (32 + 8 * s) * KB, [P, CHUNK], F32R) for s in range(2)]
        ZB = 48 * KB
        hH = at("h_high", ZB, [P, K, S], F32R)
        hL = at("h_low", ZB + 16 * KB, [P, K, S], F32R)
        x = at("x", 80 * KB, [P, T, D])
        ZD = 96 * KB
        gains = at("gains", 184 * KB, [P, 4, D])
        hf = at("hf", 200 * KB, [P, D])
        buf = [at(f"gate_buf{m}", (200 + 2 * m) * KB, [P, S]) for m in range(2)]
        ofs = 204 * KB

        def tiny(name, shape):
            nonlocal ofs
            got = at(name, ofs, shape)
            size = 4
            for d in shape[1:]:
                size *= d
            ofs += (size + 31) // 32 * 32
            assert ofs <= 206 * KB
            return got

        small = tiny("small", [P, P + N_INV + 1])
        ident, inv_count, freq = small[:, 0:P], small[:, P:P + N_INV], small[:, P + N_INV:P + N_INV + 1]
        vec = tiny("vec", [P, N_ROWS])
        mod = tiny("mod", [P, 48])
        csil = tiny("csil", [P, K])
        stat = tiny("stat", [P, T, 8])
        bn = tiny("bn", [P, 8, 6])
        mv = tiny("mv", [P, 8, 2])
        eps = tiny("eps", [P, 2])
        soft = tiny("soft", [P, 2, 8, 2])
        sinks = tiny("sinks", [P, 16])

        def dz(name, offset, shape, dt=F32):
            return at(name, ZD + 4 * offset, shape, dt)

        sv = dz("sv", 0, [P, K, S])
        mixH = dz("mix_high", 4096, [P, MIX, S], F32R)
        mixL = dz("mix_low", 12288, [P, MIX, S], F32R)
        pooled = dz("pooled", 8192, [P, K, S])
        vn = dz("v_norm", 16384, [P, T, D])
        xbuf, sum_a, sum_b = (dz(n, 20480 + 528 * j, [P, PAD + S]) for j, n in enumerate(("xbuf", "sum_a", "sum_b")))
        ones = dz("ones", 0, [P, P])
        diag = dz("diag", 128, [P, K, P])
        g_bc = gains[:, 1, 0:G_DIM]
        b_bc = gains[:, 1, G_DIM:2 * G_DIM]
        bs_bc = gains[:, 1, 2 * G_DIM:4 * G_DIM]
        ws_sb = gains[:, 2, 0:S].rearrange("p (h s) -> p h s", h=G_HEADS)
        wT = gains[:, 2, S:2 * S].rearrange("p (h t) -> p h t", h=G_HEADS)
        rows = hf[:, 0:P]
        oz = dz("o_gated", 0, [P, HEADS, S])
        qcT = dz("qc_t", 8192, [P, 2, S])
        kvT = dz("kv_t", 9216, [P, S])
        kr = dz("k_rope", 9728, [P, S])
        cosM, sinM = dz("cos_m", 10240, [P, S]), dz("sin_m", 10752, [P, S])
        turn_m = dz("turn_m", 11264, [P, P])
        qn = dz("q_nope", 11392, [P, 2, S])
        qraw = dz("q_raw", 12416, [P, S])
        ones1, diag1 = dz("ones1", 11392, [P, P]), dz("diag1", 11520, [P, K, P])
        qr = dz("q_rope", 12928, [P, S])
        kn = dz("k_nope", 13440, [P, 2, S])
        vh = dz("v_heads", 14464, [P, T, 2 * NOPE])
        sz = dz("silu_z", 15488, [P, 2, S])
        pm = [dz(f"probs{u}", 16512 + 512 * u, [P, S]) for u in range(2)]
        pT = [dz(f"probs_t{u}", 17536 + 2048 * u, [P, T, S]) for u in range(2)]
        kraw = dz("k_raw", 21632, [P, S])
        latn = dz("latent_norm", 17536, [P, T, S])
        pos = dz("pos", 19584, [P, S], I32)
        ang, turns, rest = (dz(n, 20096 + 512 * j, [P, S]) for j, n in enumerate(("ang", "turns", "rest")))
        oH = at("o_high", ZB, [P, HEADS, S], F32R)
        oL = dz("o_low", 8192, [P, HEADS, S], F32R)
        yc = dz("conv_out", 0, [P, K, S])
        cw = dz("conv_in", 4096, [P, 2 + S])
        cv = dz("conv_sum", 4704, [P, S])
        yH, yL = dz("y_high", 8192, [P, K, S], F32R), dz("y_low", 12288, [P, K, S], F32R)
        fH, fL = dz("ff_high", 0, [P, F_TILES, S], F32R), dz("ff_low", F_TILES * S, [P, F_TILES, S], F32R)
        kdup = dz("k_dup", 0, [P, KVH, S])
        vall = dz("v_all", 2048, [P, T, KVH * HD])
        swa = dz("swa", 3072, [P, P + 2 * P + 2 * S])
        turn_b, window = swa[:, 0:P], swa[:, P:3 * P]
        cosB, sinB = swa[:, 3 * P:3 * P + S], swa[:, 3 * P + S:3 * P + 2 * S]
        q2raw = dz("q2_raw", 4480, [P, 2, S])
        q2 = dz("q2", 5504, [P, 2, S])
        kg = dz("k_group", 6528, [P, S])
        vg = dz("v_group", 7040, [P, T, HD])
        sS = [dz(f"scores{u}", 7296 + 512 * u, [P, 2, 2 * P]) for u in range(2)]
        p2 = [dz(f"probs2_{u}", 8320 + 512 * u, [P, 2, 2 * P]) for u in range(2)]
        p2T = [dz(f"probs2_t{u}", 9344 + 512 * u, [P, 4, P]) for u in range(2)]
        q2tmp = dz("q2_tmp", 10368, [P, 2, S])
        o2H, o2L = dz("o2_high", 11392, [P, K, S], F32R), dz("o2_low", 15488, [P, K, S], F32R)

        PS = ctx.enter_context(nc.psum_tensor("PS", [P, 8, S], F32))

        def tile(ap, t):
            return ap[:, :, t * P:(t + 1) * P]

        def two(b):
            return PS[:, b:b + 2, :].rearrange("p a (c t) -> p (a c) t", t=P)

        def flat2(b):
            return PS[:, b:b + 2, :].rearrange("p a n -> p (a n)")

        w_full = [sem(f"w_full{s}") for s in range(2)]
        raw_free = [sem(f"raw_free{s}") for s in range(2)]
        w_high = [sem(f"w_high_ready{s}") for s in range(2)]
        w_split = [sem(f"w_split{s}") for s in range(2)]
        used = [sem(f"used{s}") for s in range(2)]
        pair_free = [sem(f"pair_free{s}") for s in range(2)]
        small_in, x_in, aux_in, gains_in, late_in = (sem(n) for n in ("small_in", "x_in", "aux_in", "gains_in", "late_in"))
        act_step, dve_step, pool_ready = sem("act_step"), sem("dve_step"), sem("pool_ready")
        rows_tr, vec_ready, csil_ready, ws_tr, wT_ready = (sem(n) for n in ("rows_tr", "vec_ready", "csil_ready", "ws_tr", "wT_ready"))
        mod_ready, diag_ready, gate_mm, gate_ready = (sem(n) for n in ("mod_ready", "diag_ready", "gate_mm", "gate_ready"))
        tr_done, h_high, h_ready, xhat_ready = (sem(n) for n in ("tr_done", "h_high_ready", "h_ready", "xhat_ready"))
        lnv_stat, lnv_sqrt, vn_ready, sp_done, sv_ready = (sem(n) for n in ("lnv_stat", "lnv_sqrt", "vn_ready", "sp_done", "sv_ready"))
        sg_ready, prod_ready, act_high, gate_low = (sem(n) for n in ("sg_ready", "prod_ready", "act_high", "gate_low"))
        xb_ready, xb_used, pooled_ready, py_done, yb_ready = (sem(n) for n in ("xb_ready", "xb_used", "pooled_ready", "py_done", "yb_ready"))
        y_ready, ln_stat, sqrt_ready, x_ready = (sem(n) for n in ("y_ready", "ln_stat", "sqrt_ready", "x_ready"))
        rest_ready, sin_ready, lat_sqrt, latn_ready, lat_tr, lat_ev, kr_turn, kr_ready = (
            sem(n) for n in ("rest_ready", "sin_ready", "lat_sqrt", "latn_ready", "lat_tr", "lat_ev", "kr_turn", "kr_ready"))
        proj_done, qa_ready, kv_ready, q_turn, qr_ready = (sem(n) for n in ("proj_done", "qa_ready", "kv_ready", "q_turn", "qr_ready"))
        s_done, m_ready, e_ready, p_ready, t_done, pT_ready, pv_done, sz_ready, oz_ready = (
            sem(n) for n in ("s_done", "m_ready", "e_ready", "p_ready", "t_done", "pT_ready", "pv_done", "sz_ready", "oz_ready"))
        oh_ready, ol_ready, yc_ready = sem("oh_ready"), sem("ol_ready"), sem("yc_ready")
        k2_raw, k2_turn, k2_rot, kd_ready, v2_ready = (sem(n) for n in ("k2_raw", "k2_turn", "k2_rot", "kd_ready", "v2_ready"))
        q2_raw, q2_turn, q2_ready, kvg_ready = (sem(n) for n in ("q2_raw_ready", "q2_turn", "q2_ready", "kvg_ready"))
        s2_done, m2_ready, e2_ready, p2_ready, t2_done, p2T_ready, pv2_done, o2_high, o2_low = (
            sem(n) for n in ("s2_done", "m2_ready", "e2_ready", "p2_ready", "t2_done", "p2T_ready", "pv2_done", "o2_high_ready", "o2_low_ready"))
        out_done = sem("out_done")

        PF, n = {}, CREDIT + BASE["ada"].pairs
        for name in ("zu", "xb", "zb", "cu", "b", "gu0", "gu1"):
            PF[name] = n
            n += BASE[name].pairs
        SG, n = {}, 0
        for name, c in (("zu", 8), ("zb", 8), ("cu", 8), ("gu0", F_TILES), ("gu1", F_TILES)):
            SG[name] = n
            n += c

        def end_use(name, s):
            return BASE[name].use[s] + BASE[name].pairs

        def wait_y(eng, b, name, t):
            if t < T - 1:
                eng.wait_ge(y_ready, (T - 1) * b + t + 1)
            else:
                eng.wait_ge(used[1], end_use(name, 1))

        BOUNDARY = ["eout", "oout", "aout", "dn0", "wo", "dn1"]
        TR = {"eout": 1, "oout": 2, "aout": 3, "dn0": 4, "q": 5, "wo": 6}

        block = ctx.enter_context(nc.Block())

        @block.sync
        def _(sp):
            w_in = {n: a[n].rearrange("(k p) n -> p k n", p=P) for n in (
                "e_w_in", "e_w_out", "o_w_in", "o_w_out", "a_w_in", "a_w_out", "w_kv", "b_w_q", "b_w_o")}
            ada_w = a["ada_w"].rearrange("l (k p) n -> l p k n", p=P)

            def load(name, i, s, pieces):
                B = BASE[name]
                assert len(pieces) == B.dmas[s]
                sp.wait_ge(raw_free[s], B.use[s] + i + CREDIT)
                for dst, src in pieces:
                    sp.dma_start(dst, src).then_inc(w_full[s], 16)

            def cols(s, w, c):
                v = raw[s][:, :].rearrange("p (k n) -> p k n", n=256)
                return [(v[:, j:j + K // 2, :], w[:, j:j + K // 2, bass.ds(c, 256)]) for j in (0, K // 2)]

            def twin(s, w, c, step):
                v = raw[s][:, :].rearrange("p (k two c) -> p k two c", two=2, c=P)
                return [(v[:, :, j, :], w[:, :, bass.ds(c + j * step, P)]) for j in range(2)]

            def deep(s, w, kt, n=2):
                c = n * D // 2
                return [(raw[s][:, j * c:(j + 1) * c], w[:, kt + j, :] if n == 2 else w[:, kt, j * c:(j + 1) * c]) for j in range(2)]

            def halves(s, w, kt, c):
                v = raw[s][:, :].rearrange("p (k n) -> p k n", n=S)
                return [(v[:, j:j + 2, :], w[:, kt + j:kt + j + 2, c:c + S]) for j in (0, 2)]

            sp.dma_start(x[:, :, :], a["x"].rearrange("(t p) d -> p t d", p=P)).then_inc(x_in, 16)
            sp.dma_start(ws_sb, a["gmlp_ws"].rearrange("h t s -> t h s")).then_inc(aux_in, 16)
            for dst, src in ((g_bc, a["gmlp_norm_g"]), (b_bc, a["gmlp_norm_b"]), (bs_bc, a["gmlp_bs"])):
                sp.dma_start(dst, src.broadcast_to((P, src.shape[1]))).then_inc(aux_in, 16)
            sp.dma_start(sinks[:, :], a["b_sinks"].broadcast_to((P, 16))).then_inc(aux_in, 16)
            for layer in range(DEPTH):
                with sp.Fori(0, 6) as i:
                    for s in range(2):
                        load("ada", i + 6 * layer, s, [(raw[s][:, :].rearrange("p (k n) -> p k n", n=256),
                                                    ada_w[layer][:, :, bass.ds(i * 512 + s * 256, 256)])])
            for c in range(4):
                load("v", c // 2, c % 2, halves(c % 2, w_in["e_w_in"], 4 * (c % 2), D + S * (c // 2)))
            with sp.Fori(0, 4) as i:
                for s in range(2):
                    load("zu", i, s, twin(s, w_in["e_w_in"], i * 256 + s * P + 2 * D, -2 * D))
            with sp.Fori(0, 2) as i:
                for s in range(2):
                    load("xb", i, s, cols(s, w_in["e_w_in"], i * 512 + s * 256 + 3 * D))
            pool_w = a["pool_w"].rearrange("g (k p) e -> p (g k) e", p=P)
            for s in range(2):
                load("pool", 0, s, [(raw[s][:, 0:1024].rearrange("p (j e) -> p j e", j=4), pool_w[:, 4 * s:4 * s + 4, :])])
            with sp.Fori(0, 2) as i:
                for s in range(2):
                    load("zb", i, s, cols(s, w_in["e_w_in"], i * 512 + s * 256 + 4 * D))
            sp.wait_ge(sv_ready, K)
            for j, n in ((1, "ln_g"), (2, "ln_b")):
                sp.dma_start(gains[:, j, :], a[n][0:1, :].broadcast_to((P, D))).then_inc(gains_in, 16)
            with sp.Fori(0, 4) as i:
                for s in range(2):
                    load("eout", i, s, deep(s, w_in["e_w_out"], i * 4 + s * 2))
            for s in range(2):
                load("lat", 0, s, halves(s, w_in["o_w_in"], 4 * s, 0))
            sp.wait_ge(used[1], end_use("eout", 1))
            sp.dma_start(pos[:, :], a["positions"].broadcast_to((P, S))).then_inc(late_in, 16)
            sp.dma_start(turn_m[:, :], a["k_turn_m"]).then_inc(late_in, 16)
            uq = a["mla_w_uq"].rearrange("(k p) h e -> p k h e", p=P)
            with sp.Fori(0, 8) as i:
                load("mla", i, 0, cols(0, w_in["o_w_in"], i * 256 + LATENT))
                load("mla", i, 1, [
                    *((raw[1][:, k * 256:(k + 1) * 256].rearrange("p (h e) -> p h e", h=2), uq[:, k, bass.ds(i * 2, 2), 0:NOPE]) for k in range(2)),
                    *((raw[1][:, 512 + k * P:512 + (k + 1) * P].rearrange("p (h e) -> p h e", h=2), uq[:, k, bass.ds(i * 2, 2), NOPE:]) for k in range(2)),
                    (raw[1][:, 768:1024].rearrange("p (h e) -> p h e", h=2), a["mla_w_uk"][:, bass.ds(i * 2, 2), :]),
                    (raw[1][:, 1024:1280].rearrange("p (h e) -> p h e", h=2), a["mla_w_uv"][:, bass.ds(i * 2, 2), :]),
                ])
            sp.wait_ge(h_ready, 2 * T)
            for j, src in ((1, a["ln_g"][1:2, :]), (2, a["ln_b"][1:2, :]), (3, a["a_pre"])):
                sp.dma_start(gains[:, j, :], src.broadcast_to((P, D))).then_inc(gains_in, 16)
            with sp.Fori(0, 4) as i:
                for s in range(2):
                    load("oout", i, s, deep(s, w_in["o_w_out"], i * 4 + s * 2))
            with sp.Fori(0, 4) as i:
                for s in range(2):
                    load("cu", i, s, twin(s, w_in["a_w_in"], i * 256 + s * P + D, D))
            with sp.Fori(0, 2) as i:
                for s in range(2):
                    load("b", i, s, cols(s, w_in["a_w_in"], i * 512 + s * 256))
            sp.wait_ge(h_ready, 3 * T)
            for j, src in ((0, a["a_post"]), (1, a["f_pre"][0:1, :])):
                sp.dma_start(gains[:, j, :], src.broadcast_to((P, D))).then_inc(gains_in, 16)
            with sp.Fori(0, 2) as i:
                for s in range(2):
                    load("aout", i, s, deep(s, w_in["a_w_out"], i * 4 + s * 2))

            def ffn(layer):
                gu, dn = f"gu{layer}", f"dn{layer}"
                w_gu = a["f_gate_up"][layer].rearrange("(k p) n -> p k n", p=P)
                w_dn = a["f_down"][layer].rearrange("(k p) n -> p k n", p=P)
                with sp.Fori(0, 11) as i:
                    for s in range(2):
                        load(gu, i, s, twin(s, w_gu, i * 256 + s * P, D_FF))
                if layer == 0:
                    sp.wait_ge(h_ready, 4 * T)
                    new = ((0, a["f_post"][0:1, :]), (1, a["kv_norm"]), (2, a["b_pre"]))
                else:
                    sp.wait_ge(h_ready, 7 * T)
                    new = ((0, a["f_post"][1:2, :]),)
                for j, src in new:
                    sp.dma_start(gains[:, j, :], src.broadcast_to((P, D))).then_inc(gains_in, 16)
                with sp.Fori(0, 5) as i:
                    for s in range(2):
                        load(dn, i, s, deep(s, w_dn, i * 4 + s * 2))
                for s in range(2):
                    load(dn, 5, s, deep(s, w_dn, 20 + s, 1))

            ffn(0)
            for s in range(2):
                load("kv", 0, s, cols(s, w_in["w_kv"], s * 256))
            sp.wait_ge(used[1], end_use("dn0", 1))
            sp.dma_start(swa[:, :], a["k_swa"]).then_inc(late_in, 16)
            with sp.Fori(0, 2) as i:
                for s in range(2):
                    load("q", i, s, cols(s, w_in["b_w_q"], i * 512 + s * 256))
            sp.wait_ge(h_ready, 6 * T)
            for j, src in ((0, a["b_post"]), (1, a["f_pre"][1:2, :])):
                sp.dma_start(gains[:, j, :], src.broadcast_to((P, D))).then_inc(gains_in, 16)
            with sp.Fori(0, 2) as i:
                for s in range(2):
                    load("wo", i, s, deep(s, w_in["b_w_o"], i * 4 + s * 2))
            ffn(1)
            out_v = out.rearrange("(t p) d -> p t d", p=P)
            for t in range(T):
                sp.wait_ge(x_ready, 5 * T + t + 1)
                sp.dma_start(out_v[:, t, :], x[:, t, :]).then_inc(out_done, 16)
            sp.wait_ge(out_done, 16 * T)

        @block.gpsimd
        def _(pool):
            nc.gpsimd.memset(eps[:, 0:1], LN_EPS)
            nc.gpsimd.memset(eps[:, 1:2], EPS2).then_inc(pool_ready, 1)
            for s in range(2):
                pool.sem_inc(raw_free[s], CREDIT)
                pool.sem_inc(pair_free[s], CREDIT)
            pool.sem_inc(gate_low, 2)
            pool.sem_inc(oz_ready, CREDIT)
            pool.sem_inc(o2_low, CREDIT)
            for name, pairs, kinds, _ in RING:
                B = BASE[name]
                with pool.Fori(0, pairs) as i:
                    for s in range(2):
                        if kinds[s] == "split":
                            pool.wait_ge(w_high[s], B.split[s] + i + 1)
                            nc.gpsimd.tensor_tensor(WL[s][:, :], raw[s][:, :], WH[s][:, :].bitcast(F32),
                                                    ALU.subtract).then_inc(w_split[s], 1)
                            pool.wait_ge(w_split[s], B.split[s] + i + 1)
                        else:
                            pool.wait_ge(used[s], B.use[s] + i + 1)
                        pool.sem_inc(raw_free[s], 1)

        @block.scalar
        def _(act):
            steps = Steps(act, act_step)
            nact = nc.scalar.activation

            def split_high(name, i, s):
                B = BASE[name]
                act.wait_ge(w_full[s], B.full[s] + (i + 1) * 32)
                act.wait_ge(used[s], B.use[s] + i)
                nact(WH[s][:, :], raw[s][:, :], ACT.Copy).then_inc(w_high[s], 1)

            def next_high(name, i, s):
                if s == 0:
                    split_high(name, i, 1)
                else:
                    split_high(name, i + 1, 0)

            for n, r, c in (("ada_b", "ada_b", 48), ("c", "c", 8), ("pool_b", "pool_b", 8), ("pool_scale", "pool_scale", 8),
                            ("q_g", "q_g", 2), ("kv_g", "kv_g", 1), ("conv", "conv", 24)):
                act.dma_start(rows[ROWS[r]:ROWS[r] + c, :], a[n].rearrange("a (m p) -> (a m) p", p=P)).then_inc(small_in, 16)
            act.dma_start(small[:, :], a["k_small"]).then_inc(small_in, 16)
            act.wait_ge(vec_ready, 1)
            nact(csil[:, :], vec[:, ROWS["c"]:ROWS["c"] + K], ACT.Silu).then_inc(csil_ready, 1)

            def gate_rows(n, b):
                act.wait_ge(gate_mm, n)
                nact(gains[:, 0, :], flat2(b), ACT.Copy).then_inc(gate_ready, 1)

            def modulate(layer, q, t):
                act.wait_ge(tr_done, T * q + t + 1)
                if t or q:
                    act.wait_ge(h_ready, T * q + t)
                for k in range(K):
                    c = 24 * layer + k
                    ins = nact(gains[:, 3, k * P:(k + 1) * P], two(2 * t)[:, k, :], ACT.Identity,
                               scale=mod[:, c + K:c + K + 1], bias=mod[:, c:c + 1])
                steps.link(ins)
                nact(tile(hH, t), gains[:, 3, :].rearrange("p (k t) -> p k t", t=P), ACT.Copy).then_inc(h_high, 1)

            act.wait_ge(mod_ready, 1)
            gate_rows(1, 0)
            split_high("v", 0, 0)
            for t in range(T):
                modulate(0, 0, t)

            act.wait_ge(pool_ready, 1)
            for n in range(2):
                split_high("v", n, 1)
                split_high("v", n + 1, 0)
                act.wait_ge(lnv_stat, n + 1)
                nact(stat[:, :, 0:2].rearrange("p a b -> p a b"), mv[:, :, 1].rearrange("p (a b) -> p a b", b=2), ACT.Sqrt, bias=eps[:, 0:1]).then_inc(lnv_sqrt, 1)

            def gated(name, first, count, highs, fn):
                B = BASE[name]
                with act.Fori(0, B.pairs) as i:
                    for s in range(2):
                        f = i * 2 + s
                        next_high(name, i, s)
                        act.wait_ge(used[s], B.use[s] + i + 1)
                        act.wait_ge(gate_low, GATED[name] + f + 1)
                        nact(buf[s][:, :], PS[:, 2 * s, :], fn).then_inc(sg_ready, 1)
                        act.wait_ge(prod_ready, GATED[name] + f + 1)
                        nact(highs[:, f, :], buf[s][:, :], ACT.Copy).then_inc(act_high, 1)

            gated("zu", 0, 8, mixH, ACT.Silu)

            B = BASE["xb"]
            for j in range(4):
                if j < 3:
                    next_high("xb", j // 2, j % 2)
                act.wait_ge(used[j % 2], B.use[j % 2] + j // 2 + 1)
                for m in range(2):
                    f = 2 * j + m
                    act.wait_ge(xb_used, f + 1)
                    nact(xbuf[:, PAD:], PS[:, 2 * (j % 2) + m, :], ACT.Copy).then_inc(xb_ready, 1)
            split_high("zb", 0, 0)
            B = BASE["zb"]
            with act.Fori(0, 2) as i:
                for s in range(2):
                    next_high("zb", i, s)
                    act.wait_ge(used[s], B.use[s] + i + 1)
                    for m in range(2):
                        f = i * 4 + (2 * s + m)
                        act.wait_ge(gate_low, GATED["zb"] + f + 1)
                        nact(buf[m][:, :], PS[:, 2 * s + m, :], ACT.Silu).then_inc(sg_ready, 1)
                    for m in range(2):
                        f = i * 4 + (2 * s + m)
                        act.wait_ge(prod_ready, GATED["zb"] + f + 1)
                        nact(mixH[:, f + K, :], buf[m][:, :], ACT.Copy).then_inc(act_high, 1)

            def highs_of(name):
                B = BASE[name]
                for c in range(2 * B.pairs):
                    next_high(name, c // 2, c % 2)

            def root(t, c, scale, e):
                nact(stat[:, t, c + 1:c + 2], stat[:, t, c:c + 1], ACT.Sqrt, bias=eps[:, e:e + 1], scale=scale).then_inc(sqrt_ready, 1)

            def high_tile(q, t, b):
                act.wait_ge(tr_done, T * q + t + 1)
                nact(tile(hH, t), two(b), ACT.Copy).then_inc(h_high, 1)

            def square_x(n, t):
                act.wait_ge(x_ready, n)
                nblk = x[:, t, :].rearrange("p (k t) -> p k t", t=P)
                steps.link(nact(tile(hL, t), nblk, ACT.Square, accum_out=stat[:, t, 3:4]))
                root(t, 3, 1.0 / D, 1)

            highs_of("eout")
            for t in range(T):
                act.wait_ge(ln_stat, t + 1)
                nact(stat[:, t, 1:2], mv[:, t, 1:2], ACT.Sqrt, bias=eps[:, 0:1]).then_inc(sqrt_ready, 1)
                if t:
                    modulate(1, TR["eout"], t - 1)
            modulate(1, TR["eout"], T - 1)

            act.wait_ge(rest_ready, 1)
            nact(sinM[:, :], rest[:, :], ACT.Sin)
            nact(cosM[:, :], turns[:, :], ACT.Sin).then_inc(sin_ready, 1)

            next_high("lat", 0, 0)
            split_high("mla", 0, 0)
            act.wait_ge(used[1], end_use("lat", 1))
            for t in range(T):
                nact(latn[:, t, 0:QR], PS[:, t, 0:QR], ACT.Square, accum_out=stat[:, t, 0:1])
                steps.link(nact(latn[:, t, QR:QR + KVR], PS[:, t, QR:QR + KVR], ACT.Square, accum_out=stat[:, t, 1:2]))
            nact(stat[:, :, 2:3], stat[:, :, 0:1], ACT.Sqrt, bias=eps[:, 0:1], scale=1.0 / QR)
            nact(stat[:, :, 3:4], stat[:, :, 1:2], ACT.Sqrt, bias=eps[:, 0:1], scale=1.0 / KVR).then_inc(lat_sqrt, 1)
            gate_rows(2, 4)
            act.wait_ge(lat_tr, 1)
            for j in range(2):
                nact(qcT[:, j, :], PS[:, 4 + j, :], ACT.Copy, scale=vec[:, ROWS["q_g"] + j:ROWS["q_g"] + j + 1])
            nact(kvT[:, :], PS[:, 6, :], ACT.Copy, scale=vec[:, ROWS["kv_g"]:ROWS["kv_g"] + 1])
            nact(kraw[:, :], PS[:, 7, :], ACT.Copy).then_inc(lat_ev, 1)

            B = BASE["mla"]
            with act.Fori(0, 8) as i:
                act.wait_ge(proj_done, i * 3 + 1)
                nact(qraw[:, :], PS[:, 2, :], ACT.Copy).then_inc(qa_ready, 1)
                nact(qn[:, :, :], PS[:, 0:2, :], ACT.Copy).then_inc(qa_ready, 1)

                def weigh(u):
                    w = (u % T + 1) * P
                    act.wait_ge(m_ready, i * 8 + u + 1)
                    nact(pm[u % 2][:, 0:w], PS[:, 2 + u % 2, 0:w], ACT.Exp, scale=MLA_SCALE, bias=soft[:, u % 2, 1, 0:1],
                         accum_out=soft[:, u % 2, 2, 0:1]).then_inc(e_ready, 1)

                def turned(u):
                    q = u % T
                    act.wait_ge(t_done, i * 8 + u + 1)
                    nact(pT[u // T][:, 0:q + 1, q * P:(q + 1) * P],
                         PS[:, 4 + u % 2, 0:(q + 1) * P].rearrange("p (k t) -> p k t", t=P), ACT.Copy).then_inc(pT_ready, 1)

                weigh(0)
                weigh(1)
                for u in range(8):
                    turned(u)
                    if u + 2 < 8:
                        weigh(u + 2)
                act.wait_ge(used[0], B.use[0] + i + 1)
                nact(sz[:, :, :], PS[:, 0:2, :], ACT.Silu).then_inc(sz_ready, 1)
                split_high("mla", i + 1, 0)

            act.wait_ge(oz_ready, HEADS + CREDIT)
            for c in range(8):
                for h in (2 * c, 2 * c + 1):
                    nact(oH[:, h, :], oz[:, h, :], ACT.Copy).then_inc(oh_ready, 1)
                next_high("oout", c // 2, c % 2)
            for t in range(T):
                act.wait_ge(ln_stat, T + t + 1)
                nact(stat[:, t, 1:2], mv[:, t, 1:2], ACT.Sqrt, bias=eps[:, 0:1]).then_inc(sqrt_ready, 1)
                if t:
                    high_tile(TR["oout"], t - 1, 2 * t - 2)
                square_x(T + t + 1, t)
            high_tile(TR["oout"], T - 1, 2 * T - 2)

            B = BASE["cu"]
            with act.Fori(0, 4) as i:
                for s in range(2):
                    next_high("cu", i, s)
                    act.wait_ge(used[s], B.use[s] + i + 1)
                    act.wait_ge(pair_free[s], i + PF["cu"])
                    nact(buf[s][:, :], PS[:, 2 * s, :], ACT.Copy).then_inc(sg_ready, 1)
            with act.Fori(0, 2) as i:
                for s in range(2):
                    next_high("b", i, s)
                    for m in range(2):
                        f = i * 4 + (2 * s + m)
                        act.wait_ge(prod_ready, GATED["b"] + f + 1)
                        nact(yH[:, f, :], buf[m][:, :], ACT.Copy).then_inc(act_high, 1)

            def boundary(name, pre):
                b = BOUNDARY.index(name)
                highs_of(name) if name != "dn1" else [next_high(name, c // 2, c % 2) for c in range(11)]
                for t in range(T):
                    wait_y(act, b, name, t)
                    steps.link(nact(tile(hH, t), two(2 * t), ACT.Square, accum_out=stat[:, t, 0:1]))
                    root(t, 0, 1.0 / D, 1)
                    if not pre:
                        continue
                    if t:
                        high_tile(TR[name], t - 1, 2 * t - 2)
                    square_x(T * b + t + 1, t)
                if pre:
                    high_tile(TR[name], T - 1, 2 * T - 2)

            boundary("aout", True)
            gated("gu0", 0, F_TILES, fH, ACT.Silu)
            boundary("dn0", True)

            next_high("kv", 0, 0)
            act.wait_ge(used[0], end_use("kv", 0))
            nact(q2raw[:, :, :], PS[:, 0:2, :], ACT.Copy).then_inc(k2_raw, 1)
            next_high("kv", 0, 1)
            act.wait_ge(k2_rot, 1)
            for g in range(KVH):
                src = q2[(g % 2) * HD:(g % 2 + 1) * HD, g // 2, :]
                for j in range(2):
                    ins = nact(kdup[j * HD:(j + 1) * HD, g, :], src, ACT.Copy)
            ins.then_inc(kd_ready, 1)
            act.wait_ge(used[1], end_use("kv", 1))
            for t in range(T):
                high_tile(TR["q"], t, 4 + 2 * (t % 2))
            act.wait_ge(v2_ready, 1)
            act.wait_ge(kd_ready, 1)
            B = BASE["q"]
            with act.Fori(0, 2) as i:
                for s in range(2):
                    g = i * 2 + s
                    next_high("q", i, s)
                    act.wait_ge(used[s], B.use[s] + i + 1)
                    nact(q2raw[:, :, :], PS[:, 0:2, :], ACT.Copy).then_inc(q2_raw, 1)
                    nact(kg[:, :], kdup[:, g, :], ACT.Copy)
                    nact(vg[:, :, :], vall[:, :, bass.ds(g * HD, HD)], ACT.Copy).then_inc(kvg_ready, 1)

                    def weigh2(u):
                        w = P if u % T == 0 else 0
                        act.wait_ge(m2_ready, g * 8 + u + 1)
                        st = soft[:, u % 2, :, :]
                        nact(st[:, 4, :], st[:, 3, :], ACT.Exp)
                        for j in range(2):
                            ins = nact(p2[u % 2][:, j, w:], sS[u % 2][:, j, w:], ACT.Exp, scale=SW_SCALE,
                                       bias=st[:, 2, j:j + 1], accum_out=st[:, 5, j:j + 1])
                        ins.then_inc(e2_ready, 1)

                    def turned2(u):
                        act.wait_ge(t2_done, g * 8 + u + 1)
                        if u % T == 0:
                            nact(p2T[u % 2][:, 1:4:2, :], PS[:, 2 + u % 2, :].rearrange("p (a t) -> p a t", t=P)[:, 1:4:2, :],
                                 ACT.Copy).then_inc(p2T_ready, 1)
                        else:
                            nact(p2T[u % 2][:, :, :], PS[:, 2 + u % 2, :].rearrange("p (a t) -> p a t", t=P),
                                 ACT.Copy).then_inc(p2T_ready, 1)

                    weigh2(0)
                    weigh2(1)
                    for u in range(8):
                        turned2(u)
                        if u + 2 < 8:
                            weigh2(u + 2)
                    act.wait_ge(pv2_done, g * 8 + 8)
                    for j in range(2):
                        nact(o2H[:, g * 2 + j, :], PS[:, j, :], ACT.Copy).then_inc(o2_high, 1)
            boundary("wo", True)
            gated("gu1", 0, F_TILES, fH, ACT.Silu)
            boundary("dn1", False)

        @block.vector
        def _(dve):
            steps = Steps(dve, dve_step)
            v = nc.vector

            dve.wait_ge(rows_tr, 1)
            v.tensor_copy(vec[:, :], PS[:, 0, 0:N_ROWS]).then_inc(vec_ready, 1)
            dve.wait_ge(ws_tr, 1)
            steps.link(v.tensor_copy(wT, PS[:, 1, :].rearrange("p (h t) -> p h t", t=P)))
            v.memset(wT[G_HALF:P, :, 0:G_HALF], 0.0).then_inc(wT_ready, 1)
            dve.wait_ge(vec_ready, 1)
            with dve.Fori(0, 12) as i:
                for s in range(2):
                    dve.wait_ge(used[s], i + 1)
                    v.tensor_tensor(mod[:, bass.ds(i * 4 + 2 * s, 2)], PS[:, 6 + s, 0:2], vec[:, bass.ds(i * 4 + 2 * s, 2)],
                                    ALU.add).then_inc(pair_free[s], 1)
            for s in range(2):
                dve.wait_ge(pair_free[s], PF["zu"])
            for layer in range(DEPTH):
                steps.link(v.tensor_scalar(mod[:, 24 * layer + K:24 * layer + 24], mod[:, 24 * layer + K:24 * layer + 24], 1.0, None, ALU.add))

            def gate_diag(layer, one, dg):
                v.memset(one[:, :], 1.0)
                for k in range(K):
                    c = 24 * layer + 2 * K + k
                    ins = v.tensor_scalar(dg[:, k, :], ident, mod[:, c:c + 1], None, ALU.mult)
                ins.then_inc(diag_ready, 1)

            gate_diag(0, ones, diag)
            steps.link(v.tensor_copy(stat[:, 0, 7:8], mod[:, 0:1]))
            v.tensor_copy(stat[:, 0, 7:8], mod[:, 0:1]).then_inc(mod_ready, 1)

            def low_mod(q, t):
                dve.wait_ge(h_high, T * q + t + 1)
                v.tensor_tensor(tile(hL, t), gains[:, 3, :].rearrange("p (k t) -> p k t", t=P), tile(hH, t).bitcast(F32),
                                ALU.subtract).then_inc(h_ready, 1)

            for t in range(T):
                low_mod(0, t)

            dve.wait_ge(aux_in, 16 * 5)
            for n in range(2):
                dve.wait_ge(used[1], BASE["v"].use[1] + n + 1)
                for t in range(T):
                    for h in range(2):
                        ins = v.bn_stats(bn[:, 2 * t + h, :], PS[:, 4 * n + t, h * G_DIM:(h + 1) * G_DIM])
                steps.link(ins)
                for j in range(8):
                    ins = v.bn_aggr(mv[:, j, :], bn[:, j, :])
                ins.then_inc(lnv_stat, 1)
                dve.wait_ge(lnv_sqrt, n + 1)
                steps.link(v.reciprocal(stat[:, :, 2:4], stat[:, :, 0:2]))
                for t in range(T):
                    for h in range(2):
                        c = n * S + h * G_DIM
                        ins = v.tensor_scalar(vn[:, t, c:c + G_DIM], PS[:, 4 * n + t, h * G_DIM:(h + 1) * G_DIM],
                                              mv[:, 2 * t + h, 0:1], stat[:, t, 2 + h:3 + h], ALU.subtract, ALU.mult)
                steps.link(ins)
                for h in range(2):
                    c = n * S + h * G_DIM
                    blk = vn[:, :, c:c + G_DIM]
                    steps.link(v.tensor_tensor(blk, blk, g_bc.unsqueeze(1).broadcast_to((P, T, G_DIM)), ALU.mult))
                    ins = v.tensor_tensor(blk, blk, b_bc.unsqueeze(1).broadcast_to((P, T, G_DIM)), ALU.add)
                ins.then_inc(vn_ready, 1)
            for f in range(K):
                dve.wait_ge(sp_done, f + 1)
                h = f // 2
                v.tensor_tensor(sv[:, f, :].rearrange("p (b t) -> p b t", t=P), PS[:, f, :].rearrange("p (b t) -> p b t", t=P),
                                bs_bc[:, h * P:(h + 1) * P].unsqueeze(1).broadcast_to((P, T, P)), ALU.add).then_inc(sv_ready, 1)
            dve.wait_ge(sv_ready, K)

            def gated(name, lows, factor=None):
                B = BASE[name]
                with dve.Fori(0, B.pairs) as i:
                    for s in range(2):
                        f = i * 2 + s
                        dve.wait_ge(sg_ready, SG[name] + f + 1)
                        if factor is None:
                            v.tensor_tensor(buf[s][:, :], buf[s][:, :], PS[:, 2 * s + 1, :], ALU.mult).then_inc(prod_ready, 1)
                            dve.wait_ge(prod_ready, GATED[name] + f + 1)
                            dve.sem_inc(pair_free[s], 1)
                        else:
                            v.tensor_tensor(buf[s][:, :], buf[s][:, :], PS[:, 2 * s + 1, :], ALU.mult).then_inc(pair_free[s], 1)
                            dve.wait_ge(pair_free[s], PF[name] + i + 1)
                            v.tensor_tensor(buf[s][:, :], buf[s][:, :], factor[:, f, :], ALU.mult).then_inc(prod_ready, 1)
                            dve.wait_ge(prod_ready, GATED[name] + f + 1)
                        dve.wait_ge(act_high, GATED[name] + f + 1)
                        v.tensor_tensor(lows[:, f, :], buf[s][:, :], highs_of[name][:, f, :].bitcast(F32), ALU.subtract).then_inc(gate_low, 1)

            highs_of = {"zu": mixH, "gu0": fH, "gu1": fH}
            gated("zu", mixL, sv)

            for z in (xbuf, sum_a, sum_b):
                ins = v.memset(z[:, 0:PAD], 0.0)
            steps.link(ins)
            dve.sem_inc(xb_used, 1)
            for f in range(K):
                g = f // 2
                win = POOL_WINDOWS[g]
                dve.wait_ge(xb_ready, f + 1)
                if f % 2:
                    dve.sem_inc(pair_free[g % 2], 1)
                cur, step, nxt = xbuf, 1, [sum_a, sum_b]
                while step < win:
                    dst = nxt[0]
                    nxt.reverse()
                    steps.link(v.tensor_tensor(dst[:, PAD:], cur[:, PAD:], cur[:, PAD - step:PAD + S - step], ALU.add))
                    cur, step = dst, 2 * step
                steps.link(v.scalar_tensor_tensor(pooled[:, f, :], cur[:, PAD:], 1.0 / win, xbuf[:, PAD:], ALU.mult, ALU.subtract))
                head = pooled[:, f, 0:PAD]
                steps.link(v.tensor_tensor(head, cur[:, PAD:2 * PAD], inv_count[:, g * PAD:(g + 1) * PAD], ALU.mult))
                v.tensor_tensor(head, head, xbuf[:, PAD:2 * PAD], ALU.subtract).then_inc(pooled_ready, 1)
                dve.wait_ge(pooled_ready, f + 1)
                dve.sem_inc(xb_used, 1)
            for f in range(K):
                dve.wait_ge(py_done, f + 1)
                v.tensor_scalar(sv[:, f, :], PS[:, f, :], vec[:, ROWS["pool_b"] + f:ROWS["pool_b"] + f + 1],
                                vec[:, ROWS["pool_scale"] + f:ROWS["pool_scale"] + f + 1], ALU.add, ALU.mult).then_inc(yb_ready, 1)
            dve.wait_ge(yb_ready, K)
            with dve.Fori(0, 2) as i:
                for s in range(2):
                    for m in range(2):
                        f = i * 4 + (2 * s + m)
                        dve.wait_ge(sg_ready, SG["zb"] + f + 1)
                        if m:
                            dve.sem_inc(pair_free[s], 1)
                        v.tensor_tensor(buf[m][:, :], buf[m][:, :], sv[:, f, :], ALU.mult).then_inc(prod_ready, 1)
                    for m in range(2):
                        f = i * 4 + (2 * s + m)
                        dve.wait_ge(act_high, GATED["zb"] + f + 1)
                        v.tensor_tensor(mixL[:, f + K, :], buf[m][:, :], mixH[:, f + K, :].bitcast(F32), ALU.subtract).then_inc(gate_low, 1)

            def deepnorm(b, name, t):
                wait_y(dve, b, name, t)
                if t:
                    if name == "oout":
                        dve.wait_ge(tr_done, T * TR[name] + t)
                if t == 0:
                    dve.wait_ge(gate_ready, b + 1)
                xt = x[:, t, :]
                steps.link(v.tensor_tensor(hf[:, :], flat2(2 * t), gains[:, 0, :], ALU.mult))
                steps.link(v.scalar_tensor_tensor(xt, xt, ALPHA, hf[:, :], ALU.mult, ALU.add))
                for j in range(2):
                    ins = v.bn_stats(bn[:, j, :], x[:, t, j * S:(j + 1) * S])
                steps.link(ins)
                v.bn_aggr(mv[:, t, :], bn[:, 0:2, :]).then_inc(ln_stat, 1)

            def deepnorm_end(b, n, t):
                xt = x[:, t, :]
                dve.wait_ge(sqrt_ready, n)
                dve.wait_ge(gains_in, 32 if b == 0 else 80)
                steps.link(v.reciprocal(stat[:, t, 2:3], stat[:, t, 1:2]))
                steps.link(v.tensor_scalar(xt, xt, mv[:, t, 0:1], stat[:, t, 2:3], ALU.subtract, ALU.mult))
                steps.link(v.tensor_tensor(xt, xt, gains[:, 1, :], ALU.mult))
                v.tensor_tensor(xt, xt, gains[:, 2, :], ALU.add).then_inc(x_ready, 1)
                dve.wait_ge(x_ready, T * b + t + 1)

            def low_tile(q, t, b):
                dve.wait_ge(h_high, T * q + t + 1)
                v.tensor_tensor(tile(hL, t), two(b), tile(hH, t).bitcast(F32), ALU.subtract).then_inc(h_ready, 1)

            def prenorm(n, t, g, q):
                dve.wait_ge(sqrt_ready, n)
                steps.link(v.reciprocal(stat[:, t, 5:6], stat[:, t, 4:5]))
                v.scalar_tensor_tensor(hf[:, :], x[:, t, :], stat[:, t, 5:6], gains[:, g, :], ALU.mult, ALU.mult).then_inc(xhat_ready, 1)

            for t in range(T):
                deepnorm(0, "eout", t)
                if t:
                    low_mod(TR["eout"], t - 1)
                deepnorm_end(0, t + 1, t)
            low_mod(TR["eout"], T - 1)

            dve.wait_ge(late_in, 32)
            steps.link(v.tensor_copy(ang[:, :], pos[:, :]))
            steps.link(v.tensor_scalar(ang[:, :], ang[:, :], freq, None, ALU.mult))
            steps.link(v.tensor_scalar(turns[:, :], ang[:, :], 1.0 / TWO_PI, ROUND, ALU.mult, ALU.add))
            steps.link(v.tensor_scalar(turns[:, :], turns[:, :], ROUND, None, ALU.subtract))
            steps.link(v.scalar_tensor_tensor(rest[:, :], turns[:, :], -PI_1, ang[:, :], ALU.mult, ALU.add))
            steps.link(v.scalar_tensor_tensor(rest[:, :], turns[:, :], -PI_2, rest[:, :], ALU.mult, ALU.add))
            steps.link(v.scalar_tensor_tensor(rest[:, :], turns[:, :], -PI_3, rest[:, :], ALU.mult, ALU.add))
            steps.link(v.tensor_scalar(rest[:, :], rest[:, :], 3.1415925, -3.1415925, ALU.min, ALU.max))
            steps.link(v.scalar_tensor_tensor(turns[:, :], rest[:, :], -1.0, rest[:, :], ALU.mult, ALU.max))
            v.tensor_scalar(turns[:, :], turns[:, :], -1.0, np.pi / 2, ALU.mult, ALU.add).then_inc(rest_ready, 1)
            gate_diag(1, ones1, diag1)

            dve.wait_ge(lat_sqrt, 1)
            steps.link(v.reciprocal(stat[:, :, 4:6], stat[:, :, 2:4]))
            for t in range(T):
                v.tensor_scalar(latn[:, t, 0:QR], PS[:, t, 0:QR], stat[:, t, 4:5], None, ALU.mult)
                v.tensor_scalar(latn[:, t, QR:QR + KVR], PS[:, t, QR:QR + KVR], stat[:, t, 5:6], None, ALU.mult)
                for j in range(2):
                    c = QR + KVR + ROPE * j
                    ins = v.tensor_copy(latn[:, t, c:c + ROPE], PS[:, t, QR + KVR:LATENT])
            ins.then_inc(latn_ready, 1)
            dve.wait_ge(kr_turn, 1)
            dve.wait_ge(sin_ready, 1)
            v.tensor_tensor(kr[:, :], kraw[:, :], cosM[:, :], ALU.mult)
            steps.link(v.tensor_tensor(qr[:, :], PS[:, 0, :], sinM[:, :], ALU.mult))
            v.tensor_tensor(kr[:, :], kr[:, :], qr[:, :], ALU.add).then_inc(kr_ready, 1)

            with dve.Fori(0, 8) as i:
                PER = 4 + 8 * 4
                steps.loop(i, PER)
                dve.wait_ge(proj_done, i * 3 + 2)
                steps.link(v.tensor_copy(kn[:, :, :], PS[:, 4:6, :]))
                dve.wait_ge(proj_done, i * 3 + 3)
                v.tensor_copy(vh[:, :, :], PS[:, 6:8, :].rearrange("p a (b n) -> p (a b) n", b=2)).then_inc(kv_ready, 1)
                dve.wait_ge(qa_ready, i * 2 + 1)
                steps.link(v.tensor_tensor(qr[:, :], qraw[:, :], cosM[:, :], ALU.mult))
                dve.wait_ge(q_turn, i + 1)
                steps.link(v.tensor_tensor(qraw[:, :], PS[:, 3, :], sinM[:, :], ALU.mult))
                v.tensor_tensor(qr[:, :], qr[:, :], qraw[:, :], ALU.add).then_inc(qr_ready, 1)

                def top(u):
                    q = u % T
                    w = (q + 1) * P
                    sc = PS[:, 2 + u % 2, 0:w]
                    dve.wait_ge(s_done, i * 8 + u + 1)
                    steps.link(v.memset(PS[0:64, 2 + u % 2, q * P + 64:w], MASKED))
                    steps.link(v.reduce_max(soft[:, u % 2, 0, 0:1], sc, AX))
                    v.tensor_scalar(soft[:, u % 2, 1, 0:1], soft[:, u % 2, 0, 0:1], -MLA_SCALE, None, ALU.mult).then_inc(m_ready, 1)

                def norm(u):
                    w = (u % T + 1) * P
                    dve.wait_ge(e_ready, i * 8 + u + 1)
                    steps.link(v.reciprocal(soft[:, u % 2, 3, 0:1], soft[:, u % 2, 2, 0:1]))
                    v.tensor_scalar(pm[u % 2][:, 0:w], pm[u % 2][:, 0:w], soft[:, u % 2, 3, 0:1], None, ALU.mult).then_inc(p_ready, 1)

                top(0)
                top(1)
                for u in range(8):
                    norm(u)
                    if u + 2 < 8:
                        top(u + 2)
                dve.wait_ge(sz_ready, i + 1)
                for h in range(2):
                    dve.wait_ge(pv_done, i * 2 + h + 1)
                    v.tensor_tensor(oz[:, i * 2 + h, :], PS[:, 6 + h, :], sz[:, h, :], ALU.mult).then_inc(oz_ready, 1)
                steps.link(v.tensor_copy(stat[:, 0, 7:8], soft[:, 1, 3, 0:1]))
                for _ in range(PER - (steps.n - steps.first)):
                    steps.link(v.tensor_copy(stat[:, 0, 7:8], soft[:, 1, 3, 0:1]))
            steps.done(8)

            dve.wait_ge(oz_ready, HEADS + CREDIT)
            for h in range(HEADS):
                dve.wait_ge(oh_ready, h + 1)
                v.tensor_tensor(oL[:, h, :], oz[:, h, :], oH[:, h, :].bitcast(F32), ALU.subtract).then_inc(ol_ready, 1)

            n = T
            for t in range(T):
                deepnorm(1, "oout", t)
                if t:
                    low_tile(TR["oout"], t - 1, 2 * t - 2)
                deepnorm_end(1, n + 2 * t + 1, t)
                prenorm(n + 2 * t + 2, t, 3, TR["oout"])
            low_tile(TR["oout"], T - 1, 2 * T - 2)
            n += 2 * T

            steps.link(v.memset(cw[:, 0:2], 0.0))
            with dve.Fori(0, 4) as i:
                steps.loop(i, 2 * 3)
                for s in range(2):
                    f = i * 2 + s

                    def tap(j):
                        return vec[:, bass.ds(f + (ROWS["conv"] + K * j), 1)]

                    dve.wait_ge(sg_ready, SG["cu"] + f + 1)
                    v.tensor_tensor(cw[:, 2:], buf[s][:, :], PS[:, 2 * s + 1, :], ALU.mult).then_inc(pair_free[s], 1)
                    dve.wait_ge(pair_free[s], PF["cu"] + i + 1)
                    steps.link(v.tensor_scalar(cv[:, :], cw[:, 0:S], tap(0), None, ALU.mult))
                    steps.link(v.scalar_tensor_tensor(cv[:, :], cw[:, 1:1 + S], tap(1), cv[:, :], ALU.mult, ALU.add))
                    steps.link(v.scalar_tensor_tensor(yc[:, f, :], cw[:, 2:], tap(2), cv[:, :], ALU.mult, ALU.add))
            steps.done(4)
            B = BASE["b"]
            with dve.Fori(0, 2) as i:
                for s in range(2):
                    dve.wait_ge(used[s], B.use[s] + i + 1)
                    for m in range(2):
                        f = i * 4 + (2 * s + m)
                        dve.wait_ge(gate_low, GATED["b"] + f + 1)
                        v.tensor_tensor(buf[m][:, :], PS[:, 2 * s + m, :], yc[:, f, :], ALU.mult).then_inc(prod_ready, 1)
                    for m in range(2):
                        f = i * 4 + (2 * s + m)
                        dve.wait_ge(act_high, GATED["b"] + f + 1)
                        v.tensor_tensor(yL[:, f, :], buf[m][:, :], yH[:, f, :].bitcast(F32), ALU.subtract).then_inc(gate_low, 1)
                    dve.sem_inc(pair_free[s], 1)

            def boundary(name, n, pre, loaded):
                b = BOUNDARY.index(name)
                dve.wait_ge(gains_in, loaded)
                for t in range(T):
                    n += 1
                    dve.wait_ge(sqrt_ready, n)
                    if t and pre:
                        dve.wait_ge(tr_done, T * TR[name] + t)
                    steps.link(v.reciprocal(stat[:, t, 2:3], stat[:, t, 1:2]))
                    steps.link(v.scalar_tensor_tensor(hf[:, :], flat2(2 * t), stat[:, t, 2:3], gains[:, 0, :], ALU.mult, ALU.mult))
                    v.tensor_tensor(x[:, t, :], x[:, t, :], hf[:, :], ALU.add).then_inc(x_ready, 1)
                    dve.wait_ge(x_ready, T * b + t + 1)
                    if not pre:
                        continue
                    if t:
                        low_tile(TR[name], t - 1, 2 * t - 2)
                    n += 1
                    prenorm(n, t, 1, TR[name])
                if pre:
                    low_tile(TR[name], T - 1, 2 * T - 2)
                return n

            n = boundary("aout", n, True, 112)
            gated("gu0", fL)
            n = boundary("dn0", n, True, 160)

            dve.wait_ge(late_in, 48)
            dve.wait_ge(k2_raw, 1)
            cos2 = cosB.unsqueeze(1).broadcast_to((P, 2, S))
            sin2 = sinB.unsqueeze(1).broadcast_to((P, 2, S))
            steps.link(v.tensor_tensor(q2[:, :, :], q2raw[:, :, :], cos2, ALU.mult))
            dve.wait_ge(k2_turn, 1)
            steps.link(v.tensor_tensor(q2tmp[:, :, :], PS[:, 0:2, :], sin2, ALU.mult))
            v.tensor_tensor(q2[:, :, :], q2[:, :, :], q2tmp[:, :, :], ALU.add).then_inc(k2_rot, 1)
            dve.wait_ge(used[1], end_use("kv", 1))
            v.tensor_copy(vall[:, :, :], PS[:, 2:4, :].rearrange("p a (b n) -> p (a b) n", b=2)).then_inc(v2_ready, 1)
            for t in range(T):
                dve.wait_ge(tr_done, T * (TR["q"] - 0) + t)
                v.scalar_tensor_tensor(hf[:, :], x[:, t, :], stat[:, t, 5:6], gains[:, 2, :], ALU.mult, ALU.mult).then_inc(xhat_ready, 1)
                if t:
                    low_tile(TR["q"], t - 1, 4 + 2 * ((t - 1) % 2))
            low_tile(TR["q"], T - 1, 4 + 2 * ((T - 1) % 2))
            dve.wait_ge(kd_ready, 1)

            with dve.Fori(0, 2) as i:
                PER = 2 * (2 + 8 * 5)
                steps.loop(i, PER)
                for s in range(2):
                    g = i * 2 + s
                    dve.wait_ge(q2_raw, g + 1)
                    steps.link(v.tensor_tensor(q2[:, :, :], q2raw[:, :, :], cos2, ALU.mult))
                    dve.wait_ge(q2_turn, g + 1)
                    steps.link(v.tensor_tensor(q2tmp[:, :, :], PS[:, 2:4, :], sin2, ALU.mult))
                    v.tensor_tensor(q2[:, :, :], q2[:, :, :], q2tmp[:, :, :], ALU.add).then_inc(q2_ready, 1)

                    def top2(u):
                        w = P if u % T == 0 else 0
                        st = soft[:, u % 2, :, :]
                        sink = sinks[:, bass.ds(g * 4 + 2 * (u // T), 2)]
                        sc = sS[u % 2][:, :, w:]
                        dve.wait_ge(s2_done, g * 8 + u + 1)
                        steps.link(v.tensor_tensor(sc, PS[:, 4 + 2 * (u % 2):6 + 2 * (u % 2), w:2 * P],
                                                   window[:, w:].unsqueeze(1).broadcast_to((P, 2, 2 * P - w)), ALU.add))
                        steps.link(v.reduce_max(st[:, 0, :], sc, AX))
                        steps.link(v.scalar_tensor_tensor(st[:, 1, :], st[:, 0, :], SW_SCALE, sink, ALU.mult, ALU.max))
                        v.tensor_tensor(st[:, 3, :], sink, st[:, 1, :], ALU.subtract)
                        v.tensor_scalar(st[:, 2, :], st[:, 1, :], -1.0, None, ALU.mult).then_inc(m2_ready, 1)

                    def norm2(u):
                        w = P if u % T == 0 else 0
                        st = soft[:, u % 2, :, :]
                        dve.wait_ge(e2_ready, g * 8 + u + 1)
                        steps.link(v.tensor_tensor(st[:, 6, :], st[:, 5, :], st[:, 4, :], ALU.add))
                        steps.link(v.reciprocal(st[:, 7, :], st[:, 6, :]))
                        pr = p2[u % 2][:, :, w:]
                        v.tensor_tensor(pr, pr, st[:, 7, :].unsqueeze(2).broadcast_to((P, 2, 2 * P - w)), ALU.mult).then_inc(p2_ready, 1)

                    top2(0)
                    top2(1)
                    for u in range(8):
                        norm2(u)
                        if u + 2 < 8:
                            top2(u + 2)
                    for j in range(2):
                        dve.wait_ge(o2_high, g * 2 + j + 1)
                        v.tensor_tensor(o2L[:, g * 2 + j, :], PS[:, j, :], o2H[:, g * 2 + j, :].bitcast(F32), ALU.subtract).then_inc(o2_low, 1)
            steps.done(2)
            n = boundary("wo", n, True, 192)
            gated("gu1", fL)
            n = boundary("dn1", n, False, 208)

        @block.tensor
        def _(pe):
            mm, tr = nc.tensor.matmul, nc.tensor.transpose

            def mm3(dst, lh, ll, rh, rl, first, last):
                mm(dst, lh, rh, start=first, stop=False, skip_group_check=True)
                mm(dst, lh, rl, start=False, stop=False, skip_group_check=True)
                return mm(dst, ll, rh, start=False, stop=last, skip_group_check=True)

            def wcols(w, s):
                return w[s][:, :].rearrange("p (k n) -> p k n", n=256)

            def in_stage(name):
                B = BASE[name]
                with pe.Fori(0, B.pairs) as i:
                    for s in range(2):
                        pe.wait_ge(w_split[s], B.split[s] + i + 1)
                        pe.wait_ge(pair_free[s], PF[name] + i)
                        for m in range(2):
                            for k in range(K):
                                c = slice(m * P, (m + 1) * P)
                                ins = mm3(PS[:, 2 * s + m, :], wcols(WH, s)[:, k, c], wcols(WL, s)[:, k, c],
                                          hH[:, k, :], hL[:, k, :], k == 0, k == K - 1)
                        ins.then_inc(used[s], 1)

            def out_stage(name, lh, ll, ready, depth=2):
                B = BASE[name]
                kt = 0
                pairs = B.pairs
                for j in range(pairs - 1):
                    for s in range(2):
                        pe.wait_ge(w_split[s], B.split[s] + j + 1)
                        for d in range(2):
                            ready(kt)
                            for t in range(T):
                                for n in range(2):
                                    c = slice(d * D + n * S, d * D + (n + 1) * S)
                                    ins = mm3(PS[:, 2 * t + n, :], lh[:, kt, t * P:(t + 1) * P], ll[:, kt, t * P:(t + 1) * P],
                                              WH[s][:, c], WL[s][:, c], kt == 0, False)
                            kt += 1
                        ins.then_inc(used[s], 1)
                for s in range(2):
                    pe.wait_ge(w_split[s], B.split[s] + pairs)
                last = 2 * depth - 1
                ready(kt + last)
                for t in range(T):
                    for j in range(2 * depth):
                        s, d = j // depth, j % depth
                        for n in range(2):
                            c = slice(d * D + n * S, d * D + (n + 1) * S)
                            ins = mm3(PS[:, 2 * t + n, :], lh[:, kt + j, t * P:(t + 1) * P], ll[:, kt + j, t * P:(t + 1) * P],
                                      WH[s][:, c], WL[s][:, c], False, j == last)
                        if t == T - 1 and j == depth - 1:
                            ins.then_inc(used[0], 1)
                    ins.then_inc(y_ready if t < T - 1 else used[1], 1)

            def turn_tiles(q, src, ready):
                for t in range(T):
                    ready(t)
                    for k in range(K):
                        ins = tr(two(2 * t)[:, k, :], src(t)[:, k * P:(k + 1) * P], ident)
                    ins.then_inc(tr_done, 1)

            pe.wait_ge(small_in, 16 * 8)
            tr(PS[:, 0, 0:N_ROWS], rows[0:N_ROWS, :], ident[0:N_ROWS, 0:N_ROWS]).then_inc(rows_tr, 1)
            pe.wait_ge(aux_in, 16 * 5)
            for h in range(G_HEADS):
                ins = tr(PS[:, 1, h * P:(h + 1) * P], ws_sb[:, h, :], ident)
            ins.then_inc(ws_tr, 1)

            pe.wait_ge(csil_ready, 1)
            with pe.Fori(0, 12) as i:
                for s in range(2):
                    pe.wait_ge(w_full[s], (i + 1) * 16)
                    pe.wait_ge(pair_free[s], i + CREDIT)
                    for m in range(2):
                        for k in range(K):
                            ins = mm(PS[:, 6 + s, m:m + 1], wcols(raw, s)[:, k, m * P:(m + 1) * P], csil[:, k:k + 1],
                                     start=(k == 0), stop=(k == K - 1))
                    ins.then_inc(used[s], 1)

            def gate_rows(n, one, dg, b):
                pe.wait_ge(diag_ready, n)
                for k in range(K):
                    ins = mm(two(b)[:, k, :], one[:, :], dg[:, k, :], start=True, stop=True)
                ins.then_inc(gate_mm, 1)

            pe.wait_ge(wT_ready, 1)
            gate_rows(1, ones, diag, 0)
            pe.wait_ge(gate_ready, 1)
            pe.wait_ge(x_in, 16)
            pe.wait_ge(mod_ready, 1)
            turn_tiles(0, lambda t: x[:, t, :], lambda t: None)

            B = BASE["v"]
            pe.wait_ge(h_ready, T)
            for c in range(4):
                n, s = c // 2, c % 2
                pe.wait_ge(w_split[s], B.split[s] + n + 1)
                for t in range(T):
                    for k in range(4):
                        kt = 4 * s + k
                        w = slice(k * S, (k + 1) * S)
                        ins = mm3(PS[:, 4 * n + t, :], hH[:, kt, t * P:(t + 1) * P], hL[:, kt, t * P:(t + 1) * P],
                                  WH[s][:, w], WL[s][:, w], kt == 0, kt == K - 1)
                ins.then_inc(used[s], 1)
            for f in range(K):
                pe.wait_ge(vn_ready, f // 4 + 1)
                for b in range(T):
                    ins = mm(PS[:, f, b * P:(b + 1) * P], vn[:, b, f * P:(f + 1) * P], wT[:, f // 2, :], start=True, stop=True)
                ins.then_inc(sp_done, 1)
            pe.wait_ge(sv_ready, T)
            in_stage("zu")
            in_stage("xb")
            B = BASE["pool"]
            for s in range(2):
                pe.wait_ge(w_full[s], B.full[s] + 16)
                pw = raw[s][:, 0:1024].rearrange("p (j e) -> p j e", j=4)
                for g in (2 * s, 2 * s + 1):
                    pe.wait_ge(pooled_ready, 2 * g + 2 if s else K)
                    for m in range(2):
                        for k in range(2):
                            ins = mm(PS[:, 2 * g + m, :], pw[:, 2 * (g % 2) + k, m * P:(m + 1) * P], pooled[:, 2 * g + k, :],
                                     start=(k == 0), stop=(k == 1))
                        if m == 0 or g % 2 == 0:
                            ins.then_inc(py_done, 1)
                ins.then_inc(used[s], 1)
                pe.wait_ge(used[s], B.use[s] + 1)
                pe.sem_inc(py_done, 1)
            pe.wait_ge(yb_ready, K)
            in_stage("zb")
            for s in range(2):
                pe.wait_ge(pair_free[s], PF["cu"])
            out_stage("eout", mixH, mixL, lambda kt: pe.wait_ge(gate_low, 2 + kt + 1))
            turn_tiles(TR["eout"], lambda t: x[:, t, :], lambda t: pe.wait_ge(x_ready, t + 1))

            B = BASE["lat"]
            pe.wait_ge(h_ready, 2 * T)
            for s in range(2):
                pe.wait_ge(w_split[s], B.split[s] + 1)
                for t in range(T):
                    for k in range(4):
                        kt = 4 * s + k
                        w = slice(k * S, k * S + LATENT)
                        ins = mm3(PS[:, t, 0:LATENT], hH[:, kt, t * P:(t + 1) * P], hL[:, kt, t * P:(t + 1) * P],
                                  WH[s][:, w], WL[s][:, w], kt == 0, kt == K - 1)
                ins.then_inc(used[s], 1)
            gate_rows(2, ones1, diag1, 4)
            pe.wait_ge(latn_ready, 1)
            pe.wait_ge(gate_ready, 2)
            for j in range(4):
                for t in range(T):
                    ins = tr(PS[:, 4 + j, t * P:(t + 1) * P], latn[:, t, j * P:(j + 1) * P], ident)
            ins.then_inc(lat_tr, 1)
            pe.wait_ge(lat_ev, 1)
            pe.wait_ge(late_in, 32)
            mm(PS[:, 0, :], turn_m[:, :], kraw[:, :], start=True, stop=True).then_inc(kr_turn, 1)
            pe.wait_ge(kr_ready, 1)

            B = BASE["mla"]
            wn = raw[1][:, 0:512].rearrange("p (k h e) -> p k h e", k=2, h=2)
            wr = raw[1][:, 512:768].rearrange("p (k m) -> p k m", k=2)
            wk = raw[1][:, 768:1024].rearrange("p (h e) -> p h e", h=2)
            wv = raw[1][:, 1024:1280]
            with pe.Fori(0, 8) as i:
                pe.wait_ge(w_full[1], B.full[1] + (i + 1) * 16 * B.dmas[1])
                pe.wait_ge(oz_ready, i * 2 + CREDIT)
                for k in range(2):
                    mm(PS[:, 2, :], wr[:, k, :], qcT[:, k, :], start=(k == 0), stop=(k == 1))
                for h in range(2):
                    for k in range(2):
                        ins = mm(PS[:, h, :], wn[:, k, h, :], qcT[:, k, :], start=(k == 0), stop=(k == 1))
                ins.then_inc(proj_done, 1)
                for h in range(2):
                    ins = mm(PS[:, 4 + h, :], wk[:, h, :], kvT[:, :], start=True, stop=True)
                ins.then_inc(proj_done, 1)
                for t in range(T):
                    ins = mm(PS[:, 6 + t // 2, (t % 2) * 256:(t % 2 + 1) * 256], kvT[:, t * P:(t + 1) * P], wv, start=True, stop=True)
                ins.then_inc(proj_done, 1)
                pe.wait_ge(proj_done, i * 3 + 3)
                pe.sem_inc(used[1], 1)
                pe.wait_ge(qa_ready, i * 2 + 1)
                mm(PS[:, 3, :], turn_m[:, :], qraw[:, :], start=True, stop=True).then_inc(q_turn, 1)
                pe.wait_ge(w_split[0], B.split[0] + i + 1)
                pe.wait_ge(qa_ready, i * 2 + 2)

                def z_part(j):
                    m = j // 4
                    for k in (2 * (j % 4), 2 * (j % 4) + 1):
                        c = slice(m * P, (m + 1) * P)
                        ins = mm3(PS[:, m, :], wcols(WH, 0)[:, k, c], wcols(WL, 0)[:, k, c], hH[:, k, :], hL[:, k, :],
                                  k == 0, k == K - 1)
                    if j == 7:
                        ins.then_inc(used[0], 1)

                def score(u):
                    h, q = u // T, u % T
                    w = (q + 1) * P
                    if u >= 2:
                        pe.wait_ge(e_ready, i * 8 + u - 1)
                    rp = slice(h * ROPE, (h + 1) * ROPE)
                    mm(PS[:, 2 + u % 2, 0:w], qn[:, h, q * P:w], kn[:, h, 0:w], start=True, stop=False)
                    mm(PS[:, 2 + u % 2, 0:w], qr[rp, q * P:w], kr[rp, 0:w], start=False, stop=True).then_inc(s_done, 1)

                def turn(u):
                    q = u % T
                    if u >= 2:
                        pe.wait_ge(pT_ready, i * 8 + u - 1)
                    pe.wait_ge(p_ready, i * 8 + u + 1)
                    for k in range(q + 1):
                        ins = tr(PS[:, 4 + u % 2, k * P:(k + 1) * P], pm[u % 2][:, k * P:(k + 1) * P], ident)
                    ins.then_inc(t_done, 1)

                def weigh(h):
                    pe.wait_ge(pT_ready, i * 8 + T * h + T)
                    for k in range(T):
                        ins = mm(PS[:, 6 + h, k * P:], vh[:, k, h * NOPE:(h + 1) * NOPE], pT[h][:, k, k * P:],
                                 start=(k == 0), stop=(k == T - 1), skip_group_check=True)
                    ins.then_inc(pv_done, 1)

                z_part(0)
                pe.wait_ge(kv_ready, i + 1)
                pe.wait_ge(qr_ready, i + 1)
                score(0)
                score(1)
                for u in range(8):
                    if u:
                        z_part(u)
                    turn(u)
                    if u + 2 < 8:
                        score(u + 2)
                    if u == T:
                        weigh(0)
                weigh(1)
            pe.wait_ge(oz_ready, HEADS + CREDIT)
            out_stage("oout", oH, oL, lambda kt: pe.wait_ge(ol_ready, kt + 1))
            turn_tiles(TR["oout"], lambda t: hf, lambda t: pe.wait_ge(xhat_ready, t + 1))
            pe.wait_ge(h_ready, 3 * T)
            in_stage("cu")
            in_stage("b")
            for s in range(2):
                pe.wait_ge(pair_free[s], PF["gu0"])
            out_stage("aout", yH, yL, lambda kt: pe.wait_ge(gate_low, 2 + GATED["b"] + kt + 1))
            turn_tiles(TR["aout"], lambda t: hf, lambda t: pe.wait_ge(xhat_ready, T + t + 1))
            pe.wait_ge(h_ready, 4 * T)
            in_stage("gu0")
            for s in range(2):
                pe.wait_ge(pair_free[s], PF["gu1"])
            out_stage("dn0", fH, fL, lambda kt: pe.wait_ge(gate_low, 2 + GATED["gu0"] + kt + 1), 1)
            turn_tiles(TR["dn0"], lambda t: hf, lambda t: pe.wait_ge(xhat_ready, 2 * T + t + 1))

            B = BASE["kv"]
            pe.wait_ge(h_ready, 5 * T)
            pe.wait_ge(w_split[0], B.split[0] + 1)
            for m in range(2):
                for k in range(K):
                    c = slice(m * P, (m + 1) * P)
                    ins = mm3(PS[:, m, :], wcols(WH, 0)[:, k, c], wcols(WL, 0)[:, k, c], hH[:, k, :], hL[:, k, :], k == 0, k == K - 1)
            ins.then_inc(used[0], 1)
            pe.wait_ge(w_split[1], B.split[1] + 1)
            for t in range(T):
                for k in range(K):
                    ins = mm3(PS[:, 2 + t // 2, (t % 2) * 256:(t % 2 + 1) * 256], hH[:, k, t * P:(t + 1) * P], hL[:, k, t * P:(t + 1) * P],
                              wcols(WH, 1)[:, k, :], wcols(WL, 1)[:, k, :], k == 0, k == K - 1)
            ins.then_inc(used[1], 1)
            pe.wait_ge(k2_raw, 1)
            pe.wait_ge(late_in, 48)
            for m in range(2):
                ins = mm(PS[:, m, :], turn_b, q2raw[:, m, :], start=True, stop=True)
            ins.then_inc(k2_turn, 1)
            for t in range(T):
                pe.wait_ge(xhat_ready, 3 * T + t + 1)
                if t >= 2:
                    pe.wait_ge(h_ready, T * TR["q"] + t - 1)
                for k in range(K):
                    ins = tr(two(4 + 2 * (t % 2))[:, k, :], hf[:, k * P:(k + 1) * P], ident)
                ins.then_inc(tr_done, 1)
            pe.wait_ge(h_ready, 6 * T)
            pe.wait_ge(kd_ready, 1)

            B = BASE["q"]
            with pe.Fori(0, 2) as i:
                for s in range(2):
                    g = i * 2 + s
                    pe.wait_ge(w_split[s], B.split[s] + i + 1)
                    pe.wait_ge(o2_low, g * 2 + CREDIT)
                    for m in range(2):
                        for k in range(K):
                            c = slice(m * P, (m + 1) * P)
                            ins = mm3(PS[:, m, :], wcols(WH, s)[:, k, c], wcols(WL, s)[:, k, c], hH[:, k, :], hL[:, k, :], k == 0, k == K - 1)
                    ins.then_inc(used[s], 1)
                    pe.wait_ge(q2_raw, g + 1)
                    for m in range(2):
                        ins = mm(PS[:, 2 + m, :], turn_b, q2raw[:, m, :], start=True, stop=True)
                    ins.then_inc(q2_turn, 1)
                    pe.wait_ge(q2_ready, g + 1)
                    pe.wait_ge(kvg_ready, g + 1)

                    def score2(u):
                        j, q = u // T, u % T
                        if u >= 2:
                            pe.wait_ge(m2_ready, g * 8 + u - 1)
                        lo = max(q - 1, 0) * P
                        for h in range(2):
                            r = slice(h * HD, (h + 1) * HD)
                            ins = mm(PS[:, 4 + 2 * (u % 2) + h, 0 if q else P:2 * P] if q else PS[:, 4 + 2 * (u % 2) + h, P:2 * P],
                                     q2[r, j, q * P:(q + 1) * P], kg[r, lo:(q + 1) * P], start=True, stop=True)
                        ins.then_inc(s2_done, 1)

                    def turn2(u):
                        if u >= 2:
                            pe.wait_ge(p2T_ready, g * 8 + u - 1)
                        pe.wait_ge(p2_ready, g * 8 + u + 1)
                        for h in range(2):
                            for k in range(2):
                                if k or u % T:
                                    ins = tr(PS[:, 2 + u % 2, (2 * h + k) * P:(2 * h + k + 1) * P], p2[u % 2][:, h, k * P:(k + 1) * P], ident)
                        ins.then_inc(t2_done, 1)

                    def weigh2(u):
                        j, q = u // T, u % T
                        pe.wait_ge(p2T_ready, g * 8 + u + 1)
                        for h in range(2):
                            ks = range(2) if q else range(1, 2)
                            for k in ks:
                                ins = mm(PS[h * HD:(h + 1) * HD, j, q * P:(q + 1) * P], vg[:, q - 1 + k, :], p2T[u % 2][:, 2 * h + k, :],
                                         start=(k == ks[0]), stop=(k == 1), skip_group_check=True)
                        ins.then_inc(pv2_done, 1)

                    score2(0)
                    score2(1)
                    for u in range(8):
                        turn2(u)
                        if u + 2 < 8:
                            score2(u + 2)
                        if u:
                            weigh2(u - 1)
                    weigh2(7)
            out_stage("wo", o2H, o2L, lambda kt: pe.wait_ge(o2_low, CREDIT + K))
            turn_tiles(TR["wo"], lambda t: hf, lambda t: pe.wait_ge(xhat_ready, 4 * T + t + 1))
            pe.wait_ge(h_ready, 7 * T)
            in_stage("gu1")
            for s in range(2):
                pe.wait_ge(pair_free[s], PF["gu1"] + 11)
            out_stage("dn1", fH, fL, lambda kt: pe.wait_ge(gate_low, 2 + GATED["gu1"] + kt + 1), 1)


_LAYOUT = [
    ("x", "x", (S, D)), ("c", "c", (1, D)), ("positions", "positions", (1, S)),
    ("ada_w", "ada_w", (DEPTH, D, 3 * D)), ("ada_b", "ada_b", (DEPTH, 3 * D)), ("ln_g", "ln_g", (DEPTH, D)), ("ln_b", "ln_b", (DEPTH, D)),
    ("e_w_in", "e_w_in", (D, 5 * D)), ("gmlp_norm_g", "gmlp_norm_g", (1, G_DIM)), ("gmlp_norm_b", "gmlp_norm_b", (1, G_DIM)),
    ("gmlp_ws", "gmlp_ws", (G_HEADS, P, P)), ("gmlp_bs", "gmlp_bs", (1, G_HEADS * P)), ("pool_w", "pool_w", (4, 256, 256)),
    ("pool_b", "pool_b", (1, D)), ("pool_scale", "pool_scale", (1, D)), ("e_w_out", "e_w_out", (2 * D, D)),
    ("o_w_in", "o_w_in", (D, LATENT + HEADS * NOPE)), ("mla_q_norm_g", "q_g", (1, QR)), ("mla_kv_norm_g", "kv_g", (1, KVR)),
    ("mla_w_uq", "mla_w_uq", (QR, HEADS, NOPE + ROPE)), ("mla_w_uk", "mla_w_uk", (KVR, HEADS, NOPE)),
    ("mla_w_uv", "mla_w_uv", (KVR, HEADS, NOPE)), ("o_w_out", "o_w_out", (2 * D, D)),
    ("a_pre_norm_2", "a_pre", (1, D)), ("a_w_in_2", "a_w_in", (D, 3 * D)), ("a_conv_w_2", "conv", (3, D)), ("a_w_out_2", "a_w_out", (D, D)),
    ("a_post_norm_2", "a_post", (1, D)), ("ffn_pre_norm_2", "f_pre", (DEPTH, D)), ("ffn_w_gate_up_2", "f_gate_up", (DEPTH, D, 2 * D_FF)),
    ("ffn_w_down_2", "f_down", (DEPTH, D_FF, D)), ("ffn_post_norm_2", "f_post", (DEPTH, D)), ("kv_norm_2", "kv_norm", (1, D)),
    ("w_kv_2", "w_kv", (D, 2 * KVH * HD)), ("b_pre_norm_2", "b_pre", (1, D)), ("b_w_q_2", "b_w_q", (D, D)), ("b_sinks_2", "b_sinks", (1, 16)),
    ("b_w_o_2", "b_w_o", (D, D)), ("b_post_norm_2", "b_post", (1, D)),
]


def kernel(**inputs):
    import numpy as _np
    import concourse.bacc as _bacc
    from concourse import mybir as _mybir
    from concourse.bass_utils import run_bass_kernel_spmd as _run

    nc = _bacc.Bacc("TRN2", target_bir_lowering=False, num_devices=1)
    arrays, args = {}, {}
    given = [(name, _np.ascontiguousarray(inputs[src]).reshape(shape)) for src, name, shape in _LAYOUT]
    for name, value in given + list(constants().items()):
        arrays[f"in_{name}"] = value
        args[name] = nc.dram_tensor(f"in_{name}", value.shape, _mybir.dt.from_np(value.dtype), kind="ExternalInput").ap()
    out = nc.dram_tensor("out_x", (S, D), F32, kind="ExternalOutput").ap()
    program(nc, args, out)
    r = _run(nc, [arrays], core_ids=[0])
    return r.results[0]["out_x"].reshape(1, S, D)
```

```python
from contextlib import ExitStack

import numpy as np
import concourse.bass as bass
from concourse import mybir

F32 = mybir.dt.float32
F32R = mybir.dt.float32r
I32 = mybir.dt.int32
ALU = mybir.AluOpType
ACT = mybir.ActivationFunctionType
AX = mybir.AxisListType.X

P = 128
S = 512
T = S // P
D = 1024
K = D // P
CHUNK = 2048
DEPTH = 2

G_HEADS, G_DIM, G_HALF = 4, 256, 64
POOL_WINDOWS = (2, 4, 8, 16)
PAD = 16
MIX = 16
LN_EPS = 1e-5
ALPHA = (2.0 * DEPTH) ** 0.25
HEADS, NOPE, ROPE, QR, KVR = 16, 128, 64, 256, 128
LATENT = QR + KVR + ROPE
MLA_SCALE = (NOPE + ROPE) ** -0.5
MASKED = -1e30
HD, KVH, GROUP = 64, 4, 4
SW_SCALE = HD ** -0.5
EPS2 = 1e-6
F_TILES = 2816 // P
D_FF = 2816

TWO_PI = 2.0 * np.pi
PI_1 = 6.28125
PI_2 = float(np.float32(np.round((TWO_PI - PI_1) * 2 ** 19) / 2 ** 19))
PI_3 = float(TWO_PI - PI_1 - PI_2)
ROUND = 12582912.0

ROWS = {}
_n = 0
for _name, _count in (("ada_b", 48), ("c", 8), ("pool_b", 8), ("pool_scale", 8), ("q_g", 2), ("kv_g", 1), ("conv", 24),
                      ("ln_g", 8), ("ln_b", 8)):
    ROWS[_name] = _n
    _n += _count
N_ROWS = _n

RING = [
    ("v", 2, ("split", "split"), (2, 2)),
    ("xb", 2, ("split", "split"), (2, 2)),
    ("zu", 4, ("split", "split"), (2, 2)),
    ("pool", 1, ("split", "split"), (2, 2)),
    ("zb", 2, ("split", "split"), (2, 2)),
    ("eout", 4, ("split", "split"), (2, 2)),
    ("lat", 1, ("split", "split"), (2, 2)),
    ("mla", 8, ("split", "raw"), (2, 6)),
    ("oout", 4, ("split", "split"), (2, 2)),
    ("cu", 4, ("split", "split"), (2, 2)),
    ("b", 2, ("split", "split"), (2, 2)),
    ("aout", 2, ("split", "split"), (2, 2)),
    ("gu0", 11, ("split", "split"), (2, 2)),
    ("dn0", 6, ("split", "split"), (2, 2)),
    ("kv", 1, ("split", "split"), (2, 2)),
    ("q", 2, ("split", "split"), (2, 2)),
    ("wo", 2, ("split", "split"), (2, 2)),
    ("gu1", 11, ("split", "split"), (2, 2)),
    ("dn1", 6, ("split", "split"), (2, 2)),
]


class Base:

    def __init__(self, pairs, kinds, dmas, full, use, split):
        self.pairs, self.kinds, self.dmas = pairs, kinds, dmas
        self.full, self.use, self.split = tuple(full), tuple(use), tuple(split)


BASE = {}
_full, _use, _split = [0, 0], [0, 0], [0, 0]
for _name, _pairs, _kinds, _dmas in RING:
    BASE[_name] = Base(_pairs, _kinds, _dmas, _full, _use, _split)
    for _s in range(2):
        _full[_s] += 16 * _dmas[_s] * _pairs
        _use[_s] += _pairs
        _split[_s] += _pairs * (_kinds[_s] == "split")
NAMES = [r[0] for r in RING]

GATED = {}
_n = 0
for _name, _count in (("zu", 8), ("zb", 8), ("b", 8), ("gu0", F_TILES), ("gu1", F_TILES)):
    GATED[_name] = _n
    _n += _count


ADA_FIRST = 2 * K // 2
ADA_AT, _n = {}, 0
for _name in ("xb", "zu", "zb"):
    ADA_AT[_name] = _n
    _n += 2 * BASE[_name].pairs
ADA_END = _n
assert 2 * K + 2 * ADA_END == 3 * K * DEPTH


class Steps:

    def __init__(self, eng, sem):
        self.eng, self.sem, self.n, self.off = eng, sem, 0, 0

    def link(self, ins):
        ins.then_inc(self.sem, 1)
        self.n += 1
        self.eng.wait_ge(self.sem, self.off + self.n)

    def loop(self, i, per):
        self.off, self.first, self.per = i * per, self.n, per

    def done(self, count):
        assert self.n - self.first == self.per, (self.n - self.first, self.per)
        self.n = self.first + self.per * count
        self.off = 0


def constants():
    ident = np.eye(P, dtype=np.float32)
    inv = np.ones((P, len(POOL_WINDOWS) * PAD), np.float32)
    for g, w in enumerate(POOL_WINDOWS):
        for t in range(PAD):
            inv[:, g * PAD + t] = np.float32(1.0) / np.float32(min(t + 1, w))
    r = np.arange(P)
    half = ROPE // 2
    freq = (np.float32(1.0) / (np.float32(10000.0) ** (np.arange(0, ROPE, 2, dtype=np.float32) / np.float32(ROPE)))).astype(np.float32)
    freq_col = freq[r % half][:, None].astype(np.float32)
    turn_m = np.zeros((P, P), np.float32)
    for m in range(P):
        low = (m % ROPE) < half
        turn_m[m + half if low else m - half, m] = -1.0 if low else 1.0
    rot, rh = HD // 4, HD // 8
    inv_freq = (np.float32(500000.0) ** (-np.arange(0, rot, 2, dtype=np.float32) / np.float32(rot))).astype(np.float32)
    ang = (np.arange(S, dtype=np.float32)[:, None] * inv_freq[None, :]).astype(np.float32)
    cos_b, sin_b = np.ones((P, S), np.float32), np.zeros((P, S), np.float32)
    turn_b = np.zeros((P, P), np.float32)
    for m in range(P):
        d = m % HD
        if d < rot:
            cos_b[m], sin_b[m] = np.cos(ang[:, d % rh]), np.sin(ang[:, d % rh])
            turn_b[m + rh if d < rh else m - rh, m] = -1.0 if d < rh else 1.0
    qi, kj = np.arange(P)[:, None], np.arange(2 * P)[None, :]
    diff = P + qi - kj
    window = np.where((diff >= 0) & (diff < P), 0.0, MASKED).astype(np.float32)
    return {
        "k_small": np.concatenate([ident, inv, freq_col, np.ones((P, 1))], axis=1).astype(np.float32),
        "k_turn_m": turn_m,
        "k_swa": np.concatenate([turn_b, window, cos_b, sin_b], axis=1).astype(np.float32),
    }


N_INV = len(POOL_WINDOWS) * PAD



UNITS = KVH * T
CREDIT = 1


def program(nc, a, out):
    with ExitStack() as ctx:

        def sem(name):
            return ctx.enter_context(nc.semaphore(name))

        KB = 1024
        arena = ctx.enter_context(nc.sbuf_tensor("arena", [P, 206 * KB // 4], F32))
        start = nc.sbuf_base - 206 * KB

        def at(name, offset, shape, dt=F32):
            return nc.alloc_sbuf_tensor_at(name, shape, dt, offset=start + offset)

        raw = [at(f"w_raw{s}", 8 * KB * s, [P, CHUNK]) for s in range(2)]
        WH = [at(f"w_high{s}", (16 + 8 * s) * KB, [P, CHUNK], F32R) for s in range(2)]
        WL = [at(f"w_low{s}", (32 + 8 * s) * KB, [P, CHUNK], F32R) for s in range(2)]
        ZB = 48 * KB
        hH = at("h_high", ZB, [P, K, S], F32R)
        hL = at("h_low", ZB + 16 * KB, [P, K, S], F32R)
        scaled = at("scaled", ZB + 16 * KB, [P, K, S])
        x = at("x", 80 * KB, [P, T, D])
        ZD = 96 * KB
        gains = at("gains", 184 * KB, [P, 4, D])
        hf = at("hf", 200 * KB, [P, D])
        buf = [at(f"gate_buf{m}", (200 + 2 * m) * KB, [P, S]) for m in range(2)]
        ofs = 204 * KB

        def tiny(name, shape):
            nonlocal ofs
            got = at(name, ofs, shape)
            size = 4
            for d in shape[1:]:
                size *= d
            ofs += (size + 31) // 32 * 32
            assert ofs <= 206 * KB
            return got

        small = tiny("small", [P, P + N_INV + 2])
        ident, inv_count, freq = small[:, 0:P], small[:, P:P + N_INV], small[:, P + N_INV:P + N_INV + 1]
        one_col = small[:, P + N_INV + 1:P + N_INV + 2]
        vec = tiny("vec", [P, N_ROWS])
        mod = tiny("mod", [P, 48])
        csil = tiny("csil", [P, K])
        stat = tiny("stat", [P, T, 8])
        bn = tiny("bn", [P, 8, 6])
        mv = tiny("mv", [P, 8, 2])
        eps = tiny("eps", [P, 2])
        sinks = tiny("sinks", [P, 16])

        def dz(name, offset, shape, dt=F32):
            return at(name, ZD + 4 * offset, shape, dt)

        sv = dz("sv", 0, [P, K, S])
        mixH = dz("mix_high", 4096, [P, MIX, S], F32R)
        mixL = dz("mix_low", 12288, [P, MIX, S], F32R)
        pooled = dz("pooled", 8192, [P, K, S])
        vn = dz("v_norm", 16384, [P, T, D])
        xbuf, sum_a, sum_b = (dz(n, 20480 + 528 * j, [P, PAD + S]) for j, n in enumerate(("xbuf", "sum_a", "sum_b")))
        xbufs = [xbuf, hf[:, 0:PAD + S]]
        poolH = dz("pool_high", 16384, [P, K, S], F32R)
        poolL = dz("pool_low", 8192, [P, K, S], F32R)
        ada_raw = [dz(f"ada_raw{c}", 2048 * c, [P, CHUNK]) for c in range(ADA_FIRST)]
        ada_buf = [gains[:, 3 * m, :].rearrange("p (k n) -> p k n", k=K) for m in range(2)]
        ada_acc = [dz(f"ada_acc{m}", 22064 + P * m, [P, P]) for m in range(2)]
        ones = dz("ones", 20480, [P, P])
        diag = dz("diag", 20480 + P, [P, K, P])
        mod_tmp = dz("mod_tmp", 0, [P, D])
        g_bc = gains[:, 1, 0:G_DIM]
        b_bc = gains[:, 1, G_DIM:2 * G_DIM]
        bs_bc = gains[:, 1, 2 * G_DIM:4 * G_DIM]
        ws_sb = gains[:, 2, 0:S].rearrange("p (h s) -> p h s", h=G_HEADS)
        wT = gains[:, 2, S:2 * S].rearrange("p (h t) -> p h t", h=G_HEADS)
        rows = hf[:, 0:P]
        x_hat = [hf, gains[:, 3, :]]
        oz = dz("o_gated", 0, [P, HEADS, S])
        qcT = dz("qc_t", 8192, [P, 2, S])
        kvT = dz("kv_t", 9216, [P, S])
        kr = dz("k_rope", 9728, [P, S])
        cosM, sinM = dz("cos_m", 10240, [P, S]), dz("sin_m", 10752, [P, S])
        turn_m = dz("turn_m", 11264, [P, P])
        qn = dz("q_nope", 11392, [P, 2, S])
        qraw = dz("q_raw", 12416, [P, S])
        ones1, diag1 = dz("ones1", 11392, [P, P]), dz("diag1", 11520, [P, K, P])
        qr = dz("q_rope", 12928, [P, S])
        kn = dz("k_nope", 13440, [P, 2, S])
        vh = dz("v_heads", 14464, [P, T, 2 * NOPE])
        sz = dz("silu_z", 15488, [P, 2, S])
        pm = [dz(f"probs{u}", 16512 + 512 * u, [P, S]) for u in range(2)]
        pT = [dz(f"probs_t{u}", 17536 + 2048 * u, [P, T, S]) for u in range(2)]
        kraw = dz("k_raw", 21632, [P, S])
        latn = dz("latent_norm", 17536, [P, T, S])
        pos = dz("pos", 19584, [P, S], I32)
        ang, turns, rest = (dz(n, 20096 + 512 * j, [P, S]) for j, n in enumerate(("ang", "turns", "rest")))
        x_hat1 = [dz(f"x_hat1_{j}", 1024 * j, [P, D]) for j in range(2)]
        oH = at("o_high", ZB, [P, HEADS, S], F32R)
        oL = dz("o_low", 8192, [P, HEADS, S], F32R)
        soft = dz("soft", 22400, [P, 2, 8, 4])
        yc = dz("conv_out", 0, [P, K, S])
        cw = dz("conv_in", 4096, [P, 2 + S])
        cv = dz("conv_sum", 4704, [P, S])
        yH, yL = dz("y_high", 8192, [P, K, S], F32R), dz("y_low", 12288, [P, K, S], F32R)
        fH, fL = dz("ff_high", 0, [P, F_TILES, S], F32R), dz("ff_low", F_TILES * S, [P, F_TILES, S], F32R)
        kdup = dz("k_dup", 0, [P, KVH, S])
        vall = dz("v_all", 2048, [P, T, KVH * HD])
        swa = dz("swa", 3072, [P, P + 2 * P + 2 * S])
        turn_b, window = swa[:, 0:P], swa[:, P:3 * P]
        cosB, sinB = swa[:, 3 * P:3 * P + S], swa[:, 3 * P + S:3 * P + 2 * S]
        q2raw = dz("q2_raw", 4480, [P, 2, S])
        q2 = [dz(f"q2_{g}", 5504 + 1024 * g, [P, 2, S]) for g in range(2)]
        q2tmp = dz("q2_tmp", 7552, [P, 2, S])
        p2 = [dz(f"probs2_{u}", 8576 + 1024 * u, [P, GROUP, 2 * P]) for u in range(2)]
        p2T = [dz(f"probs2_t{u}", 10624 + 1024 * u, [P, 2 * GROUP, P]) for u in range(2)]
        o2H, o2L = dz("o2_high", 12672, [P, K, S], F32R), dz("o2_low", 16768, [P, K, S], F32R)

        PS = ctx.enter_context(nc.psum_tensor("PS", [P, 8, S], F32))

        def tile(ap, t):
            return ap[:, :, t * P:(t + 1) * P]

        def two(b):
            return PS[:, b:b + 2, :].rearrange("p a (c t) -> p (a c) t", t=P)

        def flat2(b):
            return PS[:, b:b + 2, :].rearrange("p a n -> p (a n)")

        w_full = [sem(f"w_full{s}") for s in range(2)]
        raw_free = [sem(f"raw_free{s}") for s in range(2)]
        w_high = [sem(f"w_high_ready{s}") for s in range(2)]
        w_split = [sem(f"w_split{s}") for s in range(2)]
        used = [sem(f"used{s}") for s in range(2)]
        pair_free = [sem(f"pair_free{s}") for s in range(2)]
        ada_full = [sem(f"ada_full{c}") for c in range(ADA_FIRST)]
        ada_land = [sem(f"ada_land{m}") for m in range(2)]
        ada_prod = [sem(f"ada_prod{m}") for m in range(2)]
        ada_sum = [sem(f"ada_sum{m}") for m in range(2)]
        ada_done, ada_col = sem("ada_done"), sem("ada_col")
        small_in, x_in, ws_in, aux_in, gains_in, late_in = (sem(n) for n in ("small_in", "x_in", "ws_in", "aux_in", "gains_in", "late_in"))
        act_step, dve_step, pool_step, pool_ready = sem("act_step"), sem("dve_step"), sem("pool_step"), sem("pool_ready")
        rows_tr, vec_ready, csil_ready, ws_tr, wT_ready = (sem(n) for n in ("rows_tr", "vec_ready", "csil_ready", "ws_tr", "wT_ready"))
        mod_ready, diag_ready, gate_mm, gate_ready = (sem(n) for n in ("mod_ready", "diag_ready", "gate_mm", "gate_ready"))
        tr_done, h_high, h_ready, xhat_ready = (sem(n) for n in ("tr_done", "h_high_ready", "h_ready", "xhat_ready"))
        lnv_stat, lnv_sqrt, vn_ready, sp_done, sv_ready = (sem(n) for n in ("lnv_stat", "lnv_sqrt", "vn_ready", "sp_done", "sv_ready"))
        sg_ready, prod_ready, act_high, gate_low = (sem(n) for n in ("sg_ready", "prod_ready", "act_high", "gate_low"))
        xb_ready, pooled_ready, pool_high, pool_low, py_done, yb_ready = (
            sem(n) for n in ("xb_ready", "pooled_ready", "pool_high_ready", "pool_low_ready", "py_done", "yb_ready"))
        y_ready, ln_stat, sqrt_ready, norm_ready, x_ready = (
            sem(n) for n in ("y_ready", "ln_stat", "sqrt_ready", "norm_ready", "x_ready"))
        rest_ready, sin_ready, lat_sqrt, latn_ready, lat_tr, lat_ev, kr_turn, kr_ready = (
            sem(n) for n in ("rest_ready", "sin_ready", "lat_sqrt", "latn_ready", "lat_tr", "lat_ev", "kr_turn", "kr_ready"))
        proj_done, qa_ready, kv_ready, q_turn, qr_ready = (sem(n) for n in ("proj_done", "qa_ready", "kv_ready", "q_turn", "qr_ready"))
        s_done, m_ready, e_ready, p_ready, t_done, pT_ready, pv_done, sz_ready, oz_ready = (
            sem(n) for n in ("s_done", "m_ready", "e_ready", "p_ready", "t_done", "pT_ready", "pv_done", "sz_ready", "oz_ready"))
        oh_ready, ol_ready, yc_ready = sem("oh_ready"), sem("ol_ready"), sem("yc_ready")
        k2_raw, k2_turn, k2_rot, kd_ready, v2_ready = (sem(n) for n in ("k2_raw", "k2_turn", "k2_rot", "kd_ready", "v2_ready"))
        q2_raw, q2_turn, q2_ready = (sem(n) for n in ("q2_raw_ready", "q2_turn", "q2_ready"))
        s2_done, m2_ready, e2_ready, p2_ready, t2_done, p2T_ready, pv2_done, o2_high, o2_low = (
            sem(n) for n in ("s2_done", "m2_ready", "e2_ready", "p2_ready", "t2_done", "p2T_ready", "pv2_done", "o2_high_ready", "o2_low_ready"))
        out_done = sem("out_done")

        PF, n = {}, CREDIT
        for name in ("xb", "zu", "zb", "cu", "b", "gu0", "gu1"):
            PF[name] = n
            n += BASE[name].pairs
        PF["end"] = n
        SG, n = {}, 0
        for name, c in (("zu", 8), ("zb", 8), ("cu", 8), ("gu0", F_TILES), ("gu1", F_TILES)):
            SG[name] = n
            n += c

        def end_use(name, s):
            return BASE[name].use[s] + BASE[name].pairs

        def wait_y(eng, b, name, t):
            if t < T - 1:
                eng.wait_ge(y_ready, (T - 1) * b + t + 1)
            else:
                eng.wait_ge(used[1], end_use(name, 1))

        BOUNDARY = ["eout", "oout", "aout", "dn0", "wo", "dn1"]
        TR = {"eout": 1, "oout": 2, "aout": 3, "dn0": 4, "q": 5, "wo": 6}

        block = ctx.enter_context(nc.Block())

        @block.sync
        def _(sp):
            w_in = {n: a[n].rearrange("(k p) n -> p k n", p=P) for n in (
                "e_w_in", "e_w_out", "o_w_in", "o_w_out", "a_w_in", "a_w_out", "w_kv", "b_w_q", "b_w_o")}
            ada_w = a["ada_w"].rearrange("l (k p) n -> l p k n", p=P)

            def load(name, i, s, pieces):
                B = BASE[name]
                assert len(pieces) == B.dmas[s]
                sp.wait_ge(raw_free[s], B.use[s] + i + CREDIT)
                for dst, src in pieces:
                    sp.dma_start(dst, src).then_inc(w_full[s], 16)

            def cols(s, w, c):
                v = raw[s][:, :].rearrange("p (k n) -> p k n", n=256)
                return [(v[:, j:j + K // 2, :], w[:, j:j + K // 2, bass.ds(c, 256)]) for j in (0, K // 2)]

            def twin(s, w, c, step):
                v = raw[s][:, :].rearrange("p (k two c) -> p k two c", two=2, c=P)
                return [(v[:, :, j, :], w[:, :, bass.ds(c + j * step, P)]) for j in range(2)]

            def deep(s, w, kt, n=2):
                c = n * D // 2
                return [(raw[s][:, j * c:(j + 1) * c], w[:, kt + j, :] if n == 2 else w[:, kt, j * c:(j + 1) * c]) for j in range(2)]

            def halves(s, w, kt, c):
                v = raw[s][:, :].rearrange("p (k n) -> p k n", n=S)
                return [(v[:, j:j + 2, :], w[:, kt + j:kt + j + 2, c:c + S]) for j in (0, 2)]

            for n, r, c in (("ada_b", "ada_b", 48), ("c", "c", 8), ("pool_b", "pool_b", 8), ("pool_scale", "pool_scale", 8),
                            ("q_g", "q_g", 2), ("kv_g", "kv_g", 1), ("conv", "conv", 24)):
                sp.dma_start(rows[ROWS[r]:ROWS[r] + c, :], a[n].rearrange("a (m p) -> (a m) p", p=P)).then_inc(small_in, 16)
            for n in ("ln_g", "ln_b"):
                sp.dma_start(rows[ROWS[n]:ROWS[n] + K, :], a[n][0:1, :].rearrange("a (m p) -> (a m) p", p=P)).then_inc(small_in, 16)
            sp.dma_start(small[:, :], a["k_small"]).then_inc(small_in, 16)
            for c in range(ADA_FIRST):
                if c == ADA_FIRST // 2:
                    sp.dma_start(ws_sb, a["gmlp_ws"].rearrange("h t s -> t h s")).then_inc(ws_in, 16)
                    sp.dma_start(x[:, :, :], a["x"].rearrange("(t p) d -> p t d", p=P)).then_inc(x_in, 16)
                sp.dma_start(ada_raw[c][:, :].rearrange("p (k n) -> p k n", n=256), ada_w[0][:, :, c * 256:(c + 1) * 256]).then_inc(ada_full[c], 16)
            for dst, src in ((g_bc, a["gmlp_norm_g"]), (b_bc, a["gmlp_norm_b"]), (bs_bc, a["gmlp_bs"])):
                sp.dma_start(dst, src.broadcast_to((P, src.shape[1]))).then_inc(aux_in, 16)
            sp.dma_start(sinks[:, :], a["b_sinks"].broadcast_to((P, 16))).then_inc(aux_in, 16)

            def ada_load(layer, pos, first):
                for m in range(2):
                    sp.wait_ge(ada_sum[m], pos + CREDIT)
                    sp.dma_start(ada_buf[m], ada_w[layer][:, :, bass.ds(pos * 256 + (first + m * P), P)]).then_inc(ada_land[m], 16)

            for c in range(4):
                load("v", c // 2, c % 2, halves(c % 2, w_in["e_w_in"], 4 * (c % 2), D + S * (c // 2)))
            sp.wait_ge(h_ready, T)
            with sp.Fori(0, 2) as i:
                for s in range(2):
                    load("xb", i, s, cols(s, w_in["e_w_in"], i * 512 + s * 256 + 3 * D))
                    ada_load(0, i * 2 + s, 2 * D)
            with sp.Fori(0, 4) as i:
                for s in range(2):
                    load("zu", i, s, twin(s, w_in["e_w_in"], i * 256 + s * P + 2 * D, -2 * D))
                    ada_load(1, i * 2 + (ADA_AT["zu"] + s), -ADA_AT["zu"] * 256)
            pool_w = a["pool_w"].rearrange("g (k p) e -> p (g k) e", p=P)
            for s in range(2):
                load("pool", 0, s, [(raw[s][:, j * 512:(j + 1) * 512].rearrange("p (k e) -> p k e", k=2),
                                     pool_w[:, 4 * s + 2 * j:4 * s + 2 * j + 2, :]) for j in range(2)])
            with sp.Fori(0, 2) as i:
                for s in range(2):
                    load("zb", i, s, cols(s, w_in["e_w_in"], i * 512 + s * 256 + 4 * D))
                    ada_load(1, i * 2 + (ADA_AT["zb"] + s), -ADA_AT["zu"] * 256)
            sp.wait_ge(sv_ready, K)
            for j, n in ((1, "ln_g"), (2, "ln_b")):
                sp.dma_start(gains[:, j, :], a[n][0:1, :].broadcast_to((P, D))).then_inc(gains_in, 16)
            with sp.Fori(0, 4) as i:
                for s in range(2):
                    load("eout", i, s, deep(s, w_in["e_w_out"], i * 4 + s * 2))
            for s in range(2):
                load("lat", 0, s, halves(s, w_in["o_w_in"], 4 * s, 0))
            sp.wait_ge(used[1], end_use("eout", 1))
            sp.dma_start(pos[:, :], a["positions"].broadcast_to((P, S))).then_inc(late_in, 16)
            sp.dma_start(turn_m[:, :], a["k_turn_m"]).then_inc(late_in, 16)
            uq = a["mla_w_uq"].rearrange("(k p) h e -> p k h e", p=P)
            with sp.Fori(0, 8) as i:
                load("mla", i, 0, cols(0, w_in["o_w_in"], i * 256 + LATENT))
                load("mla", i, 1, [
                    *((raw[1][:, k * 256:(k + 1) * 256].rearrange("p (h e) -> p h e", h=2), uq[:, k, bass.ds(i * 2, 2), 0:NOPE]) for k in range(2)),
                    *((raw[1][:, 512 + k * P:512 + (k + 1) * P].rearrange("p (h e) -> p h e", h=2), uq[:, k, bass.ds(i * 2, 2), NOPE:]) for k in range(2)),
                    (raw[1][:, 768:1024].rearrange("p (h e) -> p h e", h=2), a["mla_w_uk"][:, bass.ds(i * 2, 2), :]),
                    (raw[1][:, 1024:1280].rearrange("p (h e) -> p h e", h=2), a["mla_w_uv"][:, bass.ds(i * 2, 2), :]),
                ])
            sp.wait_ge(x_ready, T)
            sp.wait_ge(h_ready, 2 * T)
            for j, src in ((1, a["ln_g"][1:2, :]), (2, a["ln_b"][1:2, :]), (3, a["a_pre"])):
                sp.dma_start(gains[:, j, :], src.broadcast_to((P, D))).then_inc(gains_in, 16)
            with sp.Fori(0, 4) as i:
                for s in range(2):
                    load("oout", i, s, deep(s, w_in["o_w_out"], i * 4 + s * 2))
            with sp.Fori(0, 4) as i:
                for s in range(2):
                    load("cu", i, s, twin(s, w_in["a_w_in"], i * 256 + s * P + D, D))
            with sp.Fori(0, 2) as i:
                for s in range(2):
                    load("b", i, s, cols(s, w_in["a_w_in"], i * 512 + s * 256))
            sp.wait_ge(h_ready, 3 * T)
            for j, src in ((0, a["a_post"]), (1, a["f_pre"][0:1, :])):
                sp.dma_start(gains[:, j, :], src.broadcast_to((P, D))).then_inc(gains_in, 16)
            with sp.Fori(0, 2) as i:
                for s in range(2):
                    load("aout", i, s, deep(s, w_in["a_w_out"], i * 4 + s * 2))

            def ffn(layer):
                gu, dn = f"gu{layer}", f"dn{layer}"
                w_gu = a["f_gate_up"][layer].rearrange("(k p) n -> p k n", p=P)
                w_dn = a["f_down"][layer].rearrange("(k p) n -> p k n", p=P)
                with sp.Fori(0, 11) as i:
                    for s in range(2):
                        load(gu, i, s, twin(s, w_gu, i * 256 + s * P, D_FF))
                if layer == 0:
                    sp.wait_ge(h_ready, 4 * T)
                    new = ((0, a["f_post"][0:1, :]), (1, a["kv_norm"]), (2, a["b_pre"]))
                else:
                    sp.wait_ge(h_ready, 7 * T)
                    new = ((0, a["f_post"][1:2, :]),)
                for j, src in new:
                    sp.dma_start(gains[:, j, :], src.broadcast_to((P, D))).then_inc(gains_in, 16)
                for s in range(2):
                    load(dn, 0, s, deep(s, w_dn, s, 1))
                with sp.Fori(1, 6) as i:
                    for s in range(2):
                        load(dn, i, s, deep(s, w_dn, i * 4 + (s * 2 - 2)))

            ffn(0)
            for s in range(2):
                load("kv", 0, s, cols(s, w_in["w_kv"], (1 - s) * 256))
            sp.wait_ge(used[1], end_use("dn0", 1))
            sp.dma_start(swa[:, :], a["k_swa"]).then_inc(late_in, 16)
            with sp.Fori(0, 2) as i:
                for s in range(2):
                    load("q", i, s, cols(s, w_in["b_w_q"], i * 512 + s * 256))
            sp.wait_ge(h_ready, 6 * T)
            for j, src in ((0, a["b_post"]), (1, a["f_pre"][1:2, :])):
                sp.dma_start(gains[:, j, :], src.broadcast_to((P, D))).then_inc(gains_in, 16)
            with sp.Fori(0, 2) as i:
                for s in range(2):
                    load("wo", i, s, deep(s, w_in["b_w_o"], i * 4 + s * 2))
            ffn(1)
            out_v = out.rearrange("(t p) d -> p t d", p=P)
            for t in range(T):
                sp.wait_ge(x_ready, 5 * T + t + 1)
                sp.dma_start(out_v[:, t, :], x[:, t, :]).then_inc(out_done, 16)
            sp.wait_ge(out_done, 16 * T)

        @block.gpsimd
        def _(pool):
            nc.gpsimd.memset(eps[:, 0:1], LN_EPS)
            nc.gpsimd.memset(eps[:, 1:2], EPS2).then_inc(pool_ready, 1)
            for s in range(2):
                pool.sem_inc(raw_free[s], CREDIT)
                pool.sem_inc(pair_free[s], CREDIT)
            pool.sem_inc(gate_low, 2)
            pool.sem_inc(oz_ready, CREDIT)
            for m in range(2):
                pool.sem_inc(ada_sum[m], CREDIT)
            for name, pairs, kinds, _ in RING:
                B = BASE[name]
                if name == "pool":
                    pool.wait_ge(pool_high, 1)
                    nc.gpsimd.tensor_tensor(poolL[:, :, :], pooled[:, :, :], poolH[:, :, :].bitcast(F32), ALU.subtract).then_inc(pool_low, 1)
                if name == "mla":
                    pool.wait_ge(gains_in, 32)
                    for t in range(T):
                        pool.wait_ge(tr_done, T * TR["eout"] + t + 1)
                        nc.gpsimd.tensor_tensor(x[:, t, :], x[:, t, :], gains[:, 1, :], ALU.mult).then_inc(pool_step, 1)
                        pool.wait_ge(pool_step, t + 1)
                        nc.gpsimd.tensor_tensor(x[:, t, :], x[:, t, :], gains[:, 2, :], ALU.add).then_inc(x_ready, 1)
                with pool.Fori(0, pairs) as i:
                    for s in range(2):
                        if kinds[s] == "split":
                            pool.wait_ge(w_high[s], B.split[s] + i + 1)
                            nc.gpsimd.tensor_tensor(WL[s][:, :], raw[s][:, :], WH[s][:, :].bitcast(F32),
                                                    ALU.subtract).then_inc(w_split[s], 1)
                            pool.wait_ge(w_split[s], B.split[s] + i + 1)
                        else:
                            pool.wait_ge(used[s], B.use[s] + i + 1)
                        pool.sem_inc(raw_free[s], 1)

        @block.scalar
        def _(act):
            steps = Steps(act, act_step)
            nact = nc.scalar.activation

            def split_high(name, i, s):
                B = BASE[name]
                act.wait_ge(w_full[s], B.full[s] + (i + 1) * 32)
                if name != "v" or i:
                    act.wait_ge(used[s], B.use[s] + i)
                nact(WH[s][:, :], raw[s][:, :], ACT.Copy).then_inc(w_high[s], 1)

            act.wait_ge(vec_ready, 1)
            nact(csil[:, :], vec[:, ROWS["c"]:ROWS["c"] + K], ACT.Silu).then_inc(csil_ready, 1)

            def gate_rows(n, b):
                act.wait_ge(gate_mm, n)
                nact(gains[:, 0, :], flat2(b), ACT.Copy).then_inc(gate_ready, 1)

            def modulate(layer, q, t, tmp):
                act.wait_ge(tr_done, T * q + t + 1)
                if t >= 2:
                    act.wait_ge(h_ready, T * q + t - 1)
                for k in range(K):
                    c = 24 * layer + k
                    ins = nact(tmp[:, k * P:(k + 1) * P], two(2 * t)[:, k, :], ACT.Identity,
                               scale=mod[:, c + K:c + K + 1], bias=mod[:, c:c + 1])
                steps.link(ins)
                nact(tile(hH, t), tmp.rearrange("p (k t) -> p k t", t=P), ACT.Copy).then_inc(h_high, 1)

            for s in range(2):
                split_high("v", 0, s)
            act.wait_ge(mod_ready, 1)
            for t in range(T):
                modulate(0, 0, t, gains[:, 3 * (1 - t % 2), :])

            act.wait_ge(pool_ready, 1)
            for n in range(2):
                for s in range(2):
                    split_high("v", n + 1, s)
                act.wait_ge(lnv_stat, n + 1)
                nact(stat[:, :, 0:2].rearrange("p a b -> p a b"), mv[:, :, 1].rearrange("p (a b) -> p a b", b=2), ACT.Sqrt, bias=eps[:, 0:1]).then_inc(lnv_sqrt, 1)

            def gated(name, highs, fn):
                B = BASE[name]
                with act.Fori(0, B.pairs) as i:
                    for s in range(2):
                        f = i * 2 + s
                        act.wait_ge(used[s], B.use[s] + i + 1)
                        act.wait_ge(gate_low, GATED[name] + f + 1)
                        nact(buf[s][:, :], PS[:, 2 * s, :], fn).then_inc(sg_ready, 1)
                        split_high(name, i + 1, s)
                        act.wait_ge(prod_ready, GATED[name] + f + 1)
                        nact(highs[:, f, :], buf[s][:, :], ACT.Copy).then_inc(act_high, 1)

            for c in range(2 * BASE["xb"].pairs):
                split_high("xb", c // 2 + 1, c % 2)
                for m in range(2):
                    f = 2 * c + m
                    if f >= 2:
                        act.wait_ge(pooled_ready, f - 1)
                    nact(xbufs[m][:, PAD:], PS[:, 2 * (c % 2) + m, :], ACT.Copy).then_inc(xb_ready, 1)
            act.wait_ge(sp_done, K)
            act.wait_ge(pooled_ready, K)
            nact(poolH[:, :, :], pooled[:, :, :], ACT.Copy).then_inc(pool_high, 1)
            gated("zu", mixH, ACT.Silu)
            for s in range(2):
                split_high("pool", 1, s)
            B = BASE["zb"]
            with act.Fori(0, 2) as i:
                for s in range(2):
                    act.wait_ge(used[s], B.use[s] + i + 1)
                    for m in range(2):
                        f = i * 4 + (2 * s + m)
                        act.wait_ge(gate_low, GATED["zb"] + f + 1)
                        nact(buf[m][:, :], PS[:, 2 * s + m, :], ACT.Silu).then_inc(sg_ready, 1)
                    split_high("zb", i + 1, s)
                    for m in range(2):
                        f = i * 4 + (2 * s + m)
                        act.wait_ge(prod_ready, GATED["zb"] + f + 1)
                        nact(mixH[:, f + K, :], buf[m][:, :], ACT.Copy).then_inc(act_high, 1)
            act.wait_ge(ada_sum[0], ADA_END + CREDIT)
            gate_rows(1, 6)

            def highs_of(name):
                for c in range(2 * (BASE[name].pairs - 1)):
                    split_high(name, c // 2 + 1, c % 2)

            def root(t, c, scale, e):
                nact(stat[:, t, c + 1:c + 2], stat[:, t, c:c + 1], ACT.Sqrt, bias=eps[:, e:e + 1], scale=scale).then_inc(sqrt_ready, 1)

            def high_tile(q, t, b):
                act.wait_ge(tr_done, T * q + t + 1)
                nact(tile(hH, t), two(b), ACT.Copy).then_inc(h_high, 1)

            def square_x(n, t):
                act.wait_ge(x_ready, n)
                nblk = x[:, t, :].rearrange("p (k t) -> p k t", t=P)
                steps.link(nact(tile(hH, t), nblk, ACT.Square, accum_out=stat[:, t, 3:4]))
                root(t, 3, 1.0 / D, 1)

            def ln_root(b, t):
                act.wait_ge(ln_stat, T * b + t + 1)
                nact(stat[:, t, 1:2], mv[:, t, 1:2], ACT.Sqrt, bias=eps[:, 0:1]).then_inc(sqrt_ready, 1)

            highs_of("eout")
            tmps = [gains[:, 3, :], mod_tmp]
            ln_root(0, 0)
            ln_root(0, 1)
            split_high("lat", 0, 0)
            modulate(1, TR["eout"], 0, tmps[0])
            split_high("lat", 0, 1)
            ln_root(0, 2)
            modulate(1, TR["eout"], 1, tmps[1])
            ln_root(0, 3)
            modulate(1, TR["eout"], 2, tmps[0])
            modulate(1, TR["eout"], 3, tmps[1])

            act.wait_ge(rest_ready, 1)
            nact(sinM[:, :], rest[:, :], ACT.Sin)
            nact(cosM[:, :], turns[:, :], ACT.Sin).then_inc(sin_ready, 1)

            split_high("mla", 0, 0)
            act.wait_ge(used[1], end_use("lat", 1))
            for t in range(T):
                nact(latn[:, t, 0:QR], PS[:, t, 0:QR], ACT.Square, accum_out=stat[:, t, 0:1])
                steps.link(nact(latn[:, t, QR:QR + KVR], PS[:, t, QR:QR + KVR], ACT.Square, accum_out=stat[:, t, 1:2]))
            nact(stat[:, :, 2:3], stat[:, :, 0:1], ACT.Sqrt, bias=eps[:, 0:1], scale=1.0 / QR)
            nact(stat[:, :, 3:4], stat[:, :, 1:2], ACT.Sqrt, bias=eps[:, 0:1], scale=1.0 / KVR).then_inc(lat_sqrt, 1)
            gate_rows(2, 4)
            act.wait_ge(lat_tr, 1)
            for j in range(2):
                nact(qcT[:, j, :], PS[:, 4 + j, :], ACT.Copy, scale=vec[:, ROWS["q_g"] + j:ROWS["q_g"] + j + 1])
            nact(kvT[:, :], PS[:, 6, :], ACT.Copy, scale=vec[:, ROWS["kv_g"]:ROWS["kv_g"] + 1])
            nact(kraw[:, :], PS[:, 7, :], ACT.Copy).then_inc(lat_ev, 1)

            B = BASE["mla"]
            with act.Fori(0, 8) as i:
                act.wait_ge(proj_done, i * 4 + 1)
                nact(qraw[:, :], PS[:, 2, :], ACT.Copy).then_inc(qa_ready, 1)
                act.wait_ge(proj_done, i * 4 + 3)
                nact(qn[:, :, :], PS[:, 0:2, :], ACT.Copy).then_inc(qa_ready, 1)

                def weigh(u):
                    w = (u % T + 1) * P
                    act.wait_ge(m_ready, i * 8 + u + 1)
                    nact(pm[u % 2][:, 0:w], PS[:, 2 + u % 2, 0:w], ACT.Exp, scale=MLA_SCALE, bias=soft[:, u % 2, 1, 0:1],
                         accum_out=soft[:, u % 2, 2, 0:1]).then_inc(e_ready, 1)

                def turned(u):
                    q = u % T
                    act.wait_ge(t_done, i * 8 + u + 1)
                    nact(pT[u // T][:, 0:q + 1, q * P:(q + 1) * P],
                         PS[:, 4 + u % 2, 0:(q + 1) * P].rearrange("p (k t) -> p k t", t=P), ACT.Copy).then_inc(pT_ready, 1)

                weigh(0)
                weigh(1)
                for u in range(8):
                    turned(u)
                    if u + 2 < 8:
                        weigh(u + 2)
                act.wait_ge(used[0], B.use[0] + i + 1)
                nact(sz[:, :, :], PS[:, 0:2, :], ACT.Silu).then_inc(sz_ready, 1)
                split_high("mla", i + 1, 0)

            split_high("oout", 0, 1)
            act.wait_ge(oz_ready, HEADS + CREDIT)
            for h in range(HEADS):
                nact(oH[:, h, :], oz[:, h, :], ACT.Copy).then_inc(oh_ready, 1)
            highs_of("oout")
            q = TR["oout"]
            ln_root(1, 0)
            ln_root(1, 1)
            square_x(T + 1, 0)
            square_x(T + 2, 1)
            split_high("cu", 0, 0)
            ln_root(1, 2)
            high_tile(q, 0, 0)
            high_tile(q, 1, 2)
            ln_root(1, 3)
            split_high("cu", 0, 1)
            square_x(T + 3, 2)
            square_x(T + 4, 3)
            high_tile(q, 2, 4)
            high_tile(q, 3, 6)

            B = BASE["cu"]
            with act.Fori(0, 4) as i:
                for s in range(2):
                    split_high("cu", i + 1, s)
                    act.wait_ge(pair_free[s], i + PF["cu"])
                    nact(buf[s][:, :], PS[:, 2 * s, :], ACT.Copy).then_inc(sg_ready, 1)
            with act.Fori(0, 2) as i:
                for s in range(2):
                    split_high("b", i + 1, s)
                    for m in range(2):
                        f = i * 4 + (2 * s + m)
                        act.wait_ge(prod_ready, GATED["b"] + f + 1)
                        nact(yH[:, f, :], buf[m][:, :], ACT.Copy).then_inc(act_high, 1)

            def boundary(name, pre):
                b, pairs = BOUNDARY.index(name), BASE[name].pairs

                def square_y(t):
                    wait_y(act, b, name, t)
                    steps.link(nact(tile(hH, t), two(2 * t), ACT.Square, accum_out=stat[:, t, 0:1]))
                    root(t, 0, 1.0 / D, 1)

                highs_of(name)
                if not pre:
                    for t in range(T):
                        square_y(t)
                    return
                q = TR[name]
                square_y(0)
                square_y(1)
                square_x(T * b + 1, 0)
                split_high(name, pairs, 0)
                square_x(T * b + 2, 1)
                square_y(2)
                high_tile(q, 0, 0)
                square_y(3)
                high_tile(q, 1, 2)
                split_high(name, pairs, 1)
                square_x(T * b + 3, 2)
                square_x(T * b + 4, 3)
                high_tile(q, 2, 4)
                high_tile(q, 3, 6)

            boundary("aout", True)
            gated("gu0", fH, ACT.Silu)
            boundary("dn0", True)

            split_high("kv", 1, 0)
            act.wait_ge(used[1], end_use("kv", 1))
            high_tile(TR["q"], 0, 4)
            nact(q2raw[:, :, :], PS[:, 2:4, :], ACT.Copy).then_inc(k2_raw, 1)
            high_tile(TR["q"], 1, 6)
            split_high("kv", 1, 1)
            for t in (2, 3):
                high_tile(TR["q"], t, 2 * t)
            act.wait_ge(k2_rot, 1)
            for g in range(KVH):
                src = q2[1][(g % 2) * HD:(g % 2 + 1) * HD, g // 2, :]
                for j in range(2):
                    ins = nact(kdup[j * HD:(j + 1) * HD, g, :], src, ACT.Copy)
            ins.then_inc(kd_ready, 1)

            def raw_queries(g):
                act.wait_ge(used[g % 2], BASE["q"].use[g % 2] + g // 2 + 1)
                act.wait_ge(q2_ready, g) if g else act.wait_ge(k2_rot, 1)
                nact(q2raw[:, :, :], PS[:, 0:2, :], ACT.Copy).then_inc(q2_raw, 1)
                split_high("q", g // 2 + 1, g % 2)

            def weigh2(n):
                w = 0 if n % T else P
                st, pr = soft[:, n % 2, :, :], p2[n % 2]
                act.wait_ge(m2_ready, n + 1)
                nact(st[:, 4, :], st[:, 3, :], ACT.Exp)
                for h in range(GROUP):
                    ins = nact(pr[:, h, w:], pr[:, h, w:], ACT.Exp, scale=SW_SCALE, bias=st[:, 2, h:h + 1], accum_out=st[:, 5, h:h + 1])
                ins.then_inc(e2_ready, 1)

            def turned2(n):
                act.wait_ge(t2_done, n + 1)
                if n >= 2:
                    act.wait_ge(pv2_done, n - 1)
                j, st = (0, 1) if n % T else (1, 2)
                nact(p2T[n % 2][:, j::st, :], two(4)[:, j::st, :], ACT.Copy).then_inc(p2T_ready, 1)

            def high_out(g):
                act.wait_ge(pv2_done, T * (g + 1))
                for j in range(2):
                    nact(o2H[:, g * 2 + j, :], PS[:, 6 + j, :], ACT.Copy).then_inc(o2_high, 1)

            raw_queries(0)
            weigh2(0)
            for n in range(UNITS):
                if n % T == 1 and n // T + 1 < KVH:
                    raw_queries(n // T + 1)
                if n + 1 < UNITS:
                    weigh2(n + 1)
                if n % T == 0 and n:
                    high_out(n // T - 1)
                turned2(n)
            high_out(KVH - 1)
            boundary("wo", True)
            gated("gu1", fH, ACT.Silu)
            boundary("dn1", False)

        @block.vector
        def _(dve):
            steps = Steps(dve, dve_step)
            v = nc.vector

            dve.wait_ge(rows_tr, 1)
            steps.link(v.tensor_copy(vec[:, :], PS[:, 7, 0:N_ROWS]))
            for layer in range(DEPTH):
                c = slice(24 * layer + K, 24 * layer + 24)
                ins = v.tensor_scalar(vec[:, c], vec[:, c], 1.0, None, ALU.add)
            ins.then_inc(vec_ready, 1)
            dve.wait_ge(ws_tr, 1)
            steps.link(v.tensor_copy(wT, PS[:, 6, :].rearrange("p (h t) -> p h t", t=P)))
            v.memset(wT[G_HALF:P, :, 0:G_HALF], 0.0).then_inc(wT_ready, 1)
            dve.wait_ge(vec_ready, 1)
            dve.wait_ge(ada_done, 1)
            v.tensor_tensor(mod[:, 0:2 * K], PS[:, 7, 256:256 + 2 * K], vec[:, 0:2 * K], ALU.add).then_inc(mod_ready, 1)

            def ada_terms(pos):
                for m in range(2):
                    dve.wait_ge(ada_land[m], pos * 16 + 16)
                    v.tensor_tensor(ada_buf[m], ada_buf[m], csil[:, :].unsqueeze(2).broadcast_to((P, K, P)), ALU.mult).then_inc(ada_prod[m], 1)
                for m in range(2):
                    dve.wait_ge(ada_prod[m], pos + 1)
                    v.reduce_sum(ada_acc[m][:, :], ada_buf[m].rearrange("p k n -> p n k"), AX).then_inc(ada_sum[m], 1)

            def ada_keep(pos, s):
                c = pos * 2 + 2 * K
                v.tensor_tensor(mod[:, bass.ds(c, 2)], PS[:, 4, 2 * s:2 * s + 2], vec[:, bass.ds(c, 2)], ALU.add).then_inc(ada_col, 1)

            def gate_diag(layer, one, dg):
                v.memset(one[:, :], 1.0)
                for k in range(K):
                    c = 24 * layer + 2 * K + k
                    ins = v.tensor_scalar(dg[:, k, :], ident, mod[:, c:c + 1], None, ALU.mult)
                ins.then_inc(diag_ready, 1)

            def low_mod(q, t, tmp):
                dve.wait_ge(h_high, T * q + t + 1)
                v.tensor_tensor(tile(hL, t), tmp.rearrange("p (k t) -> p k t", t=P), tile(hH, t).bitcast(F32),
                                ALU.subtract).then_inc(h_ready, 1)

            for t in range(T):
                low_mod(0, t, gains[:, 3 * (1 - t % 2), :])

            dve.wait_ge(aux_in, 16 * 4)
            dve.wait_ge(csil_ready, 1)
            for n in range(2):
                dve.wait_ge(used[1], BASE["v"].use[1] + n + 1)
                for t in range(T):
                    for h in range(2):
                        ins = v.bn_stats(bn[:, 2 * t + h, :], PS[:, 4 * n + t, h * G_DIM:(h + 1) * G_DIM])
                steps.link(ins)
                for j in range(8):
                    ins = v.bn_aggr(mv[:, j, :], bn[:, j, :])
                ins.then_inc(lnv_stat, 1)
                dve.wait_ge(lnv_sqrt, n + 1)
                steps.link(v.reciprocal(stat[:, :, 2:4], stat[:, :, 0:2]))
                for t in range(T):
                    for h in range(2):
                        c = n * S + h * G_DIM
                        ins = v.tensor_scalar(vn[:, t, c:c + G_DIM], PS[:, 4 * n + t, h * G_DIM:(h + 1) * G_DIM],
                                              mv[:, 2 * t + h, 0:1], stat[:, t, 2 + h:3 + h], ALU.subtract, ALU.mult)
                steps.link(ins)
                for h in range(2):
                    c = n * S + h * G_DIM
                    blk = vn[:, :, c:c + G_DIM]
                    steps.link(v.tensor_tensor(blk, blk, g_bc.unsqueeze(1).broadcast_to((P, T, G_DIM)), ALU.mult))
                    ins = v.tensor_tensor(blk, blk, b_bc.unsqueeze(1).broadcast_to((P, T, G_DIM)), ALU.add)
                ins.then_inc(vn_ready, 1)
            def spatial_bias():
                for f in range(K):
                    dve.wait_ge(sp_done, f + 1)
                    h = f // 2
                    v.tensor_tensor(sv[:, f, :].rearrange("p (b t) -> p b t", t=P), PS[:, 4 + f % 4, :].rearrange("p (b t) -> p b t", t=P),
                                    bs_bc[:, h * P:(h + 1) * P].unsqueeze(1).broadcast_to((P, T, P)), ALU.add).then_inc(sv_ready, 1)

            for z in (*xbufs, sum_a, sum_b):
                ins = v.memset(z[:, 0:PAD], 0.0)
            steps.link(ins)
            ada_terms(0)
            for c in range(2 * BASE["xb"].pairs):
                dve.wait_ge(used[c % 2], BASE["xb"].use[c % 2] + c // 2 + 1)
                ada_keep(c, c % 2)
                ada_terms(c + 1)
                if c == 2 * BASE["xb"].pairs - 1:
                    spatial_bias()
                for f in (2 * c, 2 * c + 1):
                    g = f // 2
                    win = POOL_WINDOWS[g]
                    dve.wait_ge(xb_ready, f + 1)
                    if f % 2:
                        dve.sem_inc(pair_free[g % 2], 1)
                    xbuf = xbufs[f % 2]
                    cur, step, nxt = xbuf, 1, [sum_a, sum_b]
                    while step < win:
                        dst = nxt[0]
                        nxt.reverse()
                        steps.link(v.tensor_tensor(dst[:, PAD:], cur[:, PAD:], cur[:, PAD - step:PAD + S - step], ALU.add))
                        cur, step = dst, 2 * step
                    steps.link(v.scalar_tensor_tensor(pooled[:, f, :], cur[:, PAD:], 1.0 / win, xbuf[:, PAD:], ALU.mult, ALU.subtract))
                    head = pooled[:, f, 0:PAD]
                    steps.link(v.tensor_tensor(head, cur[:, PAD:2 * PAD], inv_count[:, g * PAD:(g + 1) * PAD], ALU.mult))
                    v.tensor_tensor(head, head, xbuf[:, PAD:2 * PAD], ALU.subtract).then_inc(pooled_ready, 1)
            dve.wait_ge(pooled_ready, K)
            dve.wait_ge(sv_ready, K)

            def gated(name, lows, factor=None):
                B = BASE[name]
                with dve.Fori(0, B.pairs) as i:
                    for s in range(2):
                        f = i * 2 + s
                        if name in ADA_AT:
                            dve.wait_ge(used[s], B.use[s] + i + 1)
                            ada_keep(f + ADA_AT[name], s)
                            ada_terms(f + (ADA_AT[name] + 1))
                        dve.wait_ge(sg_ready, SG[name] + f + 1)
                        if factor is None:
                            v.tensor_tensor(buf[s][:, :], buf[s][:, :], PS[:, 2 * s + 1, :], ALU.mult).then_inc(prod_ready, 1)
                            dve.wait_ge(prod_ready, GATED[name] + f + 1)
                            dve.sem_inc(pair_free[s], 1)
                        else:
                            v.tensor_tensor(buf[s][:, :], buf[s][:, :], PS[:, 2 * s + 1, :], ALU.mult).then_inc(pair_free[s], 1)
                            dve.wait_ge(pair_free[s], PF[name] + i + 1)
                            v.tensor_tensor(buf[s][:, :], buf[s][:, :], factor[:, f, :], ALU.mult).then_inc(prod_ready, 1)
                            dve.wait_ge(prod_ready, GATED[name] + f + 1)
                        dve.wait_ge(act_high, GATED[name] + f + 1)
                        v.tensor_tensor(lows[:, f, :], buf[s][:, :], highs_of[name][:, f, :].bitcast(F32), ALU.subtract).then_inc(gate_low, 1)

            highs_of = {"zu": mixH, "gu0": fH, "gu1": fH}
            gated("zu", mixL, sv)

            for f in range(K):
                if f % 4 < 3:
                    dve.wait_ge(py_done, 3 * (f // 4) + f % 4 + 1)
                else:
                    dve.wait_ge(used[f // 4], BASE["pool"].use[f // 4] + 1)
                v.tensor_scalar(sv[:, f, :], PS[:, 4 + f % 4, :], vec[:, ROWS["pool_b"] + f:ROWS["pool_b"] + f + 1],
                                vec[:, ROWS["pool_scale"] + f:ROWS["pool_scale"] + f + 1], ALU.add, ALU.mult).then_inc(yb_ready, 1)
            dve.wait_ge(yb_ready, K)
            gate_diag(0, ones, diag)
            B = BASE["zb"]
            for c in range(2 * B.pairs):
                s = c % 2
                dve.wait_ge(used[s], B.use[s] + c // 2 + 1)
                ada_keep(ADA_AT["zb"] + c, s)
                if c + 1 < 2 * B.pairs:
                    ada_terms(ADA_AT["zb"] + c + 1)
                for m in range(2):
                    f = 2 * c + m
                    dve.wait_ge(sg_ready, SG["zb"] + f + 1)
                    if m:
                        dve.sem_inc(pair_free[s], 1)
                    v.tensor_tensor(buf[m][:, :], buf[m][:, :], sv[:, f, :], ALU.mult).then_inc(prod_ready, 1)
                for m in range(2):
                    f = 2 * c + m
                    dve.wait_ge(act_high, GATED["zb"] + f + 1)
                    v.tensor_tensor(mixL[:, f + K, :], buf[m][:, :], mixH[:, f + K, :].bitcast(F32), ALU.subtract).then_inc(gate_low, 1)

            tmps = [gains[:, 3, :], mod_tmp]
            dve.wait_ge(ada_col, ADA_END)
            g_col, b_col = (vec[:, ROWS[n]:ROWS[n] + K] for n in ("ln_g", "ln_b"))
            steps.link(v.tensor_tensor(b_col, b_col, mod[:, 24 + K:24 + 2 * K], ALU.mult))
            steps.link(v.tensor_tensor(mod[:, 24:24 + K], mod[:, 24:24 + K], b_col, ALU.add))
            steps.link(v.tensor_tensor(mod[:, 24 + K:24 + 2 * K], mod[:, 24 + K:24 + 2 * K], g_col, ALU.mult))

            def ln_gated(b, name, t):
                wait_y(dve, b, name, t)
                if t == 0:
                    dve.wait_ge(gate_ready, b + 1)
                    if b:
                        dve.wait_ge(x_ready, T)
                steps.link(v.tensor_tensor(hf[:, :], flat2(2 * t), gains[:, 0, :], ALU.mult))

            def ln_stats(t):
                xt = x[:, t, :]
                steps.link(v.scalar_tensor_tensor(xt, xt, ALPHA, hf[:, :], ALU.mult, ALU.add))
                for j in range(2):
                    ins = v.bn_stats(bn[:, j, :], x[:, t, j * S:(j + 1) * S])
                steps.link(ins)
                v.bn_aggr(mv[:, t, :], bn[:, 0:2, :]).then_inc(ln_stat, 1)

            def ln_factor(n, t):
                dve.wait_ge(sqrt_ready, n)
                steps.link(v.reciprocal(stat[:, t, 2:3], stat[:, t, 1:2]))

            def ln_normal(n, t):
                ln_factor(n, t)
                v.tensor_scalar(x[:, t, :], x[:, t, :], mv[:, t, 0:1], stat[:, t, 2:3], ALU.subtract, ALU.mult).then_inc(norm_ready, 1)

            def ln_affine(n, t):
                dve.wait_ge(gains_in, 80)
                dve.wait_ge(ln_stat, T + t + 1)
                steps.link(v.scalar_tensor_tensor(x[:, t, :], x[:, t, :], mv[:, t, 0:1], gains[:, 1, :], ALU.subtract, ALU.mult))
                ln_factor(n, t)
                v.scalar_tensor_tensor(x[:, t, :], x[:, t, :], stat[:, t, 2:3], gains[:, 2, :], ALU.mult, ALU.add).then_inc(x_ready, 1)

            def low_tile(q, t, b):
                dve.wait_ge(h_high, T * q + t + 1)
                v.tensor_tensor(tile(hL, t), two(b), tile(hH, t).bitcast(F32), ALU.subtract).then_inc(h_ready, 1)

            def prenorm(n, t, g, q, hats):
                dve.wait_ge(sqrt_ready, n)
                if t >= 2:
                    dve.wait_ge(tr_done, T * q + t - 1)
                steps.link(v.reciprocal(stat[:, t, 5:6], stat[:, t, 4:5]))
                v.scalar_tensor_tensor(hats[t % 2][:, :], x[:, t, :], stat[:, t, 5:6], gains[:, g, :], ALU.mult, ALU.mult).then_inc(xhat_ready, 1)

            q = TR["eout"]
            ln_gated(0, "eout", 0)
            ln_stats(0)
            ln_gated(0, "eout", 1)
            ln_normal(1, 0)
            ln_stats(1)
            ln_gated(0, "eout", 2)
            ln_normal(2, 1)
            low_mod(q, 0, tmps[0])
            ln_stats(2)
            ln_gated(0, "eout", 3)
            ln_normal(3, 2)
            low_mod(q, 1, tmps[1])
            ln_stats(3)
            ln_normal(4, 3)
            for t in (2, 3):
                low_mod(q, t, tmps[t % 2])

            dve.wait_ge(late_in, 32)
            steps.link(v.tensor_copy(ang[:, :], pos[:, :]))
            steps.link(v.tensor_scalar(ang[:, :], ang[:, :], freq, None, ALU.mult))
            steps.link(v.tensor_scalar(turns[:, :], ang[:, :], 1.0 / TWO_PI, ROUND, ALU.mult, ALU.add))
            steps.link(v.tensor_scalar(turns[:, :], turns[:, :], ROUND, None, ALU.subtract))
            steps.link(v.scalar_tensor_tensor(rest[:, :], turns[:, :], -PI_1, ang[:, :], ALU.mult, ALU.add))
            steps.link(v.scalar_tensor_tensor(rest[:, :], turns[:, :], -PI_2, rest[:, :], ALU.mult, ALU.add))
            steps.link(v.scalar_tensor_tensor(rest[:, :], turns[:, :], -PI_3, rest[:, :], ALU.mult, ALU.add))
            steps.link(v.tensor_scalar(rest[:, :], rest[:, :], 3.1415925, -3.1415925, ALU.min, ALU.max))
            steps.link(v.scalar_tensor_tensor(turns[:, :], rest[:, :], -1.0, rest[:, :], ALU.mult, ALU.max))
            v.tensor_scalar(turns[:, :], turns[:, :], -1.0, np.pi / 2, ALU.mult, ALU.add).then_inc(rest_ready, 1)
            gate_diag(1, ones1, diag1)

            dve.wait_ge(lat_sqrt, 1)
            steps.link(v.reciprocal(stat[:, :, 4:6], stat[:, :, 2:4]))
            for t in range(T):
                v.tensor_scalar(latn[:, t, 0:QR], PS[:, t, 0:QR], stat[:, t, 4:5], None, ALU.mult)
                v.tensor_scalar(latn[:, t, QR:QR + KVR], PS[:, t, QR:QR + KVR], stat[:, t, 5:6], None, ALU.mult)
                for j in range(2):
                    c = QR + KVR + ROPE * j
                    ins = v.tensor_copy(latn[:, t, c:c + ROPE], PS[:, t, QR + KVR:LATENT])
            ins.then_inc(latn_ready, 1)
            dve.wait_ge(kr_turn, 1)
            dve.wait_ge(sin_ready, 1)
            v.tensor_tensor(kr[:, :], kraw[:, :], cosM[:, :], ALU.mult)
            steps.link(v.tensor_tensor(qr[:, :], PS[:, 0, :], sinM[:, :], ALU.mult))
            v.tensor_tensor(kr[:, :], kr[:, :], qr[:, :], ALU.add).then_inc(kr_ready, 1)

            with dve.Fori(0, 8) as i:
                PER = 3 + 8 * 4
                steps.loop(i, PER)
                dve.wait_ge(proj_done, i * 4 + 2)
                v.tensor_copy(kn[:, :, :], PS[:, 4:6, :])
                dve.wait_ge(qa_ready, i * 2 + 1)
                steps.link(v.tensor_tensor(qr[:, :], qraw[:, :], cosM[:, :], ALU.mult))
                dve.wait_ge(q_turn, i + 1)
                steps.link(v.tensor_tensor(qraw[:, :], PS[:, 3, :], sinM[:, :], ALU.mult))
                v.tensor_tensor(qr[:, :], qr[:, :], qraw[:, :], ALU.add).then_inc(qr_ready, 1)
                dve.wait_ge(proj_done, i * 4 + 4)
                v.tensor_copy(vh[:, :, :], PS[:, 6:8, :].rearrange("p a (b n) -> p (a b) n", b=2)).then_inc(kv_ready, 1)

                def top(u):
                    q = u % T
                    w = (q + 1) * P
                    sc = PS[:, 2 + u % 2, 0:w]
                    dve.wait_ge(s_done, i * 8 + u + 1)
                    steps.link(v.memset(PS[0:64, 2 + u % 2, q * P + 64:w], MASKED))
                    steps.link(v.reduce_max(soft[:, u % 2, 0, 0:1], sc, AX))
                    v.tensor_scalar(soft[:, u % 2, 1, 0:1], soft[:, u % 2, 0, 0:1], -MLA_SCALE, None, ALU.mult).then_inc(m_ready, 1)

                def norm(u):
                    w = (u % T + 1) * P
                    dve.wait_ge(e_ready, i * 8 + u + 1)
                    steps.link(v.reciprocal(soft[:, u % 2, 3, 0:1], soft[:, u % 2, 2, 0:1]))
                    v.tensor_scalar(pm[u % 2][:, 0:w], pm[u % 2][:, 0:w], soft[:, u % 2, 3, 0:1], None, ALU.mult).then_inc(p_ready, 1)

                top(0)
                top(1)
                for u in range(8):
                    norm(u)
                    if u + 2 < 8:
                        top(u + 2)
                dve.wait_ge(sz_ready, i + 1)
                for h in range(2):
                    dve.wait_ge(pv_done, i * 2 + h + 1)
                    v.tensor_tensor(oz[:, i * 2 + h, :], PS[:, 6 + h, :], sz[:, h, :], ALU.mult).then_inc(oz_ready, 1)
                steps.link(v.tensor_copy(stat[:, 0, 7:8], soft[:, 1, 3, 0:1]))
                for _ in range(PER - (steps.n - steps.first)):
                    steps.link(v.tensor_copy(stat[:, 0, 7:8], soft[:, 1, 3, 0:1]))
            steps.done(8)

            dve.wait_ge(oz_ready, HEADS + CREDIT)
            for h in range(HEADS):
                dve.wait_ge(oh_ready, h + 1)
                v.tensor_tensor(oL[:, h, :], oz[:, h, :], oH[:, h, :].bitcast(F32), ALU.subtract).then_inc(ol_ready, 1)

            n, q = T, TR["oout"]
            ln_gated(1, "oout", 0)
            ln_stats(0)
            ln_gated(1, "oout", 1)
            ln_affine(n + 1, 0)
            ln_stats(1)
            ln_affine(n + 2, 1)
            prenorm(n + 3, 0, 3, q, x_hat1)
            prenorm(n + 4, 1, 3, q, x_hat1)
            ln_gated(1, "oout", 2)
            ln_stats(2)
            low_tile(q, 0, 0)
            low_tile(q, 1, 2)
            ln_affine(n + 5, 2)
            ln_gated(1, "oout", 3)
            ln_stats(3)
            ln_affine(n + 6, 3)
            prenorm(n + 7, 2, 3, q, x_hat1)
            prenorm(n + 8, 3, 3, q, x_hat1)
            low_tile(q, 2, 4)
            low_tile(q, 3, 6)
            n += 2 * T

            steps.link(v.memset(cw[:, 0:2], 0.0))
            with dve.Fori(0, 4) as i:
                steps.loop(i, 2 * 3)
                for s in range(2):
                    f = i * 2 + s

                    def tap(j):
                        return vec[:, bass.ds(f + (ROWS["conv"] + K * j), 1)]

                    dve.wait_ge(sg_ready, SG["cu"] + f + 1)
                    v.tensor_tensor(cw[:, 2:], buf[s][:, :], PS[:, 2 * s + 1, :], ALU.mult).then_inc(pair_free[s], 1)
                    dve.wait_ge(pair_free[s], PF["cu"] + i + 1)
                    steps.link(v.tensor_scalar(cv[:, :], cw[:, 0:S], tap(0), None, ALU.mult))
                    steps.link(v.scalar_tensor_tensor(cv[:, :], cw[:, 1:1 + S], tap(1), cv[:, :], ALU.mult, ALU.add))
                    steps.link(v.scalar_tensor_tensor(yc[:, f, :], cw[:, 2:], tap(2), cv[:, :], ALU.mult, ALU.add))
            steps.done(4)
            B = BASE["b"]
            with dve.Fori(0, 2) as i:
                for s in range(2):
                    dve.wait_ge(used[s], B.use[s] + i + 1)
                    for m in range(2):
                        f = i * 4 + (2 * s + m)
                        dve.wait_ge(gate_low, GATED["b"] + f + 1)
                        v.tensor_tensor(buf[m][:, :], PS[:, 2 * s + m, :], yc[:, f, :], ALU.mult).then_inc(prod_ready, 1)
                    for m in range(2):
                        f = i * 4 + (2 * s + m)
                        dve.wait_ge(act_high, GATED["b"] + f + 1)
                        v.tensor_tensor(yL[:, f, :], buf[m][:, :], yH[:, f, :].bitcast(F32), ALU.subtract).then_inc(gate_low, 1)
                    dve.sem_inc(pair_free[s], 1)

            def boundary(name, n, pre, loaded):
                b = BOUNDARY.index(name)
                dve.wait_ge(gains_in, loaded)

                def residual(n, t):
                    dve.wait_ge(sqrt_ready, n)
                    blocks = x[:, t, :].rearrange("p (k t) -> p k t", t=P)
                    tmp = tile(scaled, t)
                    steps.link(v.reciprocal(stat[:, t, 2:3], stat[:, t, 1:2]))
                    steps.link(v.scalar_tensor_tensor(tmp, two(2 * t), stat[:, t, 2:3], gains[:, 0, :].rearrange("p (k t) -> p k t", t=P),
                                                      ALU.mult, ALU.mult))
                    v.tensor_tensor(blocks, blocks, tmp, ALU.add).then_inc(x_ready, 1)

                if not pre:
                    for t in range(T):
                        residual(n + t + 1, t)
                    return n + T
                q = TR[name]
                residual(n + 1, 0)
                residual(n + 2, 1)
                prenorm(n + 3, 0, 1, q, x_hat)
                prenorm(n + 4, 1, 1, q, x_hat)
                residual(n + 5, 2)
                low_tile(q, 0, 0)
                low_tile(q, 1, 2)
                residual(n + 6, 3)
                prenorm(n + 7, 2, 1, q, x_hat)
                prenorm(n + 8, 3, 1, q, x_hat)
                low_tile(q, 2, 4)
                low_tile(q, 3, 6)
                return n + 2 * T

            n = boundary("aout", n, True, 112)
            gated("gu0", fL)
            n = boundary("dn0", n, True, 160)

            q = TR["q"]

            def query_norm(t):
                if t >= 2:
                    dve.wait_ge(tr_done, T * q + t - 1)
                v.scalar_tensor_tensor(x_hat[t % 2][:, :], x[:, t, :], stat[:, t, 5:6], gains[:, 2, :], ALU.mult, ALU.mult).then_inc(xhat_ready, 1)

            query_norm(0)
            query_norm(1)
            dve.wait_ge(used[0], end_use("kv", 0))
            v.tensor_copy(vall[:, :, :], PS[:, 0:2, :].rearrange("p a (b n) -> p (a b) n", b=2)).then_inc(v2_ready, 1)
            query_norm(2)
            query_norm(3)
            cos2 = cosB.unsqueeze(1).broadcast_to((P, 2, S))
            sin2 = sinB.unsqueeze(1).broadcast_to((P, 2, S))

            def rotate(dst, bank, raw_ready, turned, n):
                dve.wait_ge(raw_ready, n)
                v.tensor_tensor(dst[:, :, :], q2raw[:, :, :], cos2, ALU.mult)
                dve.wait_ge(turned, n)
                steps.link(v.tensor_tensor(q2tmp[:, :, :], PS[:, bank:bank + 2, :], sin2, ALU.mult))
                return v.tensor_tensor(dst[:, :, :], dst[:, :, :], q2tmp[:, :, :], ALU.add)

            dve.wait_ge(late_in, 48)
            low_tile(q, 0, 4)
            low_tile(q, 1, 6)
            rotate(q2[1], 2, k2_raw, k2_turn, 1).then_inc(k2_rot, 1)
            low_tile(q, 2, 4)
            low_tile(q, 3, 6)

            def top2(n):
                g, w = n // T, 0 if n % T else P
                st = soft[:, n % 2, :, :]

                def pairs(c):
                    return st[:, c, :].rearrange("p (o j) -> p o j", o=2)

                sink = sinks[:, g * GROUP:(g + 1) * GROUP].rearrange("p (j o) -> p o j", o=2)
                sc = p2[n % 2][:, :, w:]
                dve.wait_ge(s2_done, n + 1)
                if n >= 2:
                    dve.wait_ge(t2_done, n - 1)
                steps.link(v.tensor_tensor(sc, two(2).rearrange("p (h k) t -> p h (k t)", h=GROUP)[:, :, w:],
                                           window[:, w:].unsqueeze(1).broadcast_to((P, GROUP, 2 * P - w)), ALU.add))
                steps.link(v.reduce_max(st[:, 0, :], sc, AX))
                steps.link(v.scalar_tensor_tensor(pairs(1), pairs(0), SW_SCALE, sink, ALU.mult, ALU.max))
                v.tensor_tensor(pairs(3), sink, pairs(1), ALU.subtract)
                v.tensor_scalar(st[:, 2, :], st[:, 1, :], -1.0, None, ALU.mult).then_inc(m2_ready, 1)

            def norm2(n):
                w = 0 if n % T else P
                st = soft[:, n % 2, :, :]
                dve.wait_ge(e2_ready, n + 1)
                steps.link(v.tensor_tensor(st[:, 6, :], st[:, 5, :], st[:, 4, :], ALU.add))
                steps.link(v.reciprocal(st[:, 7, :], st[:, 6, :]))
                pr = p2[n % 2][:, :, w:]
                v.tensor_tensor(pr, pr, st[:, 7, :].unsqueeze(2).broadcast_to((P, GROUP, 2 * P - w)), ALU.mult).then_inc(p2_ready, 1)

            def low_out(g):
                for j in range(2):
                    dve.wait_ge(o2_high, g * 2 + j + 1)
                    v.tensor_tensor(o2L[:, g * 2 + j, :], PS[:, 6 + j, :], o2H[:, g * 2 + j, :].bitcast(F32), ALU.subtract).then_inc(o2_low, 1)

            rotate(q2[0], 6, q2_raw, q2_turn, 1).then_inc(q2_ready, 1)
            top2(0)
            for n2 in range(UNITS):
                norm2(n2)
                if n2 + 1 < UNITS:
                    top2(n2 + 1)
                g = n2 // T + 1
                if n2 % T == 0 and n2:
                    low_out(n2 // T - 1)
                if n2 % T == 1 and g < KVH:
                    if g == 1:
                        dve.wait_ge(kd_ready, 1)
                    rotate(q2[g % 2], 0, q2_raw, q2_turn, g + 1).then_inc(q2_ready, 1)
            low_out(KVH - 1)
            n = boundary("wo", n, True, 192)
            gated("gu1", fL)
            n = boundary("dn1", n, False, 208)

        @block.tensor
        def _(pe):
            mm, tr = nc.tensor.matmul, nc.tensor.transpose

            def mm3(dst, lh, ll, rh, rl, first, last):
                mm(dst, lh, rh, start=first, stop=False, skip_group_check=True)
                mm(dst, lh, rl, start=False, stop=False, skip_group_check=True)
                return mm(dst, ll, rh, start=False, stop=last, skip_group_check=True)

            def wcols(w, s):
                return w[s][:, :].rearrange("p (k n) -> p k n", n=256)

            def in_stage(name, turns=None):
                B = BASE[name]

                def chunk(s, tok):
                    for m in range(2):
                        for k in range(K):
                            c = slice(m * P, (m + 1) * P)
                            ins = mm3(PS[:, 2 * s + m, tok], wcols(WH, s)[:, k, c], wcols(WL, s)[:, k, c],
                                      hH[:, k, tok], hL[:, k, tok], k == 0, k == K - 1)
                    return ins

                if turns:
                    q, turn = turns
                    pe.wait_ge(h_ready, T * q + 2)
                    for s in range(2):
                        pe.wait_ge(w_split[s], B.split[s] + 1)
                        pe.wait_ge(pair_free[s], PF[name])
                        chunk(s, slice(0, S // 2))
                        if s == 0:
                            turn(2)
                            turn(3)
                    pe.wait_ge(h_ready, T * q + 4)
                    for s in range(2):
                        chunk(s, slice(S // 2, S)).then_inc(used[s], 1)
                with pe.Fori(1 if turns else 0, B.pairs) as i:
                    for s in range(2):
                        pe.wait_ge(w_split[s], B.split[s] + i + 1)
                        pe.wait_ge(pair_free[s], PF[name] + i)
                        ins = chunk(s, slice(0, S))
                        if name in ADA_AT:
                            for m in range(2):
                                pe.wait_ge(ada_sum[m], i * 2 + (ADA_AT[name] + s + 1 + CREDIT))
                                ins = mm(PS[:, 4, 2 * s + m:2 * s + m + 1], ada_acc[m][:, :], one_col, start=True, stop=True)
                        ins.then_inc(used[s], 1)

            def out_stage(name, lh, ll, ready, bank_ready, first_depth=2, turn=None):
                B = BASE[name]
                kt = 0
                pairs = B.pairs

                def tiles(kt, s, d, t, first, last):
                    for n in range(2):
                        c = slice(d * D + n * S, d * D + (n + 1) * S)
                        ins = mm3(PS[:, 2 * t + n, :], lh[:, kt, t * P:(t + 1) * P], ll[:, kt, t * P:(t + 1) * P],
                                  WH[s][:, c], WL[s][:, c], first, last)
                    return ins

                for j in range(pairs - 1):
                    depth = first_depth if j == 0 else 2
                    for s in range(2):
                        pe.wait_ge(w_split[s], B.split[s] + j + 1)
                        if kt == 0:
                            ready(depth - 1)
                            for t in (2, 3, 0, 1):
                                bank_ready(t)
                                for d in range(depth):
                                    ins = tiles(d, s, d, t, d == 0, False)
                        else:
                            for d in range(depth):
                                ready(kt + d)
                                for t in range(T):
                                    ins = tiles(kt + d, s, d, t, False, False)
                        kt += depth
                        ins.then_inc(used[s], 1)

                def part(s, t):
                    for d in range(2):
                        ins = tiles(kt + 2 * s + d, s, d, t, False, s == 1 and d == 1)
                    return ins

                pe.wait_ge(w_split[0], B.split[0] + pairs)
                ready(kt + 1)
                for t in range(3):
                    part(0, t)
                pe.wait_ge(w_split[1], B.split[1] + pairs)
                ready(kt + 3)
                for t in range(2):
                    part(1, t).then_inc(y_ready, 1)
                part(0, 3).then_inc(used[0], 1)
                part(1, 2).then_inc(y_ready, 1)
                if turn:
                    turn(0)
                part(1, 3).then_inc(used[1], 1)
                if turn:
                    turn(1)

            def turn_tile(q, t, src, ready, b=None):
                ready(t)
                for k in range(K):
                    ins = tr(two(2 * t if b is None else b)[:, k, :], src[:, k * P:(k + 1) * P], ident)
                ins.then_inc(tr_done, 1)

            pe.wait_ge(small_in, 16 * 10)
            tr(PS[:, 7, 0:N_ROWS], rows[0:N_ROWS, :], ident[0:N_ROWS, 0:N_ROWS]).then_inc(rows_tr, 1)
            pe.wait_ge(csil_ready, 1)

            def ada_chunk(c):
                pe.wait_ge(ada_full[c], 16)
                w = ada_raw[c][:, :].rearrange("p (k n) -> p k n", n=256)
                for m in range(2):
                    for k in range(K):
                        ins = mm(PS[:, 7, 256 + 2 * c + m:257 + 2 * c + m], w[:, k, m * P:(m + 1) * P], csil[:, k:k + 1],
                                 start=(k == 0), stop=(k == K - 1))
                return ins

            for c in range(ADA_FIRST // 2 + 1):
                ada_chunk(c)
            pe.wait_ge(x_in, 16)
            for t in range(3):
                turn_tile(0, t, x[:, t, :], lambda t: None)
            pe.wait_ge(ws_in, 16)
            for h in range(G_HEADS):
                ins = tr(PS[:, 6, h * P:(h + 1) * P], ws_sb[:, h, :], ident)
            ins.then_inc(ws_tr, 1)
            for c in range(ADA_FIRST // 2 + 1, ADA_FIRST):
                ins = ada_chunk(c)
            ins.then_inc(ada_done, 1)
            pe.wait_ge(mod_ready, 1)
            turn_tile(0, 3, x[:, 3, :], lambda t: None)

            def left(name):
                return lambda t: pe.wait_ge(pair_free[t], PF[name]) if t < 2 else None

            def gate_rows(n, one, dg, b):
                pe.wait_ge(diag_ready, n)
                for k in range(K):
                    ins = mm(two(b)[:, k, :], one[:, :], dg[:, k, :], start=True, stop=True)
                ins.then_inc(gate_mm, 1)

            B = BASE["v"]
            for c in range(4):
                n, s = c // 2, c % 2
                pe.wait_ge(w_split[s], B.split[s] + n + 1)
                for t in range(T):
                    if c == 0:
                        pe.wait_ge(h_ready, t + 1)
                    for k in range(4):
                        kt = 4 * s + k
                        w = slice(k * S, (k + 1) * S)
                        ins = mm3(PS[:, 4 * n + t, :], hH[:, kt, t * P:(t + 1) * P], hL[:, kt, t * P:(t + 1) * P],
                                  WH[s][:, w], WL[s][:, w], kt == 0, kt == K - 1)
                ins.then_inc(used[s], 1)
            pe.wait_ge(vn_ready, 1)
            in_stage("xb")
            pe.wait_ge(vn_ready, 2)
            pe.wait_ge(wT_ready, 1)
            pe.wait_ge(ada_col, ADA_AT["zu"])
            for f in range(K):
                if f >= 4:
                    pe.wait_ge(sv_ready, f - 3)
                for b in range(T):
                    ins = mm(PS[:, 4 + f % 4, b * P:(b + 1) * P], vn[:, b, f * P:(f + 1) * P], wT[:, f // 2, :], start=True, stop=True)
                ins.then_inc(sp_done, 1)
            pe.wait_ge(sv_ready, K)
            in_stage("zu")
            B = BASE["pool"]
            pe.wait_ge(pool_low, 1)
            pe.wait_ge(ada_col, ADA_AT["zb"])
            for f in range(K):
                g, m, s = f // 2, f % 2, f // 4
                if f % 4 == 0:
                    pe.wait_ge(w_split[s], B.split[s] + 1)
                if f >= 4:
                    pe.wait_ge(yb_ready, f - 3)
                for k in range(2):
                    c = (2 * (g % 2) + k) * 256 + m * P
                    ins = mm3(PS[:, 4 + f % 4, :], WH[s][:, c:c + P], WL[s][:, c:c + P], poolH[:, 2 * g + k, :], poolL[:, 2 * g + k, :], k == 0, k == 1)
                ins.then_inc(used[s] if f % 4 == 3 else py_done, 1)
            pe.wait_ge(yb_ready, K)
            in_stage("zb")
            pe.wait_ge(ada_col, ADA_END)
            gate_rows(1, ones, diag, 6)
            def turn_norm(t):
                turn_tile(TR["eout"], t, x[:, t, :], lambda t: pe.wait_ge(norm_ready, t + 1))

            out_stage("eout", mixH, mixL, lambda kt: pe.wait_ge(gate_low, 2 + kt + 1),
                      lambda t: pe.wait_ge(gate_ready, 1) if t == 3 else left("cu")(t), turn=turn_norm)

            B = BASE["lat"]
            for t in range(T):
                pe.wait_ge(h_ready, T + t + 1)
                for s in range(2):
                    pe.wait_ge(w_split[s], B.split[s] + 1)
                    for k in range(4):
                        kt = 4 * s + k
                        w = slice(k * S, k * S + LATENT)
                        ins = mm3(PS[:, t, 0:LATENT], hH[:, kt, t * P:(t + 1) * P], hL[:, kt, t * P:(t + 1) * P],
                                  WH[s][:, w], WL[s][:, w], kt == 0, kt == K - 1)
                    if t == T - 1:
                        ins.then_inc(used[s], 1)
                if 1 <= t < 3:
                    turn_norm(t + 1)
            gate_rows(2, ones1, diag1, 4)
            pe.wait_ge(latn_ready, 1)
            pe.wait_ge(gate_ready, 2)
            for j in range(4):
                for t in range(T):
                    ins = tr(PS[:, 4 + j, t * P:(t + 1) * P], latn[:, t, j * P:(j + 1) * P], ident)
            ins.then_inc(lat_tr, 1)
            pe.wait_ge(lat_ev, 1)
            pe.wait_ge(late_in, 32)
            mm(PS[:, 0, :], turn_m[:, :], kraw[:, :], start=True, stop=True).then_inc(kr_turn, 1)
            pe.wait_ge(kr_ready, 1)

            B = BASE["mla"]
            wn = raw[1][:, 0:512].rearrange("p (k h e) -> p k h e", k=2, h=2)
            wr = raw[1][:, 512:768].rearrange("p (k m) -> p k m", k=2)
            wk = raw[1][:, 768:1024].rearrange("p (h e) -> p h e", h=2)
            wv = raw[1][:, 1024:1280]
            with pe.Fori(0, 8) as i:
                pe.wait_ge(w_full[1], B.full[1] + (i + 1) * 16 * B.dmas[1])
                for k in range(2):
                    ins = mm(PS[:, 2, :], wr[:, k, :], qcT[:, k, :], start=(k == 0), stop=(k == 1))
                ins.then_inc(proj_done, 1)
                for h in range(2):
                    ins = mm(PS[:, 4 + h, :], wk[:, h, :], kvT[:, :], start=True, stop=True)
                ins.then_inc(proj_done, 1)
                pe.wait_ge(qa_ready, i * 2 + 1)
                mm(PS[:, 3, :], turn_m[:, :], qraw[:, :], start=True, stop=True).then_inc(q_turn, 1)
                pe.wait_ge(oz_ready, i * 2 + CREDIT)
                for h in range(2):
                    for k in range(2):
                        ins = mm(PS[:, h, :], wn[:, k, h, :], qcT[:, k, :], start=(k == 0), stop=(k == 1))
                ins.then_inc(proj_done, 1)
                for t in range(T):
                    ins = mm(PS[:, 6 + t // 2, (t % 2) * 256:(t % 2 + 1) * 256], kvT[:, t * P:(t + 1) * P], wv, start=True, stop=True)
                ins.then_inc(proj_done, 1)
                pe.wait_ge(proj_done, i * 4 + 4)
                pe.sem_inc(used[1], 1)
                pe.wait_ge(w_split[0], B.split[0] + i + 1)
                pe.wait_ge(qa_ready, i * 2 + 2)

                def z_part(j):
                    m = j // 4
                    for k in (2 * (j % 4), 2 * (j % 4) + 1):
                        c = slice(m * P, (m + 1) * P)
                        ins = mm3(PS[:, m, :], wcols(WH, 0)[:, k, c], wcols(WL, 0)[:, k, c], hH[:, k, :], hL[:, k, :],
                                  k == 0, k == K - 1)
                    if j == 7:
                        ins.then_inc(used[0], 1)

                def score(u):
                    h, q = u // T, u % T
                    w = (q + 1) * P
                    if u >= 2:
                        pe.wait_ge(e_ready, i * 8 + u - 1)
                    rp = slice(h * ROPE, (h + 1) * ROPE)
                    mm(PS[:, 2 + u % 2, 0:w], qn[:, h, q * P:w], kn[:, h, 0:w], start=True, stop=False)
                    mm(PS[:, 2 + u % 2, 0:w], qr[rp, q * P:w], kr[rp, 0:w], start=False, stop=True).then_inc(s_done, 1)

                def turn(u):
                    q = u % T
                    if u >= 2:
                        pe.wait_ge(pT_ready, i * 8 + u - 1)
                    pe.wait_ge(p_ready, i * 8 + u + 1)
                    for k in range(q + 1):
                        ins = tr(PS[:, 4 + u % 2, k * P:(k + 1) * P], pm[u % 2][:, k * P:(k + 1) * P], ident)
                    ins.then_inc(t_done, 1)

                def weigh(h):
                    pe.wait_ge(kv_ready, i + 1)
                    pe.wait_ge(pT_ready, i * 8 + T * h + T)
                    for k in range(T):
                        ins = mm(PS[:, 6 + h, k * P:], vh[:, k, h * NOPE:(h + 1) * NOPE], pT[h][:, k, k * P:],
                                 start=(k == 0), stop=(k == T - 1), skip_group_check=True)
                    ins.then_inc(pv_done, 1)

                z_part(0)
                pe.wait_ge(qr_ready, i + 1)
                score(0)
                score(1)
                z_part(1)
                z_part(2)
                for u in range(8):
                    turn(u)
                    if u + 2 < 8:
                        score(u + 2)
                    if u == T:
                        weigh(0)
                    if u + 3 < 8:
                        z_part(u + 3)
                weigh(1)
            pe.wait_ge(oz_ready, HEADS + CREDIT)

            def turner(name, n, hats):
                q = TR[name]
                return lambda t: turn_tile(q, t, hats[t % 2], lambda t: pe.wait_ge(xhat_ready, n * T + t + 1))

            turn = turner("oout", 0, x_hat1)
            out_stage("oout", oH, oL, lambda kt: pe.wait_ge(ol_ready, kt + 1), lambda t: None, turn=turn)
            in_stage("cu", (TR["oout"], turn))
            in_stage("b")
            turn = turner("aout", 1, x_hat)
            out_stage("aout", yH, yL, lambda kt: pe.wait_ge(gate_low, 2 + GATED["b"] + kt + 1), left("gu0"), turn=turn)
            in_stage("gu0", (TR["aout"], turn))
            turn = turner("dn0", 2, x_hat)
            out_stage("dn0", fH, fL, lambda kt: pe.wait_ge(gate_low, 2 + GATED["gu0"] + kt + 1), left("gu1"), 1, turn=turn)

            B = BASE["kv"]
            pe.wait_ge(w_split[0], B.split[0] + 1)
            for t in range(T):
                pe.wait_ge(h_ready, T * TR["q"] - T + t + 1)
                for k in range(K):
                    ins = mm3(PS[:, t // 2, (t % 2) * 256:(t % 2 + 1) * 256], hH[:, k, t * P:(t + 1) * P], hL[:, k, t * P:(t + 1) * P],
                              wcols(WH, 0)[:, k, :], wcols(WL, 0)[:, k, :], k == 0, k == K - 1)
                if 1 <= t < 3:
                    turn(t + 1)
            ins.then_inc(used[0], 1)
            def turn_queries(t):
                if t >= 2:
                    pe.wait_ge(h_ready, T * TR["q"] + t - 1)
                turn_tile(TR["q"], t, x_hat[t % 2], lambda t: pe.wait_ge(xhat_ready, 3 * T + t + 1), 4 + 2 * (t % 2))

            turn_queries(0)
            turn_queries(1)
            pe.wait_ge(w_split[1], B.split[1] + 1)
            for m in range(2):
                for k in range(K):
                    c = slice(m * P, (m + 1) * P)
                    ins = mm3(PS[:, 2 + m, :], wcols(WH, 1)[:, k, c], wcols(WL, 1)[:, k, c], hH[:, k, :], hL[:, k, :], k == 0, k == K - 1)
            ins.then_inc(used[1], 1)
            pe.wait_ge(k2_raw, 1)
            pe.wait_ge(late_in, 48)
            for m in range(2):
                ins = mm(PS[:, 2 + m, :], turn_b, q2raw[:, m, :], start=True, stop=True)
            ins.then_inc(k2_turn, 1)
            turn_queries(2)
            turn_queries(3)

            B = BASE["q"]

            def queries(g, first, last, tok=slice(0, S)):
                s = g % 2
                if first == 0:
                    pe.wait_ge(w_split[s], B.split[s] + g // 2 + 1)
                    if g >= 2:
                        pe.wait_ge(q2_ready, g)
                for j in range(first, last):
                    m, k = j // K, j % K
                    c = slice(m * P, (m + 1) * P)
                    ins = mm3(PS[:, m, tok], wcols(WH, s)[:, k, c], wcols(WL, s)[:, k, c], hH[:, k, tok], hL[:, k, tok], k == 0, k == K - 1)
                if last == 2 * K and tok.stop == S:
                    ins.then_inc(used[s], 1)

            def partners(g):
                pe.wait_ge(q2_raw, g + 1)
                for m in range(2):
                    ins = mm(PS[:, m if g else 6 + m, :], turn_b, q2raw[:, m, :], start=True, stop=True)
                ins.then_inc(q2_turn, 1)

            def score2(n):
                g, b = n // T, n % T
                if b == 0:
                    pe.wait_ge(q2_ready, g + 1)
                if n:
                    pe.wait_ge(m2_ready, n)
                lo = max(b - 1, 0) * P
                for h in range(GROUP):
                    r = slice((h % 2) * HD, (h % 2 + 1) * HD)
                    c = (h // 2) * 2 * P
                    ins = mm(PS[:, 2 + h % 2, c + (0 if b else P):c + 2 * P], q2[g % 2][r, h // 2, b * P:(b + 1) * P],
                             kdup[r, g, lo:(b + 1) * P], start=True, stop=True)
                ins.then_inc(s2_done, 1)

            def turn2(n):
                if n:
                    pe.wait_ge(p2T_ready, n)
                pe.wait_ge(p2_ready, n + 1)
                for h in range(GROUP):
                    for k in range(0 if n % T else 1, 2):
                        ins = tr(two(4)[:, 2 * h + k, :], p2[n % 2][:, h, k * P:(k + 1) * P], ident)
                ins.then_inc(t2_done, 1)

            def weigh2(n):
                g, b = n // T, n % T
                if b == 0 and g:
                    pe.wait_ge(o2_low, 2 * g)
                pe.wait_ge(p2T_ready, n + 1)
                for h in range(GROUP):
                    o, j = h // 2, h % 2
                    ks = range(0 if b else 1, 2)
                    for k in ks:
                        ins = mm(PS[o * HD:(o + 1) * HD, 6 + j, b * P:(b + 1) * P], vall[:, b - 1 + k, g * HD:(g + 1) * HD],
                                 p2T[n % 2][:, 2 * h + k, :], start=(k == ks[0]), stop=(k == 1), skip_group_check=True)
                ins.then_inc(pv2_done, 1)

            pe.wait_ge(v2_ready, 1)
            pe.wait_ge(h_ready, T * TR["q"] + 2)
            queries(0, 0, 2 * K, slice(0, S // 2))
            pe.wait_ge(h_ready, T * TR["q"] + 4)
            queries(0, 0, 2 * K, slice(S // 2, S))
            partners(0)
            queries(1, 0, 10)
            pe.wait_ge(kd_ready, 1)
            score2(0)
            for n in range(UNITS):
                g, b = n // T, n % T
                if n + 1 < UNITS:
                    score2(n + 1)
                if n:
                    weigh2(n - 1)
                if b == 0 and g + 1 < KVH:
                    queries(g + 1, 10, 2 * K)
                elif b == 1 and g + 1 < KVH:
                    partners(g + 1)
                turn2(n)
                if b == 2 and g + 2 < KVH:
                    queries(g + 2, 0, 4)
                elif b == 3 and g + 2 < KVH:
                    queries(g + 2, 4, 10)
            weigh2(UNITS - 1)
            turn = turner("wo", 4, x_hat)
            out_stage("wo", o2H, o2L, lambda kt: pe.wait_ge(o2_low, kt + 1),
                      lambda t: pe.wait_ge(o2_low, K) if t == 3 else None, turn=turn)
            in_stage("gu1", (TR["wo"], turn))
            out_stage("dn1", fH, fL, lambda kt: pe.wait_ge(gate_low, 2 + GATED["gu1"] + kt + 1), left("end"), 1)


_LAYOUT = [
    ("x", "x", (S, D)), ("c", "c", (1, D)), ("positions", "positions", (1, S)),
    ("ada_w", "ada_w", (DEPTH, D, 3 * D)), ("ada_b", "ada_b", (DEPTH, 3 * D)), ("ln_g", "ln_g", (DEPTH, D)), ("ln_b", "ln_b", (DEPTH, D)),
    ("e_w_in", "e_w_in", (D, 5 * D)), ("gmlp_norm_g", "gmlp_norm_g", (1, G_DIM)), ("gmlp_norm_b", "gmlp_norm_b", (1, G_DIM)),
    ("gmlp_ws", "gmlp_ws", (G_HEADS, P, P)), ("gmlp_bs", "gmlp_bs", (1, G_HEADS * P)), ("pool_w", "pool_w", (4, 256, 256)),
    ("pool_b", "pool_b", (1, D)), ("pool_scale", "pool_scale", (1, D)), ("e_w_out", "e_w_out", (2 * D, D)),
    ("o_w_in", "o_w_in", (D, LATENT + HEADS * NOPE)), ("mla_q_norm_g", "q_g", (1, QR)), ("mla_kv_norm_g", "kv_g", (1, KVR)),
    ("mla_w_uq", "mla_w_uq", (QR, HEADS, NOPE + ROPE)), ("mla_w_uk", "mla_w_uk", (KVR, HEADS, NOPE)),
    ("mla_w_uv", "mla_w_uv", (KVR, HEADS, NOPE)), ("o_w_out", "o_w_out", (2 * D, D)),
    ("a_pre_norm_2", "a_pre", (1, D)), ("a_w_in_2", "a_w_in", (D, 3 * D)), ("a_conv_w_2", "conv", (3, D)), ("a_w_out_2", "a_w_out", (D, D)),
    ("a_post_norm_2", "a_post", (1, D)), ("ffn_pre_norm_2", "f_pre", (DEPTH, D)), ("ffn_w_gate_up_2", "f_gate_up", (DEPTH, D, 2 * D_FF)),
    ("ffn_w_down_2", "f_down", (DEPTH, D_FF, D)), ("ffn_post_norm_2", "f_post", (DEPTH, D)), ("kv_norm_2", "kv_norm", (1, D)),
    ("w_kv_2", "w_kv", (D, 2 * KVH * HD)), ("b_pre_norm_2", "b_pre", (1, D)), ("b_w_q_2", "b_w_q", (D, D)), ("b_sinks_2", "b_sinks", (1, 16)),
    ("b_w_o_2", "b_w_o", (D, D)), ("b_post_norm_2", "b_post", (1, D)),
]


def kernel(**inputs):
    import numpy as _np
    import concourse.bacc as _bacc
    from concourse import mybir as _mybir
    from concourse.bass_utils import run_bass_kernel_spmd as _run

    nc = _bacc.Bacc("TRN2", target_bir_lowering=False, num_devices=1)
    arrays, args = {}, {}
    given = [(name, _np.ascontiguousarray(inputs[src]).reshape(shape)) for src, name, shape in _LAYOUT]
    for name, value in given + list(constants().items()):
        arrays[f"in_{name}"] = value
        args[name] = nc.dram_tensor(f"in_{name}", value.shape, _mybir.dt.from_np(value.dtype), kind="ExternalInput").ap()
    out = nc.dram_tensor("out_x", (S, D), F32, kind="ExternalOutput").ap()
    program(nc, args, out)
    r = _run(nc, [arrays], core_ids=[0])
    return r.results[0]["out_x"].reshape(1, S, D)
```

```python
from contextlib import ExitStack

import numpy as np
import concourse.bass as bass
from concourse import mybir

F32 = mybir.dt.float32
F32R = mybir.dt.float32r
I32 = mybir.dt.int32
ALU = mybir.AluOpType
ACT = mybir.ActivationFunctionType
AX = mybir.AxisListType.X

P = 128
S = 512
T = S // P
D = 1024
K = D // P
CHUNK = 2048
DEPTH = 2

G_HEADS, G_DIM, G_HALF = 4, 256, 64
POOL_WINDOWS = (2, 4, 8, 16)
PAD = 16
MIX = 16
LN_EPS = 1e-5
ALPHA = (2.0 * DEPTH) ** 0.25
HEADS, NOPE, ROPE, QR, KVR = 16, 128, 64, 256, 128
LATENT = QR + KVR + ROPE
MLA_CHUNK = 2 * (2 * (QR // P) * NOPE // 2 + QR // P * ROPE + 2 * NOPE)
MLA_SCALE = (NOPE + ROPE) ** -0.5
MASKED = -1e30
HD, KVH, GROUP = 64, 4, 4
SW_SCALE = HD ** -0.5
EPS2 = 1e-6
F_TILES = 2816 // P
D_FF = 2816

TWO_PI = 2.0 * np.pi
PI_1 = 6.28125
PI_2 = float(np.float32(np.round((TWO_PI - PI_1) * 2 ** 19) / 2 ** 19))
PI_3 = float(TWO_PI - PI_1 - PI_2)
ROUND = 12582912.0

ROWS = {}
_n = 0
for _name, _count in (("ada_b", 48), ("c", 8), ("pool_b", 8), ("pool_scale", 8), ("q_g", 2), ("kv_g", 1), ("conv", 24),
                      ("ln_g", 8), ("ln_b", 8)):
    ROWS[_name] = _n
    _n += _count
N_ROWS = _n
N_FIRST = ROWS["pool_b"]

RING = [
    ("v", 2, (2, 2)),
    ("xb", 2, (2, 2)),
    ("zu", 4, (2, 2)),
    ("pool", 1, (2, 2)),
    ("zb", 2, (2, 2)),
    ("eout", 4, (2, 2)),
    ("lat", 1, (2, 2)),
    ("mla", 8, (2, 6)),
    ("oout", 4, (2, 2)),
    ("cu", 4, (2, 2)),
    ("b", 2, (2, 2)),
    ("aout", 2, (2, 2)),
    ("gu0", 11, (2, 2)),
    ("dn0", 6, (2, 2)),
    ("kv", 1, (2, 2)),
    ("q", 2, (2, 2)),
    ("wo", 2, (2, 2)),
    ("gu1", 11, (2, 2)),
    ("dn1", 6, (2, 2)),
]


class Base:

    def __init__(self, pairs, dmas, full, use, split):
        self.pairs, self.dmas = pairs, dmas
        self.full, self.use, self.split = tuple(full), tuple(use), tuple(split)


BASE = {}
_full, _use, _split = [0, 0], [0, 0], [0, 0]
for _name, _pairs, _dmas in RING:
    BASE[_name] = Base(_pairs, _dmas, _full, _use, _split)
    for _s in range(2):
        _full[_s] += 16 * _dmas[_s] * _pairs
        _use[_s] += _pairs
        _split[_s] += _pairs
NAMES = [r[0] for r in RING]

GATED = {}
_n = 0
for _name, _count in (("zu", 8), ("zb", 8), ("b", 8), ("gu0", F_TILES), ("gu1", F_TILES)):
    GATED[_name] = _n
    _n += _count


ADA_FIRST = 2 * K // 2
ADA_AT, _n = {}, 0
for _name in ("xb", "zu", "zb"):
    ADA_AT[_name] = _n
    _n += 2 * BASE[_name].pairs
ADA_END = _n
assert 2 * K + 2 * ADA_END == 3 * K * DEPTH


class Steps:

    def __init__(self, eng, sem):
        self.eng, self.sem, self.n, self.off = eng, sem, 0, 0

    def link(self, ins):
        ins.then_inc(self.sem, 1)
        self.n += 1
        self.eng.wait_ge(self.sem, self.off + self.n)

    def loop(self, i, per):
        self.off, self.first, self.per = i * per, self.n, per

    def done(self, count):
        assert self.n - self.first == self.per, (self.n - self.first, self.per)
        self.n = self.first + self.per * count
        self.off = 0


def constants():
    ident = np.eye(P, dtype=np.float32)
    inv = np.ones((P, len(POOL_WINDOWS) * PAD), np.float32)
    for g, w in enumerate(POOL_WINDOWS):
        for t in range(PAD):
            inv[:, g * PAD + t] = np.float32(1.0) / np.float32(min(t + 1, w))
    r = np.arange(P)
    half = ROPE // 2
    freq = (np.float32(1.0) / (np.float32(10000.0) ** (np.arange(0, ROPE, 2, dtype=np.float32) / np.float32(ROPE)))).astype(np.float32)
    freq_col = freq[r % half][:, None].astype(np.float32)
    turn_m = np.zeros((P, P), np.float32)
    for m in range(P):
        low = (m % ROPE) < half
        turn_m[m + half if low else m - half, m] = -1.0 if low else 1.0
    rot, rh = HD // 4, HD // 8
    inv_freq = (np.float32(500000.0) ** (-np.arange(0, rot, 2, dtype=np.float32) / np.float32(rot))).astype(np.float32)
    ang = (np.arange(S, dtype=np.float32)[:, None] * inv_freq[None, :]).astype(np.float32)
    cos_b, sin_b = np.ones((P, S), np.float32), np.zeros((P, S), np.float32)
    turn_b = np.zeros((P, P), np.float32)
    for m in range(P):
        d = m % HD
        if d < rot:
            cos_b[m], sin_b[m] = np.cos(ang[:, d % rh]), np.sin(ang[:, d % rh])
            turn_b[m + rh if d < rh else m - rh, m] = -1.0 if d < rh else 1.0
    qi, kj = np.arange(P)[:, None], np.arange(2 * P)[None, :]
    diff = P + qi - kj
    window = np.where((diff >= 0) & (diff < P), 0.0, MASKED).astype(np.float32)
    return {
        "k_small": np.concatenate([ident, inv, freq_col, np.ones((P, 1))], axis=1).astype(np.float32),
        "k_turn_m": turn_m,
        "k_swa": np.concatenate([turn_b, window, cos_b, sin_b], axis=1).astype(np.float32),
    }


N_INV = len(POOL_WINDOWS) * PAD


UNITS = KVH * T
CREDIT = 1


def program(nc, a, out):
    with ExitStack() as ctx:

        def sem(name):
            return ctx.enter_context(nc.semaphore(name))

        KB = 1024
        arena = ctx.enter_context(nc.sbuf_tensor("arena", [P, 206 * KB // 4], F32))
        start = nc.sbuf_base - 206 * KB

        def at(name, offset, shape, dt=F32):
            return nc.alloc_sbuf_tensor_at(name, shape, dt, offset=start + offset)

        raw = [at(f"w_raw{s}", 8 * KB * s, [P, CHUNK]) for s in range(2)]
        WH = [at(f"w_high{s}", (16 + 8 * s) * KB, [P, CHUNK], F32R) for s in range(2)]
        WL = [at(f"w_low{s}", (32 + 8 * s) * KB, [P, CHUNK], F32R) for s in range(2)]
        ZB = 48 * KB
        hH = at("h_high", ZB, [P, K, S], F32R)
        hL = at("h_low", ZB + 16 * KB, [P, K, S], F32R)
        scaled = at("scaled", ZB + 16 * KB, [P, K, S])
        x = at("x", 80 * KB, [P, T, D])
        ZD = 96 * KB
        gains = at("gains", 184 * KB, [P, 4, D])
        hf = at("hf", 200 * KB, [P, D])
        buf = [at(f"gate_buf{m}", (200 + 2 * m) * KB, [P, S]) for m in range(2)]
        ofs = 204 * KB

        def tiny(name, shape):
            nonlocal ofs
            got = at(name, ofs, shape)
            size = 4
            for d in shape[1:]:
                size *= d
            ofs += (size + 31) // 32 * 32
            assert ofs <= 206 * KB
            return got

        small = tiny("small", [P, P + N_INV + 2])
        ident, inv_count, freq = small[:, 0:P], small[:, P:P + N_INV], small[:, P + N_INV:P + N_INV + 1]
        one_col = small[:, P + N_INV + 1:P + N_INV + 2]
        vec = tiny("vec", [P, N_ROWS])
        mod = tiny("mod", [P, 48])
        csil = tiny("csil", [P, K])
        stat = tiny("stat", [P, T, 8])
        bn = tiny("bn", [P, 8, 6])
        mv = tiny("mv", [P, 8, 2])
        eps = tiny("eps", [P, 2])
        sinks = tiny("sinks", [P, 16])

        def dz(name, offset, shape, dt=F32):
            return at(name, ZD + 4 * offset, shape, dt)

        sv = dz("sv", 0, [P, K, S])
        mixH = dz("mix_high", 4096, [P, MIX, S], F32R)
        mixL = dz("mix_low", 12288, [P, MIX, S], F32R)
        pooled = dz("pooled", 8192, [P, K, S])
        vn = dz("v_norm", 16384, [P, T, D])
        xbuf, sum_a, sum_b = (dz(n, 20480 + 528 * j, [P, PAD + S]) for j, n in enumerate(("xbuf", "sum_a", "sum_b")))
        xbufs = [xbuf, hf[:, 0:PAD + S]]
        poolH = dz("pool_high", 16384, [P, K, S], F32R)
        poolL = dz("pool_low", 8192, [P, K, S], F32R)
        ada_raw = [dz(f"ada_raw{c}", 2048 * c, [P, CHUNK]) for c in range(ADA_FIRST)]
        ada_part = [dz(f"ada_part{c}", 16384 + 512 * c, [P, 2, 256]) for c in range(ADA_FIRST)]
        ada_buf = [gains[:, 3 * m, :].rearrange("p (k n) -> p k n", k=K) for m in range(2)]
        ada_acc = [dz(f"ada_acc{m}", 22064 + P * m, [P, P]) for m in range(2)]
        ones = dz("ones", 20480, [P, P])
        diag = dz("diag", 20480 + P, [P, K, P])
        mod_tmp = dz("mod_tmp", 0, [P, D])
        g_bc = gains[:, 1, 0:G_DIM]
        b_bc = gains[:, 1, G_DIM:2 * G_DIM]
        bs_bc = gains[:, 1, 2 * G_DIM:4 * G_DIM]
        ws_sb = gains[:, 2, 0:S].rearrange("p (h s) -> p h s", h=G_HEADS)
        wT = gains[:, 2, S:2 * S].rearrange("p (h t) -> p h t", h=G_HEADS)
        rows = hf[:, 0:P]
        x_hat = [hf, gains[:, 3, :]]
        oz = dz("o_gated", 0, [P, HEADS, S])
        qcH, qcL = dz("qc_high", 8192, [P, 2, S], F32R), dz("qc_low", 15488, [P, 2, S], F32R)
        kvH, kvL = dz("kv_high", 9216, [P, S], F32R), dz("kv_low", 21632, [P, S], F32R)
        kr, krL = dz("k_rope", 9728, [P, S]), dz("k_rope_low", 9728, [P, S], F32R)
        cosM, sinM = dz("cos_m", 10240, [P, S]), dz("sin_m", 10752, [P, S])
        turn_m = dz("turn_m", 11264, [P, P])
        qnH, qnL = dz("q_nope_high", 11392, [P, 2, S], F32R), at("q_nope_low", 188 * KB, [P, 2, S], F32R)
        qraw = dz("q_raw", 12416, [P, S])
        ones1, diag1 = dz("ones1", 11392, [P, P]), dz("diag1", 11520, [P, K, P])
        qr, qrL = dz("q_rope", 12928, [P, S]), dz("q_rope_low", 12928, [P, S], F32R)
        knH, knL = dz("k_nope_high", 13440, [P, 2, S], F32R), at("k_nope_low", 192 * KB, [P, 2, S], F32R)
        qrH, krH = (at(n, (196 + 2 * j) * KB, [P, S], F32R) for j, n in enumerate(("q_rope_high", "k_rope_high")))
        vh = dz("v_heads", 14464, [P, T, 2 * NOPE])
        pm = [dz(f"probs{u}", 16512 + 512 * u, [P, S]) for u in range(2)]
        pT = [dz(f"probs_t{u}", 17536 + 2048 * u, [P, T, S]) for u in range(2)]
        kraw = dz("k_raw", 16512, [P, S])
        latn = dz("latent_norm", 17536, [P, T, S])
        pos = dz("pos", 1024, [P, S], I32)
        ang, turns, rest = (dz(n, 1536 + 512 * j, [P, S]) for j, n in enumerate(("ang", "turns", "rest")))
        x_hat1 = [dz(f"x_hat1_{j}", 1024 * j, [P, D]) for j in range(2)]
        oH = at("o_high", ZB, [P, HEADS, S], F32R)
        oL = dz("o_low", 8192, [P, HEADS, S], F32R)
        soft = dz("soft", 22400, [P, 2, 8, 4])
        yc = dz("conv_out", 0, [P, K, S])
        cw = dz("conv_in", 4096, [P, 2 + S])
        cv = dz("conv_sum", 4704, [P, S])
        yH, yL = dz("y_high", 8192, [P, K, S], F32R), dz("y_low", 12288, [P, K, S], F32R)
        fH, fL = dz("ff_high", 0, [P, F_TILES, S], F32R), dz("ff_low", F_TILES * S, [P, F_TILES, S], F32R)
        kdup = dz("k_dup", 0, [P, KVH, S])
        vall = dz("v_all", 2048, [P, T, KVH * HD])
        swa = dz("swa", 3072, [P, P + 2 * P + 2 * S])
        turn_b, window = swa[:, 0:P], swa[:, P:3 * P]
        cosB, sinB = swa[:, 3 * P:3 * P + S], swa[:, 3 * P + S:3 * P + 2 * S]
        q2raw = dz("q2_raw", 4480, [P, 2, S])
        q2 = [dz(f"q2_{g}", 5504 + 1024 * g, [P, 2, S]) for g in range(2)]
        q2tmp = dz("q2_tmp", 7552, [P, 2, S])
        p2 = [dz(f"probs2_{u}", o, [P, GROUP, 2 * P]) for u, o in enumerate((8576, 9600, 20864))]
        p2T = [dz(f"probs2_t{u}", 10624 + 1024 * u, [P, 2 * GROUP, P]) for u in range(2)]
        o2H, o2L = dz("o2_high", 12672, [P, K, S], F32R), dz("o2_low", 16768, [P, K, S], F32R)

        PS = ctx.enter_context(nc.psum_tensor("PS", [P, 8, S], F32))

        def tile(ap, t):
            return ap[:, :, t * P:(t + 1) * P]

        def two(b):
            return PS[:, b:b + 2, :].rearrange("p a (c t) -> p (a c) t", t=P)

        def flat2(b):
            return PS[:, b:b + 2, :].rearrange("p a n -> p (a n)")

        w_full = [sem(f"w_full{s}") for s in range(2)]
        raw_free = [sem(f"raw_free{s}") for s in range(2)]
        w_high = [sem(f"w_high_ready{s}") for s in range(2)]
        w_split = [sem(f"w_split{s}") for s in range(2)]
        used = [sem(f"used{s}") for s in range(2)]
        pair_free = [sem(f"pair_free{s}") for s in range(2)]
        ada_full = [sem(f"ada_full{c}") for c in range(ADA_FIRST)]
        ada_land = [sem(f"ada_land{m}") for m in range(2)]
        ada_prod = [sem(f"ada_prod{m}") for m in range(2)]
        ada_sum = [sem(f"ada_sum{m}") for m in range(2)]
        x_in = [sem(f"x_in{t}") for t in range(T)]
        ada_first = sem("ada_first")
        ada_done, ada_col = sem("ada_done"), sem("ada_col")
        small_in, rest_in, aux_in, gains_in, late_in = (sem(n) for n in ("small_in", "rest_in", "aux_in", "gains_in", "late_in"))
        act_step, dve_step, pool_step, pool_ready = sem("act_step"), sem("dve_step"), sem("pool_step"), sem("pool_ready")
        rows_tr, vec_ready, csil_ready, ws_tr, wT_ready = (sem(n) for n in ("rows_tr", "vec_ready", "csil_ready", "ws_tr", "wT_ready"))
        mod_ready, diag_ready, gate_mm, gate_ready = (sem(n) for n in ("mod_ready", "diag_ready", "gate_mm", "gate_ready"))
        tr_done, h_high, h_ready, xhat_ready = (sem(n) for n in ("tr_done", "h_high_ready", "h_ready", "xhat_ready"))
        pool_half, dve_half = sem("pool_half"), sem("dve_half")
        mod_half, v_left = sem("mod_half"), sem("v_left")
        lnv_stat, lnv_sqrt, vn_ready, sp_done, sv_ready = (sem(n) for n in ("lnv_stat", "lnv_sqrt", "vn_ready", "sp_done", "sv_ready"))
        sg_ready, prod_ready, act_high, gate_low = (sem(n) for n in ("sg_ready", "prod_ready", "act_high", "gate_low"))
        xb_ready, pooled_ready, pool_high, pool_low, py_done, yb_ready = (
            sem(n) for n in ("xb_ready", "pooled_ready", "pool_high_ready", "pool_low_ready", "py_done", "yb_ready"))
        y_ready, ln_stat, sqrt_ready, norm_ready, x_ready = (
            sem(n) for n in ("y_ready", "ln_stat", "sqrt_ready", "norm_ready", "x_ready"))
        rest_ready, sin_ready, lat_done, lat_sqrt, latn_ready, lat_tr, lat_ev, kr_turn, kr_ready = (
            sem(n) for n in ("rest_ready", "sin_ready", "lat_done", "lat_sqrt", "latn_ready", "lat_tr", "lat_ev", "kr_turn", "kr_ready"))
        lat_low, kr_sum, kr_high, qr_sum, qr_high, kn_high = (
            sem(n) for n in ("lat_low_ready", "kr_sum", "kr_high_ready", "qr_sum", "qr_high_ready", "kn_high_ready"))
        proj_done, qa_ready, kv_ready, q_turn, qr_ready, qn_ready = (
            sem(n) for n in ("proj_done", "qa_ready", "kv_ready", "q_turn", "qr_ready", "qn_ready"))
        s_done, m_ready, e_ready, p_ready, t_done, pT_ready, pv_done, sz_ready, oz_ready = (
            sem(n) for n in ("s_done", "m_ready", "e_ready", "p_ready", "t_done", "pT_ready", "pv_done", "sz_ready", "oz_ready"))
        oh_ready, ol_ready, yc_ready = sem("oh_ready"), sem("ol_ready"), sem("yc_ready")
        k2_raw, k2_turn, k2_rot, kd_ready, v2_ready = (sem(n) for n in ("k2_raw", "k2_turn", "k2_rot", "kd_ready", "v2_ready"))
        q2_raw, q2_turn, q2_ready, q2_sin, q2_cos = (sem(n) for n in ("q2_raw_ready", "q2_turn", "q2_ready", "q2_sin", "q2_cos"))
        s2_done, m2_ready, e2_ready, p2_ready, t2_done, p2T_ready, pv2_done, o2_high, o2_low = (
            sem(n) for n in ("s2_done", "m2_ready", "e2_ready", "p2_ready", "t2_done", "p2T_ready", "pv2_done", "o2_high_ready", "o2_low_ready"))
        out_done = sem("out_done")

        PF, n = {}, CREDIT
        for name in ("xb", "zu", "zb", "cu", "b", "gu0", "gu1"):
            PF[name] = n
            n += BASE[name].pairs
        PF["end"] = n
        SG, n = {}, 0
        for name, c in (("zu", 8), ("zb", 8), ("cu", 8), ("gu0", F_TILES), ("gu1", F_TILES)):
            SG[name] = n
            n += c

        def end_use(name, s):
            return BASE[name].use[s] + BASE[name].pairs

        def wait_y(eng, b, name, t):
            if t < T - 1:
                eng.wait_ge(y_ready, (T - 1) * b + t + 1)
            else:
                eng.wait_ge(used[1], end_use(name, 1))

        EARLY = ["cu", "gu0", "gu1", "dn0", "dn1"]
        SIDE = (4, 5, 6, 7, 0, 1, 5, 6)
        SHARED = ["gu0", "kv", "gu1"]
        BOUNDARY = ["eout", "oout", "aout", "dn0", "wo", "dn1"]
        TR = {"eout": 1, "oout": 2, "aout": 3, "dn0": 4, "q": 5, "wo": 6}

        block = ctx.enter_context(nc.Block())

        @block.sync
        def _(sp):
            w_in = {n: a[n].rearrange("(k p) n -> p k n", p=P) for n in (
                "e_w_in", "e_w_out", "o_w_in", "o_w_out", "a_w_in", "a_w_out", "w_kv", "b_w_q", "b_w_o")}
            ada_w = a["ada_w"].rearrange("l (k p) n -> l p k n", p=P)

            def load(name, i, s, pieces):
                B = BASE[name]
                assert len(pieces) == B.dmas[s]
                sp.wait_ge(raw_free[s], B.use[s] + i + CREDIT)
                for dst, src in pieces:
                    sp.dma_start(dst, src).then_inc(w_full[s], 16)

            def cols(s, w, c):
                v = raw[s][:, :].rearrange("p (k n) -> p k n", n=256)
                return [(v[:, j:j + K // 2, :], w[:, j:j + K // 2, bass.ds(c, 256)]) for j in (0, K // 2)]

            def twin(s, w, c, step):
                v = raw[s][:, :].rearrange("p (k two c) -> p k two c", two=2, c=P)
                return [(v[:, :, j, :], w[:, :, bass.ds(c + j * step, P)]) for j in range(2)]

            def deep(s, w, kt, n=2):
                c = n * D // 2
                return [(raw[s][:, j * c:(j + 1) * c], w[:, kt + j, :] if n == 2 else w[:, kt, j * c:(j + 1) * c]) for j in range(2)]

            def halves(s, w, kt, c):
                v = raw[s][:, :].rearrange("p (k n) -> p k n", n=S)
                return [(v[:, j:j + 2, :], w[:, kt + j:kt + j + 2, c:c + S]) for j in (0, 2)]

            for n, r, c in (("c", "c", 8), ("ada_b", "ada_b", 48)):
                sp.dma_start(rows[ROWS[r]:ROWS[r] + c, :], a[n].rearrange("a (m p) -> (a m) p", p=P)).then_inc(small_in, 16)
            sp.dma_start(small[:, :], a["k_small"]).then_inc(small_in, 16)
            for c in range(ADA_FIRST):
                sp.dma_start(ada_raw[c][:, :].rearrange("p (k n) -> p k n", n=256), ada_w[0][:, :, c * 256:(c + 1) * 256]).then_inc(ada_full[c], 16)
            load("v", 0, 0, halves(0, w_in["e_w_in"], 0, D))
            for t in range(T):
                sp.dma_start(x[:, t, :], a["x"][t * P:(t + 1) * P, :]).then_inc(x_in[t], 16)
            load("v", 0, 1, halves(1, w_in["e_w_in"], 4, D))
            for dst, src in ((g_bc, a["gmlp_norm_g"]), (b_bc, a["gmlp_norm_b"]), (bs_bc, a["gmlp_bs"])):
                sp.dma_start(dst, src.broadcast_to((P, src.shape[1]))).then_inc(aux_in, 16)
            sp.dma_start(sinks[:, :], a["b_sinks"].broadcast_to((P, 16))).then_inc(aux_in, 16)

            def ada_load(layer, pos, first):
                for m in range(2):
                    sp.wait_ge(ada_sum[m], pos + CREDIT)
                    sp.dma_start(ada_buf[m], ada_w[layer][:, :, bass.ds(pos * 256 + (first + m * P), P)]).then_inc(ada_land[m], 16)

            for c in (2, 3):
                load("v", c // 2, c % 2, halves(c % 2, w_in["e_w_in"], 4 * (c % 2), D + S * (c // 2)))
            sp.wait_ge(h_ready, T)
            with sp.Fori(0, 2) as i:
                for s in range(2):
                    load("xb", i, s, cols(s, w_in["e_w_in"], i * 512 + s * 256 + 3 * D))
                    ada_load(0, i * 2 + s, 2 * D)
            with sp.Fori(0, 4) as i:
                for s in range(2):
                    load("zu", i, s, twin(s, w_in["e_w_in"], i * 256 + s * P + 2 * D, -2 * D))
                    ada_load(1, i * 2 + (ADA_AT["zu"] + s), -ADA_AT["zu"] * 256)
            pool_w = a["pool_w"].rearrange("g (k p) e -> p (g k) e", p=P)
            for s in range(2):
                load("pool", 0, s, [(raw[s][:, j * 512:(j + 1) * 512].rearrange("p (k e) -> p k e", k=2),
                                     pool_w[:, 4 * s + 2 * j:4 * s + 2 * j + 2, :]) for j in range(2)])
            ada_load(1, ADA_AT["zb"], -ADA_AT["zu"] * 256)
            for c in range(-1, 2 * BASE["zb"].pairs):
                if c >= 1:
                    ada_load(1, ADA_AT["zb"] + c, -ADA_AT["zu"] * 256)
                if c + 1 < 2 * BASE["zb"].pairs:
                    load("zb", (c + 1) // 2, (c + 1) % 2, cols((c + 1) % 2, w_in["e_w_in"], (c + 1) * 256 + 4 * D))
            sp.wait_ge(sv_ready, K)
            for j, n in ((1, "ln_g"), (2, "ln_b")):
                sp.dma_start(gains[:, j, :], a[n][0:1, :].broadcast_to((P, D))).then_inc(gains_in, 16)
            with sp.Fori(0, 2) as i:
                for s in range(2):
                    load("eout", i, s, deep(s, w_in["e_w_out"], i * 4 + s * 2))
            sp.wait_ge(gate_low, 2 + GATED["b"])
            sp.dma_start(pos[:, :], a["positions"].broadcast_to((P, S))).then_inc(late_in, 16)
            with sp.Fori(2, 4) as i:
                for s in range(2):
                    load("eout", i, s, deep(s, w_in["e_w_out"], i * 4 + s * 2))
            for s in range(2):
                load("lat", 0, s, halves(s, w_in["o_w_in"], 4 * s, 0))
            sp.wait_ge(used[1], end_use("eout", 1))
            sp.dma_start(turn_m[:, :], a["k_turn_m"]).then_inc(late_in, 16)
            uq = a["mla_w_uq"].rearrange("(k p) h e -> p k h e", p=P)
            with sp.Fori(0, 8) as i:
                load("mla", i, 0, cols(0, w_in["o_w_in"], i * 256 + LATENT))
                load("mla", i, 1, [
                    *((raw[1][:, k * 256:(k + 1) * 256].rearrange("p (h e) -> p h e", h=2), uq[:, k, bass.ds(i * 2, 2), 0:NOPE]) for k in range(2)),
                    *((raw[1][:, 512 + k * P:512 + (k + 1) * P].rearrange("p (h e) -> p h e", h=2), uq[:, k, bass.ds(i * 2, 2), NOPE:]) for k in range(2)),
                    (raw[1][:, 768:1024].rearrange("p (h e) -> p h e", h=2), a["mla_w_uk"][:, bass.ds(i * 2, 2), :]),
                    (raw[1][:, 1024:1280].rearrange("p (h e) -> p h e", h=2), a["mla_w_uv"][:, bass.ds(i * 2, 2), :]),
                ])
            for s in range(2):
                load("oout", 0, s, deep(s, w_in["o_w_out"], s * 2))
            sp.wait_ge(oz_ready, HEADS + CREDIT)
            for j, src in ((1, a["ln_g"][1:2, :]), (2, a["ln_b"][1:2, :]), (3, a["a_pre"])):
                sp.dma_start(gains[:, j, :], src.broadcast_to((P, D))).then_inc(gains_in, 16)
            with sp.Fori(1, 4) as i:
                for s in range(2):
                    load("oout", i, s, deep(s, w_in["o_w_out"], i * 4 + s * 2))
            with sp.Fori(0, 4) as i:
                for s in range(2):
                    load("cu", i, s, twin(s, w_in["a_w_in"], i * 256 + s * P + D, D))
            with sp.Fori(0, 2) as i:
                for s in range(2):
                    load("b", i, s, cols(s, w_in["a_w_in"], i * 512 + s * 256))
            sp.wait_ge(h_ready, 3 * T)
            for j, src in ((0, a["a_post"]), (1, a["f_pre"][0:1, :])):
                sp.dma_start(gains[:, j, :], src.broadcast_to((P, D))).then_inc(gains_in, 16)
            with sp.Fori(0, 2) as i:
                for s in range(2):
                    load("aout", i, s, deep(s, w_in["a_w_out"], i * 4 + s * 2))

            def ffn(layer):
                gu, dn = f"gu{layer}", f"dn{layer}"
                w_gu = a["f_gate_up"][layer].rearrange("(k p) n -> p k n", p=P)
                w_dn = a["f_down"][layer].rearrange("(k p) n -> p k n", p=P)
                with sp.Fori(0, 11) as i:
                    for s in range(2):
                        load(gu, i, s, twin(s, w_gu, i * 256 + s * P, D_FF))
                if layer == 0:
                    sp.wait_ge(h_ready, 4 * T)
                    new = ((0, a["f_post"][0:1, :]), (1, a["kv_norm"]), (2, a["b_pre"]))
                else:
                    sp.wait_ge(h_ready, 7 * T)
                    new = ((0, a["f_post"][1:2, :]),)
                for j, src in new:
                    sp.dma_start(gains[:, j, :], src.broadcast_to((P, D))).then_inc(gains_in, 16)
                for s in range(2):
                    load(dn, 0, s, deep(s, w_dn, s, 1))
                with sp.Fori(1, 6) as i:
                    for s in range(2):
                        load(dn, i, s, deep(s, w_dn, i * 4 + (s * 2 - 2)))

            ffn(0)
            for s in range(2):
                load("kv", 0, s, cols(s, w_in["w_kv"], (1 - s) * 256))
            sp.wait_ge(used[1], end_use("dn0", 1))
            sp.dma_start(swa[:, :], a["k_swa"]).then_inc(late_in, 16)
            with sp.Fori(0, 2) as i:
                for s in range(2):
                    load("q", i, s, cols(s, w_in["b_w_q"], i * 512 + s * 256))
            sp.wait_ge(h_ready, 6 * T)
            for j, src in ((0, a["b_post"]), (1, a["f_pre"][1:2, :])):
                sp.dma_start(gains[:, j, :], src.broadcast_to((P, D))).then_inc(gains_in, 16)
            with sp.Fori(0, 2) as i:
                for s in range(2):
                    load("wo", i, s, deep(s, w_in["b_w_o"], i * 4 + s * 2))
            ffn(1)
            out_v = out.rearrange("(t p) d -> p t d", p=P)
            for t in range(T):
                sp.wait_ge(x_ready, 5 * T + t + 1)
                sp.dma_start(out_v[:, t, :], x[:, t, :]).then_inc(out_done, 16)
            sp.wait_ge(out_done, 16 * T)

        @block.gpsimd
        def _(pool):
            nc.gpsimd.memset(eps[:, 0:1], LN_EPS)
            nc.gpsimd.memset(eps[:, 1:2], EPS2).then_inc(pool_ready, 1)
            for s in range(2):
                pool.sem_inc(raw_free[s], CREDIT)
                pool.sem_inc(pair_free[s], CREDIT)
            pool.sem_inc(gate_low, 2)
            pool.sem_inc(oz_ready, CREDIT)
            pool.sem_inc(sz_ready, CREDIT)
            for m in range(2):
                pool.sem_inc(ada_sum[m], CREDIT)

            def turn_queries(g):
                dst = q2[g % 2][:, :, :]
                pool.wait_ge(q2_raw, g + 1)
                nc.gpsimd.tensor_tensor(dst, q2raw[:, :, :], cosB.unsqueeze(1).broadcast_to((P, 2, S)), ALU.mult).then_inc(q2_cos, 1)
                pool.wait_ge(q2_cos, g)
                pool.wait_ge(q2_sin, g)
                nc.gpsimd.tensor_tensor(dst, dst, q2tmp[:, :, :], ALU.add).then_inc(q2_ready, 1)

            for name, pairs, _ in RING:
                B = BASE[name]
                if name == "mla":
                    pool.wait_ge(gains_in, 32)
                    for t in range(T):
                        pool.wait_ge(tr_done, T * TR["eout"] + t + 1)
                        nc.gpsimd.tensor_tensor(x[:, t, :], x[:, t, :], gains[:, 1, :], ALU.mult).then_inc(pool_step, 1)
                        pool.wait_ge(pool_step, t + 1)
                        nc.gpsimd.tensor_tensor(x[:, t, :], x[:, t, :], gains[:, 2, :], ALU.add).then_inc(x_ready, 1)

                def low(i, s, n=CHUNK):
                    pool.wait_ge(w_high[s], B.split[s] + i + 1)
                    nc.gpsimd.tensor_tensor(WL[s][:, 0:n], raw[s][:, 0:n], WH[s][:, 0:n].bitcast(F32), ALU.subtract).then_inc(w_split[s], 1)
                    pool.wait_ge(w_split[s], B.split[s] + i + 1)
                    pool.sem_inc(raw_free[s], 1)

                first, last = 0, pairs - (name in BOUNDARY)
                if name in SHARED:
                    low(0, 0)
                    pool.wait_ge(w_high[1], B.split[1] + 1)
                    h = CHUNK // 2
                    nc.gpsimd.tensor_tensor(WL[1][:, h:], raw[1][:, h:], WH[1][:, h:].bitcast(F32), ALU.subtract).then_inc(pool_half, 1)
                    pool.wait_ge(pool_half, SHARED.index(name) + 1)
                    pool.wait_ge(dve_half, SHARED.index(name) + 1)
                    pool.sem_inc(w_split[1], 1)
                    pool.sem_inc(raw_free[1], 1)
                    first = 1
                if name in SHARED and name in EARLY:
                    low(1, 1)
                    first = 2
                elif name in EARLY:
                    for s in range(2):
                        low(0, s, D if name in ("dn0", "dn1") else CHUNK)
                    low(1, 1)
                    first = 2
                if name == "q":
                    low(0, 0)
                    low(0, 1)
                    low(1, 0)
                    turn_queries(1)
                    low(1, 1)
                    turn_queries(2)
                    continue
                if name == "zu":
                    first = 2
                    for i in range(2):
                        for s in range(2):
                            low(i, s)
                    pool.wait_ge(pool_high, 1)
                    nc.gpsimd.tensor_tensor(poolL[:, :, :], pooled[:, :, :], poolH[:, :, :].bitcast(F32), ALU.subtract).then_inc(pool_low, 1)
                if name == "oout":
                    first = 1
                    low(0, 1)
                if name == "wo":
                    first = 1
                    low(0, 0)
                    turn_queries(3)
                    low(0, 1)
                if last > first:
                    with pool.Fori(first, last) as i:
                        for s in (1, 0) if name == "mla" else (0, 1):
                            low(i, s, MLA_CHUNK if name == "mla" and s else CHUNK)
                if name in BOUNDARY:
                    low(pairs - 1, 0)

        @block.scalar
        def _(act):
            steps = Steps(act, act_step)
            nact = nc.scalar.activation

            def split_high(name, i, s):
                B = BASE[name]
                act.wait_ge(w_full[s], B.full[s] + (i + 1) * (16 * B.dmas[s]))
                if name != "v" or i:
                    act.wait_ge(used[s], B.use[s] + i)
                n = MLA_CHUNK if name == "mla" and s else CHUNK
                nact(WH[s][:, 0:n], raw[s][:, 0:n], ACT.Copy).then_inc(w_high[s], 1)

            for n, c in (("pool_b", 8), ("pool_scale", 8), ("q_g", 2), ("kv_g", 1), ("conv", 24)):
                act.dma_start(rows[ROWS[n]:ROWS[n] + c, :], a[n].rearrange("a (m p) -> (a m) p", p=P)).then_inc(rest_in, 16)
            for n in ("ln_g", "ln_b"):
                act.dma_start(rows[ROWS[n]:ROWS[n] + K, :], a[n][0:1, :].rearrange("a (m p) -> (a m) p", p=P)).then_inc(rest_in, 16)
            act.dma_start(ws_sb, a["gmlp_ws"].rearrange("h t s -> t h s")).then_inc(rest_in, 16)
            act.wait_ge(vec_ready, 1)
            nact(csil[:, :], vec[:, ROWS["c"]:ROWS["c"] + K], ACT.Silu).then_inc(csil_ready, 1)

            def gate_rows(n, b):
                act.wait_ge(gate_mm, n)
                nact(gains[:, 0, :], flat2(b), ACT.Copy).then_inc(gate_ready, 1)

            def modulate(layer, q, t, tmp):
                act.wait_ge(tr_done, T * q + t + 1)
                if t >= 2:
                    act.wait_ge(h_ready, T * q + t - 1)
                for k in range(K // 2):
                    c = 24 * layer + k
                    ins = nact(tmp[:, k * P:(k + 1) * P], two(2 * t)[:, k, :], ACT.Identity,
                               scale=mod[:, c + K:c + K + 1], bias=mod[:, c:c + 1])
                steps.link(ins)
                act.wait_ge(mod_half, T * layer + t + 1)
                nact(tile(hH, t), tmp.rearrange("p (k t) -> p k t", t=P), ACT.Copy).then_inc(h_high, 1)

            split_high("v", 0, 0)
            act.wait_ge(mod_ready, 1)
            for t in range(T):
                if t == T - 1:
                    split_high("v", 0, 1)
                modulate(0, 0, t, gains[:, 3 * (1 - t % 2), :])

            act.wait_ge(pool_ready, 1)
            for n in range(2):
                for s in range(2):
                    split_high("v", n + 1, s)
                act.wait_ge(lnv_stat, n + 1)
                nact(stat[:, :, 0:2].rearrange("p a b -> p a b"), mv[:, :, 1].rearrange("p (a b) -> p a b", b=2), ACT.Sqrt, bias=eps[:, 0:1]).then_inc(lnv_sqrt, 1)

            def gated(name, highs, fn):
                B = BASE[name]
                with act.Fori(0, B.pairs) as i:
                    for s in range(2):
                        f = i * 2 + s
                        split_high(name, i + 1, s)
                        act.wait_ge(gate_low, GATED[name] + f + 1)
                        nact(buf[s][:, :], PS[:, 2 * s, :], fn).then_inc(sg_ready, 1)
                        act.wait_ge(prod_ready, GATED[name] + f + 1)
                        nact(highs[:, f, :], buf[s][:, :], ACT.Copy).then_inc(act_high, 1)

            for c in range(2 * BASE["xb"].pairs):
                split_high("xb", c // 2 + 1, c % 2)
                for m in range(2):
                    f = 2 * c + m
                    if f >= 2:
                        act.wait_ge(pooled_ready, f - 1)
                    nact(xbufs[m][:, PAD:], PS[:, 2 * (c % 2) + m, :], ACT.Copy).then_inc(xb_ready, 1)
            act.wait_ge(sp_done, K)
            act.wait_ge(pooled_ready, K)
            nact(poolH[:, :, :], pooled[:, :, :], ACT.Copy).then_inc(pool_high, 1)
            gated("zu", mixH, ACT.Silu)
            for s in range(2):
                split_high("pool", 1, s)
            B = BASE["zb"]
            with act.Fori(0, 2) as i:
                for s in range(2):
                    act.wait_ge(used[s], B.use[s] + i + 1)
                    for m in range(2):
                        f = i * 4 + (2 * s + m)
                        act.wait_ge(gate_low, GATED["zb"] + f + 1)
                        nact(buf[m][:, :], PS[:, 2 * s + m, :], ACT.Silu).then_inc(sg_ready, 1)
                    split_high("zb", i + 1, s)
                    for m in range(2):
                        f = i * 4 + (2 * s + m)
                        act.wait_ge(prod_ready, GATED["zb"] + f + 1)
                        nact(mixH[:, f + K, :], buf[m][:, :], ACT.Copy).then_inc(act_high, 1)
            act.wait_ge(ada_sum[0], ADA_END + CREDIT)
            gate_rows(1, 6)

            def highs_of(name):
                for c in range(2 * (BASE[name].pairs - 1)):
                    split_high(name, c // 2 + 1, c % 2)

            def root(t, c, scale, e):
                nact(stat[:, t, c + 1:c + 2], stat[:, t, c:c + 1], ACT.Sqrt, bias=eps[:, e:e + 1], scale=scale).then_inc(sqrt_ready, 1)

            def high_tile(q, t, b):
                act.wait_ge(tr_done, T * q + t + 1)
                nact(tile(hH, t), two(b), ACT.Copy).then_inc(h_high, 1)

            def square_x(n, t):
                act.wait_ge(x_ready, n)
                nblk = x[:, t, :].rearrange("p (k t) -> p k t", t=P)
                steps.link(nact(tile(hH, t), nblk, ACT.Square, accum_out=stat[:, t, 3:4]))
                root(t, 3, 1.0 / D, 1)

            def ln_root(b, t):
                act.wait_ge(ln_stat, T * b + t + 1)
                blocks = x[:, t, :].rearrange("p (k t) -> p k t", t=P)
                steps.link(nact(tile(hH, t), blocks, ACT.Square, scale=-1.0, bias=mv[:, t, 0:1], accum_out=stat[:, t, 0:1]))
                root(t, 0, 1.0 / D, 0)

            def load_sqrt():
                nact(stat[:, 0, 7:8], eps[:, 0:1], ACT.Sqrt)

            highs_of("eout")
            load_sqrt()
            tmps = [gains[:, 3, :], mod_tmp]
            ln_root(0, 0)
            ln_root(0, 1)
            split_high("lat", 0, 0)
            modulate(1, TR["eout"], 0, tmps[0])
            split_high("lat", 0, 1)
            modulate(1, TR["eout"], 1, tmps[1])
            ln_root(0, 2)
            ln_root(0, 3)
            modulate(1, TR["eout"], 2, tmps[0])
            act.wait_ge(rest_ready, 1)
            act.wait_ge(used[1], end_use("eout", 1))
            nact(sinM[:, :], rest[:, :], ACT.Sin)
            nact(cosM[:, :], turns[:, :], ACT.Sin).then_inc(sin_ready, 1)
            modulate(1, TR["eout"], 3, tmps[1])

            for t in range(T):
                if t < T - 1:
                    act.wait_ge(lat_done, t + 1)
                else:
                    act.wait_ge(used[1], end_use("lat", 1))
                nact(latn[:, t, 0:QR], PS[:, t, 0:QR], ACT.Square, accum_out=stat[:, t, 0:1])
                steps.link(nact(latn[:, t, QR:QR + KVR], PS[:, t, QR:QR + KVR], ACT.Square, accum_out=stat[:, t, 1:2]))
                nact(stat[:, t, 2:3], stat[:, t, 0:1], ACT.Sqrt, bias=eps[:, 0:1], scale=1.0 / QR)
                nact(stat[:, t, 3:4], stat[:, t, 1:2], ACT.Sqrt, bias=eps[:, 0:1], scale=1.0 / KVR).then_inc(lat_sqrt, 1)
            split_high("mla", 0, 1)
            act.wait_ge(lat_tr, 1)
            for j in range(2):
                nact(qcH[:, j, :], PS[:, 4 + j, :], ACT.Copy, scale=vec[:, ROWS["q_g"] + j:ROWS["q_g"] + j + 1]).then_inc(lat_ev, 1)
            nact(kraw[:, :], PS[:, 7, :], ACT.Copy).then_inc(lat_ev, 1)
            nact(kvH[:, :], PS[:, 6, :], ACT.Copy, scale=vec[:, ROWS["kv_g"]:ROWS["kv_g"] + 1]).then_inc(lat_ev, 1)
            gate_rows(2, 2)
            split_high("mla", 0, 0)
            act.wait_ge(kr_sum, 1)
            nact(krH[:, :], kr[:, :], ACT.Copy).then_inc(kr_high, 1)

            B = BASE["mla"]

            def high_o(h):
                nact(oH[:, h, :], oz[:, h, :], ACT.Copy).then_inc(oh_ready, 1)

            def attend(i, more):
                act.wait_ge(proj_done, i * 4 + 1)
                nact(qnH[:, :, :], PS[:, 0:2, :], ACT.Copy).then_inc(qa_ready, 1)
                act.wait_ge(proj_done, i * 4 + 2)
                nact(qraw[:, :], PS[:, 2, :], ACT.Copy).then_inc(qa_ready, 1)
                act.wait_ge(proj_done, i * 4 + 3)
                nact(knH[:, :, :], PS[:, 4:6, :], ACT.Copy).then_inc(kn_high, 1)
                act.wait_ge(qr_sum, i + 1)
                nact(qrH[:, :], qr[:, :], ACT.Copy).then_inc(qr_high, 1)

                def weigh(u):
                    w = (u % T + 1) * P
                    act.wait_ge(m_ready, i * 8 + u + 1)
                    nact(pm[u % 2][:, 0:w], PS[:, 2 + u % 2, 0:w], ACT.Exp, scale=MLA_SCALE, bias=soft[:, u % 2, 1, 0:1],
                         accum_out=soft[:, u % 2, 2, 0:1]).then_inc(e_ready, 1)

                def turned(u):
                    q = u % T
                    act.wait_ge(t_done, i * 8 + u + 1)
                    nact(pT[u // T][:, 0:q + 1, q * P:(q + 1) * P],
                         PS[:, 4 + u % 2, 0:(q + 1) * P].rearrange("p (k t) -> p k t", t=P), ACT.Copy).then_inc(pT_ready, 1)

                weigh(0)
                weigh(1)
                for u in range(8):
                    turned(u)
                    if u + 2 < 8:
                        weigh(u + 2)
                    if u == T and more:
                        split_high("mla", i + 1, 1)
                act.wait_ge(used[0], B.use[0] + i + 1)
                if not more:
                    split_high("mla", i + 1, 0)
                    high_o(0)
                    high_o(1)
                nact(oz[:, bass.ds(i * 2, 2), :], PS[:, 0:2, :], ACT.Silu).then_inc(sz_ready, 1)
                if more:
                    split_high("mla", i + 1, 0)

            with act.Fori(0, 7) as i:
                attend(i, True)
            attend(7, False)

            split_high("oout", 0, 1)
            act.wait_ge(oz_ready, HEADS + CREDIT)
            for h in range(2, HEADS):
                high_o(h)
            highs_of("oout")
            load_sqrt()
            q = TR["oout"]
            ln_root(1, 0)
            ln_root(1, 1)
            square_x(T + 1, 0)
            split_high("cu", 0, 0)
            square_x(T + 2, 1)
            high_tile(q, 0, 0)
            high_tile(q, 1, 2)
            ln_root(1, 2)
            split_high("cu", 0, 1)
            square_x(T + 3, 2)
            ln_root(1, 3)
            square_x(T + 4, 3)
            high_tile(q, 2, 4)
            high_tile(q, 3, 6)

            B = BASE["cu"]
            with act.Fori(0, 4) as i:
                for s in range(2):
                    split_high("cu", i + 1, s)
                    act.wait_ge(pair_free[s], i + PF["cu"])
                    nact(buf[s][:, :], PS[:, 2 * s, :], ACT.Copy).then_inc(sg_ready, 1)
            with act.Fori(0, 2) as i:
                for s in range(2):
                    split_high("b", i + 1, s)
                    for m in range(2):
                        f = i * 4 + (2 * s + m)
                        act.wait_ge(prod_ready, GATED["b"] + f + 1)
                        nact(yH[:, f, :], buf[m][:, :], ACT.Copy).then_inc(act_high, 1)

            def boundary(name, pre):
                b, pairs = BOUNDARY.index(name), BASE[name].pairs

                def square_y(t):
                    wait_y(act, b, name, t)
                    steps.link(nact(tile(hH, t), two(2 * t), ACT.Square, accum_out=stat[:, t, 0:1]))
                    root(t, 0, 1.0 / D, 1)

                highs_of(name)
                load_sqrt()
                if not pre:
                    for t in range(T):
                        square_y(t)
                    return
                q = TR[name]
                square_y(0)
                square_y(1)
                square_x(T * b + 1, 0)
                square_x(T * b + 2, 1)
                split_high(name, pairs, 0)
                square_y(2)
                high_tile(q, 0, 0)
                high_tile(q, 1, 2)
                square_y(3)
                split_high(name, pairs, 1)
                square_x(T * b + 3, 2)
                square_x(T * b + 4, 3)
                high_tile(q, 2, 4)
                high_tile(q, 3, 6)

            boundary("aout", True)
            gated("gu0", fH, ACT.Silu)
            boundary("dn0", True)

            split_high("kv", 1, 0)
            high_tile(TR["q"], 0, 4)
            high_tile(TR["q"], 1, 6)
            act.wait_ge(used[1], end_use("kv", 1))
            nact(q2raw[:, :, :], PS[:, 2:4, :], ACT.Copy).then_inc(k2_raw, 1)
            split_high("kv", 1, 1)
            for t in (2, 3):
                high_tile(TR["q"], t, 2 * t)
            act.wait_ge(k2_rot, 1)
            for g in range(KVH):
                src = q2[1][(g % 2) * HD:(g % 2 + 1) * HD, g // 2, :]
                for j in range(2):
                    ins = nact(kdup[j * HD:(j + 1) * HD, g, :], src, ACT.Copy)
            ins.then_inc(kd_ready, 1)

            def raw_queries(g):
                act.wait_ge(used[g % 2], BASE["q"].use[g % 2] + g // 2 + 1)
                if g == 1:
                    act.wait_ge(kd_ready, 1)
                act.wait_ge(q2_ready, g) if g else act.wait_ge(k2_rot, 1)
                nact(q2raw[:, :, :], PS[:, 0:2, :], ACT.Copy).then_inc(q2_raw, 1)

            def weigh2(n):
                w = 0 if n % T else P
                st, pr = soft[:, n % 2, :, :], p2[n % 3]
                act.wait_ge(m2_ready, n + 1)
                nact(st[:, 4, :], st[:, 3, :], ACT.Exp)
                for h in range(GROUP):
                    ins = nact(pr[:, h, w:], pr[:, h, w:], ACT.Exp, scale=SW_SCALE, bias=st[:, 2, h:h + 1], accum_out=st[:, 5, h:h + 1])
                ins.then_inc(e2_ready, 1)

            def turned2(n):
                act.wait_ge(t2_done, n + 1)
                if n >= 2:
                    act.wait_ge(pv2_done, n - 1)
                j, st = (0, 1) if n % T else (1, 2)
                nact(p2T[n % 2][:, j::st, :], two(4)[:, j::st, :], ACT.Copy).then_inc(p2T_ready, 1)

            def high_out(g):
                act.wait_ge(pv2_done, T * (g + 1))
                for j in range(2):
                    nact(o2H[:, g * 2 + j, :], PS[:, 6 + j, :], ACT.Copy).then_inc(o2_high, 1)

            raw_queries(0)
            split_high("q", 1, 0)
            weigh2(0)
            for n in range(UNITS):
                g, b = n // T, n % T
                if b == 0 and g + 1 < KVH:
                    raw_queries(g + 1)
                if n + 1 < UNITS:
                    weigh2(n + 1)
                turned2(n)
                if b == 0 and g:
                    high_out(g - 1)
                if b == 1 and g + 1 < KVH:
                    split_high("q", (g + 1) // 2 + 1, (g + 1) % 2)
            high_out(KVH - 1)
            boundary("wo", True)
            gated("gu1", fH, ACT.Silu)
            boundary("dn1", False)

        @block.vector
        def _(dve):
            steps = Steps(dve, dve_step)
            v = nc.vector

            dve.wait_ge(rows_tr, 1)
            steps.link(v.tensor_copy(vec[:, 0:N_FIRST], PS[:, 7, 0:N_FIRST]))
            for layer in range(DEPTH):
                c = slice(24 * layer + K, 24 * layer + 24)
                ins = v.tensor_scalar(vec[:, c], vec[:, c], 1.0, None, ALU.add)
            ins.then_inc(vec_ready, 1)
            dve.wait_ge(csil_ready, 1)
            for c in range(ADA_FIRST):
                dve.wait_ge(ada_full[c], 16)
                w = ada_raw[c][:, :].rearrange("p (k n) -> p k n", n=256)
                for k in range(K):
                    dst, ck = ada_part[c][:, k % 2, :], csil[:, k:k + 1]
                    if k < 2:
                        ins = v.tensor_scalar(dst, w[:, k, :], ck, None, ALU.mult)
                    else:
                        dve.wait_ge(ada_first, K * c + k - 1)
                        ins = v.scalar_tensor_tensor(dst, w[:, k, :], ck, dst, ALU.mult, ALU.add)
                    ins.then_inc(ada_first, 1)
            dve.wait_ge(vec_ready, 1)
            dve.wait_ge(ada_done, 1)
            v.tensor_tensor(mod[:, 0:2 * K], PS[:, 7, 256:256 + 2 * K], vec[:, 0:2 * K], ALU.add).then_inc(mod_ready, 1)

            def ada_terms(pos):
                for m in range(2):
                    dve.wait_ge(ada_land[m], pos * 16 + 16)
                    v.tensor_tensor(ada_buf[m], ada_buf[m], csil[:, :].unsqueeze(2).broadcast_to((P, K, P)), ALU.mult).then_inc(ada_prod[m], 1)
                for m in range(2):
                    dve.wait_ge(ada_prod[m], pos + 1)
                    v.reduce_sum(ada_acc[m][:, :], ada_buf[m].rearrange("p k n -> p n k"), AX).then_inc(ada_sum[m], 1)

            def ada_keep(pos, s):
                c = pos * 2 + 2 * K
                v.tensor_tensor(mod[:, bass.ds(c, 2)], PS[:, 4, 2 * s:2 * s + 2], vec[:, bass.ds(c, 2)], ALU.add).then_inc(ada_col, 1)

            def gate_diag(layer, one, dg):
                v.memset(one[:, :], 1.0)
                for k in range(K):
                    c = 24 * layer + 2 * K + k
                    ins = v.tensor_scalar(dg[:, k, :], ident, mod[:, c:c + 1], None, ALU.mult)
                ins.then_inc(diag_ready, 1)

            def mod_rest(layer, q, t, tmp):
                dve.wait_ge(tr_done, T * q + t + 1)
                if t >= 2:
                    dve.wait_ge(h_ready, T * q + t - 1)
                for k in range(K // 2, K):
                    c = 24 * layer + k
                    ins = v.tensor_scalar(tmp[:, k * P:(k + 1) * P], two(2 * t)[:, k, :], mod[:, c + K:c + K + 1], mod[:, c:c + 1],
                                          ALU.mult, ALU.add)
                ins.then_inc(mod_half, 1)

            def low_mod(q, t, tmp):
                dve.wait_ge(h_high, T * q + t + 1)
                v.tensor_tensor(tile(hL, t), tmp.rearrange("p (k t) -> p k t", t=P), tile(hH, t).bitcast(F32),
                                ALU.subtract).then_inc(h_ready, 1)

            dve.wait_ge(mod_ready, 1)
            for t in range(T):
                mod_rest(0, 0, t, gains[:, 3 * (1 - t % 2), :])
                if t:
                    low_mod(0, t - 1, gains[:, 3 * (t % 2), :])
            low_mod(0, T - 1, gains[:, 3 * (T % 2), :])

            dve.wait_ge(aux_in, 16 * 4)
            for n in range(2):
                if n:
                    ada_terms(0)
                else:
                    dve.wait_ge(rows_tr, 2)
                    steps.link(v.tensor_copy(vec[:, N_FIRST:], PS[:, 7, N_FIRST:N_ROWS]))
                    dve.wait_ge(ws_tr, 1)
                    steps.link(v.tensor_copy(wT, PS[:, 6, :].rearrange("p (h t) -> p h t", t=P)))
                    v.memset(wT[G_HALF:P, :, 0:G_HALF], 0.0).then_inc(wT_ready, 1)
                dve.wait_ge(used[1], BASE["v"].use[1] + n + 1)
                for t in range(T):
                    for h in range(2):
                        ins = v.bn_stats(bn[:, 2 * t + h, :], PS[:, 4 * n + t, h * G_DIM:(h + 1) * G_DIM])
                steps.link(ins)
                for j in range(8):
                    ins = v.bn_aggr(mv[:, j, :], bn[:, j, :])
                ins.then_inc(lnv_stat, 1)
                dve.wait_ge(lnv_sqrt, n + 1)
                steps.link(v.reciprocal(stat[:, :, 2:4], stat[:, :, 0:2]))
                for t in range(T):
                    for h in range(2):
                        c = n * S + h * G_DIM
                        ins = v.tensor_scalar(vn[:, t, c:c + G_DIM], PS[:, 4 * n + t, h * G_DIM:(h + 1) * G_DIM],
                                              mv[:, 2 * t + h, 0:1], stat[:, t, 2 + h:3 + h], ALU.subtract, ALU.mult)
                steps.link(ins)
                dve.sem_inc(v_left, 1)
                for h in range(2):
                    c = n * S + h * G_DIM
                    blk = vn[:, :, c:c + G_DIM]
                    steps.link(v.tensor_tensor(blk, blk, g_bc.unsqueeze(1).broadcast_to((P, T, G_DIM)), ALU.mult))
                    ins = v.tensor_tensor(blk, blk, b_bc.unsqueeze(1).broadcast_to((P, T, G_DIM)), ALU.add)
                ins.then_inc(vn_ready, 1)

            def spatial_bias():
                for f in range(K):
                    dve.wait_ge(sp_done, f + 1)
                    h = f // 2
                    v.tensor_tensor(sv[:, f, :].rearrange("p (b t) -> p b t", t=P), PS[:, SIDE[f], :].rearrange("p (b t) -> p b t", t=P),
                                    bs_bc[:, h * P:(h + 1) * P].unsqueeze(1).broadcast_to((P, T, P)), ALU.add).then_inc(sv_ready, 1)

            for z in (*xbufs, sum_a, sum_b):
                ins = v.memset(z[:, 0:PAD], 0.0)
            steps.link(ins)
            for c in range(2 * BASE["xb"].pairs):
                dve.wait_ge(used[c % 2], BASE["xb"].use[c % 2] + c // 2 + 1)
                ada_keep(c, c % 2)
                ada_terms(c + 1)
                if c == 2 * BASE["xb"].pairs - 1:
                    spatial_bias()
                for f in (2 * c, 2 * c + 1):
                    g = f // 2
                    win = POOL_WINDOWS[g]
                    dve.wait_ge(xb_ready, f + 1)
                    if f % 2:
                        dve.sem_inc(pair_free[g % 2], 1)
                    xbuf = xbufs[f % 2]
                    cur, step, nxt = xbuf, 1, [sum_a, sum_b]
                    while step < win:
                        dst = nxt[0]
                        nxt.reverse()
                        steps.link(v.tensor_tensor(dst[:, PAD:], cur[:, PAD:], cur[:, PAD - step:PAD + S - step], ALU.add))
                        cur, step = dst, 2 * step
                    steps.link(v.scalar_tensor_tensor(pooled[:, f, :], cur[:, PAD:], 1.0 / win, xbuf[:, PAD:], ALU.mult, ALU.subtract))
                    head = pooled[:, f, 0:PAD]
                    steps.link(v.tensor_tensor(head, cur[:, PAD:2 * PAD], inv_count[:, g * PAD:(g + 1) * PAD], ALU.mult))
                    v.tensor_tensor(head, head, xbuf[:, PAD:2 * PAD], ALU.subtract).then_inc(pooled_ready, 1)
            dve.wait_ge(pooled_ready, K)
            dve.wait_ge(sv_ready, K)

            def gated(name, lows, factor=None):
                B = BASE[name]
                with dve.Fori(0, B.pairs) as i:
                    for s in range(2):
                        f = i * 2 + s
                        if name in ADA_AT:
                            dve.wait_ge(used[s], B.use[s] + i + 1)
                            ada_keep(f + ADA_AT[name], s)
                            ada_terms(f + (ADA_AT[name] + 1))
                        dve.wait_ge(sg_ready, SG[name] + f + 1)
                        if factor is None:
                            v.tensor_tensor(buf[s][:, :], buf[s][:, :], PS[:, 2 * s + 1, :], ALU.mult).then_inc(prod_ready, 1)
                            dve.wait_ge(prod_ready, GATED[name] + f + 1)
                            dve.sem_inc(pair_free[s], 1)
                        else:
                            v.tensor_tensor(buf[s][:, :], buf[s][:, :], PS[:, 2 * s + 1, :], ALU.mult).then_inc(pair_free[s], 1)
                            dve.wait_ge(pair_free[s], PF[name] + i + 1)
                            v.tensor_tensor(buf[s][:, :], buf[s][:, :], factor[:, f, :], ALU.mult).then_inc(prod_ready, 1)
                            dve.wait_ge(prod_ready, GATED[name] + f + 1)
                        dve.wait_ge(act_high, GATED[name] + f + 1)
                        v.tensor_tensor(lows[:, f, :], buf[s][:, :], highs_of[name][:, f, :].bitcast(F32), ALU.subtract).then_inc(gate_low, 1)

            highs_of = {"zu": mixH, "gu0": fH, "gu1": fH}
            gated("zu", mixL, sv)

            for f in range(K):
                if f % 4 < 3:
                    dve.wait_ge(py_done, 3 * (f // 4) + f % 4 + 1)
                else:
                    dve.wait_ge(used[f // 4], BASE["pool"].use[f // 4] + 1)
                v.tensor_scalar(sv[:, f, :], PS[:, SIDE[f], :], vec[:, ROWS["pool_b"] + f:ROWS["pool_b"] + f + 1],
                                vec[:, ROWS["pool_scale"] + f:ROWS["pool_scale"] + f + 1], ALU.add, ALU.mult).then_inc(yb_ready, 1)
            dve.wait_ge(yb_ready, K)
            gate_diag(0, ones, diag)
            B = BASE["zb"]
            for c in range(2 * B.pairs):
                s = c % 2
                dve.wait_ge(used[s], B.use[s] + c // 2 + 1)
                ada_keep(ADA_AT["zb"] + c, s)
                if c + 1 < 2 * B.pairs:
                    ada_terms(ADA_AT["zb"] + c + 1)
                for m in range(2):
                    f = 2 * c + m
                    dve.wait_ge(sg_ready, SG["zb"] + f + 1)
                    if m:
                        dve.sem_inc(pair_free[s], 1)
                    v.tensor_tensor(buf[m][:, :], buf[m][:, :], sv[:, f, :], ALU.mult).then_inc(prod_ready, 1)
                for m in range(2):
                    f = 2 * c + m
                    dve.wait_ge(act_high, GATED["zb"] + f + 1)
                    v.tensor_tensor(mixL[:, f + K, :], buf[m][:, :], mixH[:, f + K, :].bitcast(F32), ALU.subtract).then_inc(gate_low, 1)

            def split_low(name, j, s):
                n = BASE[name].split[s] + j + 1
                dve.wait_ge(w_high[s], n)
                v.tensor_tensor(WL[s][:, :], raw[s][:, :], WH[s][:, :].bitcast(F32), ALU.subtract).then_inc(w_split[s], 1)
                dve.wait_ge(w_split[s], n)
                dve.sem_inc(raw_free[s], 1)

            def split_half(name):
                h = CHUNK // 2
                dve.wait_ge(w_high[1], BASE[name].split[1] + 1)
                v.tensor_tensor(WL[1][:, 0:h], raw[1][:, 0:h], WH[1][:, 0:h].bitcast(F32), ALU.subtract).then_inc(dve_half, 1)

            def split_last(name):
                split_low(name, BASE[name].pairs - 1, 1)

            tmps = [gains[:, 3, :], mod_tmp]
            dve.wait_ge(ada_col, ADA_END)
            g_col, b_col = (vec[:, ROWS[n]:ROWS[n] + K] for n in ("ln_g", "ln_b"))
            steps.link(v.tensor_tensor(b_col, b_col, mod[:, 24 + K:24 + 2 * K], ALU.mult))
            steps.link(v.tensor_tensor(mod[:, 24:24 + K], mod[:, 24:24 + K], b_col, ALU.add))
            steps.link(v.tensor_tensor(mod[:, 24 + K:24 + 2 * K], mod[:, 24 + K:24 + 2 * K], g_col, ALU.mult))

            dve.wait_ge(late_in, 16)
            steps.link(v.tensor_copy(ang[:, :], pos[:, :]))
            steps.link(v.tensor_scalar(ang[:, :], ang[:, :], freq, None, ALU.mult))
            steps.link(v.tensor_scalar(turns[:, :], ang[:, :], 1.0 / TWO_PI, ROUND, ALU.mult, ALU.add))
            steps.link(v.tensor_scalar(turns[:, :], turns[:, :], ROUND, None, ALU.subtract))
            steps.link(v.scalar_tensor_tensor(rest[:, :], turns[:, :], -PI_1, ang[:, :], ALU.mult, ALU.add))
            steps.link(v.scalar_tensor_tensor(rest[:, :], turns[:, :], -PI_2, rest[:, :], ALU.mult, ALU.add))
            steps.link(v.scalar_tensor_tensor(rest[:, :], turns[:, :], -PI_3, rest[:, :], ALU.mult, ALU.add))
            steps.link(v.tensor_scalar(rest[:, :], rest[:, :], 3.1415925, -3.1415925, ALU.min, ALU.max))
            steps.link(v.scalar_tensor_tensor(turns[:, :], rest[:, :], -1.0, rest[:, :], ALU.mult, ALU.max))
            v.tensor_scalar(turns[:, :], turns[:, :], -1.0, np.pi / 2, ALU.mult, ALU.add).then_inc(rest_ready, 1)

            def ln_gated(b, name, t):
                wait_y(dve, b, name, t)
                if t == 0:
                    dve.wait_ge(gate_ready, b + 1)
                    if b:
                        dve.wait_ge(x_ready, T)
                steps.link(v.tensor_tensor(hf[:, :], flat2(2 * t), gains[:, 0, :], ALU.mult))

            def ln_stats(t):
                xt = x[:, t, :]
                steps.link(v.scalar_tensor_tensor(xt, xt, ALPHA, hf[:, :], ALU.mult, ALU.add, accum_out=mv[:, t, 1:2]))
                v.tensor_scalar(mv[:, t, 0:1], mv[:, t, 1:2], 1.0 / D, None, ALU.mult).then_inc(ln_stat, 1)

            def ln_factor(n, t):
                dve.wait_ge(sqrt_ready, n)
                steps.link(v.reciprocal(stat[:, t, 2:3], stat[:, t, 1:2]))

            def ln_normal(n, t):
                ln_factor(n, t)
                v.tensor_scalar(x[:, t, :], x[:, t, :], mv[:, t, 0:1], stat[:, t, 2:3], ALU.subtract, ALU.mult).then_inc(norm_ready, 1)

            def ln_affine(n, t):
                dve.wait_ge(gains_in, 80)
                ln_factor(n, t)
                steps.link(v.scalar_tensor_tensor(x[:, t, :], x[:, t, :], mv[:, t, 0:1], gains[:, 1, :], ALU.subtract, ALU.mult))
                v.scalar_tensor_tensor(x[:, t, :], x[:, t, :], stat[:, t, 2:3], gains[:, 2, :], ALU.mult, ALU.add).then_inc(x_ready, 1)

            def low_tile(q, t, b):
                dve.wait_ge(h_high, T * q + t + 1)
                v.tensor_tensor(tile(hL, t), two(b), tile(hH, t).bitcast(F32), ALU.subtract).then_inc(h_ready, 1)

            def prenorm(n, t, g, q, hats):
                dve.wait_ge(sqrt_ready, n)
                if t >= 2:
                    dve.wait_ge(tr_done, T * q + t - 1)
                steps.link(v.reciprocal(stat[:, t, 5:6], stat[:, t, 4:5]))
                v.scalar_tensor_tensor(hats[t % 2][:, :], x[:, t, :], stat[:, t, 5:6], gains[:, g, :], ALU.mult, ALU.mult).then_inc(xhat_ready, 1)

            split_last("eout")
            q = TR["eout"]
            ln_gated(0, "eout", 0)
            ln_stats(0)
            ln_gated(0, "eout", 1)
            ln_stats(1)
            ln_normal(1, 0)
            ln_normal(2, 1)
            ln_gated(0, "eout", 2)
            mod_rest(1, q, 0, tmps[0])
            mod_rest(1, q, 1, tmps[1])
            low_mod(q, 0, tmps[0])
            ln_stats(2)
            low_mod(q, 1, tmps[1])
            ln_normal(3, 2)
            ln_gated(0, "eout", 3)
            ln_stats(3)
            mod_rest(1, q, 2, tmps[0])
            ln_normal(4, 3)
            low_mod(q, 2, tmps[0])
            mod_rest(1, q, 3, tmps[1])
            low_mod(q, 3, tmps[1])
            gate_diag(1, ones1, diag1)

            for t in range(T):
                dve.wait_ge(lat_sqrt, t + 1)
                steps.link(v.reciprocal(stat[:, t, 4:6], stat[:, t, 2:4]))
                v.tensor_scalar(latn[:, t, 0:QR], PS[:, t, 0:QR], stat[:, t, 4:5], None, ALU.mult)
                v.tensor_scalar(latn[:, t, QR:QR + KVR], PS[:, t, QR:QR + KVR], stat[:, t, 5:6], None, ALU.mult)
                for j in range(2):
                    c = QR + KVR + ROPE * j
                    ins = v.tensor_copy(latn[:, t, c:c + ROPE], PS[:, t, QR + KVR:LATENT])
                ins.then_inc(latn_ready, 1)
            for j in range(2):
                dve.wait_ge(lat_ev, j + 1)
                ins = v.scalar_tensor_tensor(qcL[:, j, :], PS[:, 4 + j, :], vec[:, ROWS["q_g"] + j:ROWS["q_g"] + j + 1],
                                             qcH[:, j, :].bitcast(F32), ALU.mult, ALU.subtract)
            ins.then_inc(lat_low, 1)
            dve.wait_ge(lat_ev, 4)
            v.scalar_tensor_tensor(kvL[:, :], PS[:, 6, :], vec[:, ROWS["kv_g"]:ROWS["kv_g"] + 1], kvH[:, :].bitcast(F32),
                                   ALU.mult, ALU.subtract).then_inc(lat_low, 1)
            dve.wait_ge(kr_turn, 1)
            dve.wait_ge(sin_ready, 1)
            v.tensor_tensor(kr[:, :], kraw[:, :], cosM[:, :], ALU.mult)
            steps.link(v.tensor_tensor(qr[:, :], PS[:, 7, :], sinM[:, :], ALU.mult))
            v.tensor_tensor(kr[:, :], kr[:, :], qr[:, :], ALU.add).then_inc(kr_sum, 1)
            dve.wait_ge(kr_high, 1)
            v.tensor_tensor(krL[:, :], kr[:, :], krH[:, :].bitcast(F32), ALU.subtract).then_inc(kr_ready, 1)
            dve.wait_ge(x_ready, T)

            def low_o(h):
                dve.wait_ge(oh_ready, h + 1)
                v.tensor_tensor(oL[:, h, :], oz[:, h, :], oH[:, h, :].bitcast(F32), ALU.subtract).then_inc(ol_ready, 1)

            def attend(i, more):
                dve.wait_ge(qa_ready, i * 2 + 1)
                v.tensor_tensor(qnL[:, :, :], PS[:, 0:2, :], qnH[:, :, :].bitcast(F32), ALU.subtract).then_inc(qn_ready, 1)
                dve.wait_ge(qa_ready, i * 2 + 2)
                steps.link(v.tensor_tensor(qr[:, :], qraw[:, :], cosM[:, :], ALU.mult))
                dve.wait_ge(kn_high, i + 1)
                v.tensor_tensor(knL[:, :, :], PS[:, 4:6, :], knH[:, :, :].bitcast(F32), ALU.subtract)
                dve.wait_ge(q_turn, i + 1)
                steps.link(v.tensor_tensor(qraw[:, :], PS[:, 3, :], sinM[:, :], ALU.mult))
                v.tensor_tensor(qr[:, :], qr[:, :], qraw[:, :], ALU.add).then_inc(qr_sum, 1)
                dve.wait_ge(proj_done, i * 4 + 4)
                v.tensor_copy(vh[:, :, :], PS[:, 6:8, :].rearrange("p a (b n) -> p (a b) n", b=2)).then_inc(kv_ready, 1)
                dve.wait_ge(qr_high, i + 1)
                v.tensor_tensor(qrL[:, :], qr[:, :], qrH[:, :].bitcast(F32), ALU.subtract).then_inc(qr_ready, 1)

                def top(u):
                    q = u % T
                    w = (q + 1) * P
                    sc = PS[:, 2 + u % 2, 0:w]
                    dve.wait_ge(s_done, i * 8 + u + 1)
                    steps.link(v.memset(PS[0:64, 2 + u % 2, q * P + 64:w], MASKED))
                    steps.link(v.reduce_max(soft[:, u % 2, 0, 0:1], sc, AX))
                    v.tensor_scalar(soft[:, u % 2, 1, 0:1], soft[:, u % 2, 0, 0:1], -MLA_SCALE, None, ALU.mult).then_inc(m_ready, 1)

                def norm(u):
                    w = (u % T + 1) * P
                    dve.wait_ge(e_ready, i * 8 + u + 1)
                    steps.link(v.reciprocal(soft[:, u % 2, 3, 0:1], soft[:, u % 2, 2, 0:1]))
                    v.tensor_scalar(pm[u % 2][:, 0:w], pm[u % 2][:, 0:w], soft[:, u % 2, 3, 0:1], None, ALU.mult).then_inc(p_ready, 1)

                top(0)
                top(1)
                for u in range(8):
                    norm(u)
                    if u + 2 < 8:
                        top(u + 2)
                if not more:
                    split_low("oout", 0, 0)
                    low_o(0)
                    low_o(1)
                dve.wait_ge(sz_ready, i + 1 + CREDIT)
                for h in range(2):
                    dve.wait_ge(pv_done, i * 2 + h + 1)
                    v.tensor_tensor(oz[:, i * 2 + h, :], PS[:, 6 + h, :], oz[:, i * 2 + h, :], ALU.mult).then_inc(oz_ready, 1)

            with dve.Fori(0, 7) as i:
                steps.loop(i, 2 + 8 * 3)
                attend(i, True)
            steps.done(7)
            attend(7, False)

            dve.wait_ge(oz_ready, HEADS + CREDIT)
            for h in range(2, HEADS):
                low_o(h)

            split_last("oout")
            n, q = T, TR["oout"]
            ln_gated(1, "oout", 0)
            ln_stats(0)
            ln_gated(1, "oout", 1)
            ln_stats(1)
            ln_affine(n + 1, 0)
            ln_affine(n + 2, 1)
            prenorm(n + 3, 0, 3, q, x_hat1)
            ln_gated(1, "oout", 2)
            prenorm(n + 4, 1, 3, q, x_hat1)
            low_tile(q, 0, 0)
            ln_stats(2)
            low_tile(q, 1, 2)
            ln_gated(1, "oout", 3)
            ln_affine(n + 5, 2)
            ln_stats(3)
            prenorm(n + 6, 2, 3, q, x_hat1)
            ln_affine(n + 7, 3)
            prenorm(n + 8, 3, 3, q, x_hat1)
            low_tile(q, 2, 4)
            low_tile(q, 3, 6)
            n += 2 * T

            split_low("cu", 1, 0)
            steps.link(v.memset(cw[:, 0:2], 0.0))
            with dve.Fori(0, 4) as i:
                steps.loop(i, 2 * 3)
                for s in range(2):
                    f = i * 2 + s

                    def tap(j):
                        return vec[:, bass.ds(f + (ROWS["conv"] + K * j), 1)]

                    dve.wait_ge(sg_ready, SG["cu"] + f + 1)
                    v.tensor_tensor(cw[:, 2:], buf[s][:, :], PS[:, 2 * s + 1, :], ALU.mult).then_inc(pair_free[s], 1)
                    dve.wait_ge(pair_free[s], PF["cu"] + i + 1)
                    steps.link(v.tensor_scalar(cv[:, :], cw[:, 0:S], tap(0), None, ALU.mult))
                    steps.link(v.scalar_tensor_tensor(cv[:, :], cw[:, 1:1 + S], tap(1), cv[:, :], ALU.mult, ALU.add))
                    steps.link(v.scalar_tensor_tensor(yc[:, f, :], cw[:, 2:], tap(2), cv[:, :], ALU.mult, ALU.add))
            steps.done(4)
            B = BASE["b"]
            with dve.Fori(0, 2) as i:
                for s in range(2):
                    dve.wait_ge(used[s], B.use[s] + i + 1)
                    for m in range(2):
                        f = i * 4 + (2 * s + m)
                        dve.wait_ge(gate_low, GATED["b"] + f + 1)
                        v.tensor_tensor(buf[m][:, :], PS[:, 2 * s + m, :], yc[:, f, :], ALU.mult).then_inc(prod_ready, 1)
                    for m in range(2):
                        f = i * 4 + (2 * s + m)
                        dve.wait_ge(act_high, GATED["b"] + f + 1)
                        v.tensor_tensor(yL[:, f, :], buf[m][:, :], yH[:, f, :].bitcast(F32), ALU.subtract).then_inc(gate_low, 1)
                    dve.sem_inc(pair_free[s], 1)

            def boundary(name, n, pre, loaded):
                b = BOUNDARY.index(name)
                split_last(name)
                dve.wait_ge(gains_in, loaded)

                def residual(n, t):
                    dve.wait_ge(sqrt_ready, n)
                    blocks = x[:, t, :].rearrange("p (k t) -> p k t", t=P)
                    tmp = tile(scaled, t)
                    steps.link(v.reciprocal(stat[:, t, 2:3], stat[:, t, 1:2]))
                    steps.link(v.scalar_tensor_tensor(tmp, two(2 * t), stat[:, t, 2:3], gains[:, 0, :].rearrange("p (k t) -> p k t", t=P),
                                                      ALU.mult, ALU.mult))
                    v.tensor_tensor(blocks, blocks, tmp, ALU.add).then_inc(x_ready, 1)

                if not pre:
                    for t in range(T):
                        residual(n + t + 1, t)
                    return n + T
                q = TR[name]
                residual(n + 1, 0)
                residual(n + 2, 1)
                prenorm(n + 3, 0, 1, q, x_hat)
                prenorm(n + 4, 1, 1, q, x_hat)
                low_tile(q, 0, 0)
                low_tile(q, 1, 2)
                residual(n + 5, 2)
                split_half(NAMES[NAMES.index(name) + 1])
                residual(n + 6, 3)
                prenorm(n + 7, 2, 1, q, x_hat)
                prenorm(n + 8, 3, 1, q, x_hat)
                low_tile(q, 2, 4)
                low_tile(q, 3, 6)
                return n + 2 * T

            n = boundary("aout", n, True, 112)
            split_low("gu0", 1, 0)
            gated("gu0", fL)
            split_low("dn0", 1, 0)
            n = boundary("dn0", n, True, 160)

            q = TR["q"]

            def query_norm(t):
                if t >= 2:
                    dve.wait_ge(tr_done, T * q + t - 1)
                v.scalar_tensor_tensor(x_hat[t % 2][:, :], x[:, t, :], stat[:, t, 5:6], gains[:, 2, :], ALU.mult, ALU.mult).then_inc(xhat_ready, 1)

            query_norm(0)
            query_norm(1)
            dve.wait_ge(used[0], end_use("kv", 0))
            v.tensor_copy(vall[:, :, :], PS[:, 0:2, :].rearrange("p a (b n) -> p (a b) n", b=2)).then_inc(v2_ready, 1)
            query_norm(2)
            query_norm(3)
            cos2 = cosB.unsqueeze(1).broadcast_to((P, 2, S))
            sin2 = sinB.unsqueeze(1).broadcast_to((P, 2, S))

            def rotate(dst, bank, raw_ready, turned, n):
                dve.wait_ge(raw_ready, n)
                v.tensor_tensor(dst[:, :, :], q2raw[:, :, :], cos2, ALU.mult)
                dve.wait_ge(turned, n)
                steps.link(v.tensor_tensor(q2tmp[:, :, :], PS[:, bank:bank + 2, :], sin2, ALU.mult))
                return v.tensor_tensor(dst[:, :, :], dst[:, :, :], q2tmp[:, :, :], ALU.add)

            dve.wait_ge(late_in, 48)
            low_tile(q, 0, 4)
            low_tile(q, 1, 6)
            rotate(q2[1], 2, k2_raw, k2_turn, 1).then_inc(k2_rot, 1)
            low_tile(q, 2, 4)
            low_tile(q, 3, 6)

            def top2(n):
                g, w = n // T, 0 if n % T else P
                st = soft[:, n % 2, :, :]

                def pairs(c):
                    return st[:, c, :].rearrange("p (o j) -> p o j", o=2)

                sink = sinks[:, g * GROUP:(g + 1) * GROUP].rearrange("p (j o) -> p o j", o=2)
                sc = p2[n % 3][:, :, w:]
                dve.wait_ge(s2_done, n + 1)
                if n >= 3:
                    dve.wait_ge(t2_done, n - 2)
                steps.link(v.tensor_tensor(sc, two(2).rearrange("p (h k) t -> p h (k t)", h=GROUP)[:, :, w:],
                                           window[:, w:].unsqueeze(1).broadcast_to((P, GROUP, 2 * P - w)), ALU.add))
                steps.link(v.reduce_max(st[:, 0, :], sc, AX))
                steps.link(v.scalar_tensor_tensor(pairs(1), pairs(0), SW_SCALE, sink, ALU.mult, ALU.max))
                v.tensor_tensor(pairs(3), sink, pairs(1), ALU.subtract)
                v.tensor_scalar(st[:, 2, :], st[:, 1, :], -1.0, None, ALU.mult).then_inc(m2_ready, 1)

            def norm2(n):
                w = 0 if n % T else P
                st = soft[:, n % 2, :, :]
                dve.wait_ge(e2_ready, n + 1)
                steps.link(v.tensor_tensor(st[:, 6, :], st[:, 5, :], st[:, 4, :], ALU.add))
                steps.link(v.reciprocal(st[:, 7, :], st[:, 6, :]))
                pr = p2[n % 3][:, :, w:]
                v.tensor_tensor(pr, pr, st[:, 7, :].unsqueeze(2).broadcast_to((P, GROUP, 2 * P - w)), ALU.mult).then_inc(p2_ready, 1)

            def low_out(g):
                for j in range(2):
                    dve.wait_ge(o2_high, g * 2 + j + 1)
                    v.tensor_tensor(o2L[:, g * 2 + j, :], PS[:, 6 + j, :], o2H[:, g * 2 + j, :].bitcast(F32), ALU.subtract).then_inc(o2_low, 1)

            rotate(q2[0], 6, q2_raw, q2_turn, 1).then_inc(q2_ready, 1)
            top2(0)
            for n2 in range(UNITS):
                g, b = n2 // T, n2 % T
                if n2 + 1 < UNITS:
                    top2(n2 + 1)
                if b == 1 and g + 1 < KVH:
                    dve.wait_ge(q2_turn, g + 2)
                    dve.wait_ge(q2_ready, g + 1)
                    v.tensor_tensor(q2tmp[:, :, :], PS[:, 0:2, :], sin2, ALU.mult).then_inc(q2_sin, 1)
                if b == 1 and g:
                    low_out(g - 1)
                norm2(n2)
            low_out(KVH - 1)
            n = boundary("wo", n, True, 192)
            split_low("gu1", 1, 0)
            gated("gu1", fL)
            split_low("dn1", 1, 0)
            n = boundary("dn1", n, False, 208)

        @block.tensor
        def _(pe):
            mm, tr = nc.tensor.matmul, nc.tensor.transpose

            def mm3(dst, lh, ll, rh, rl, first, last):
                mm(dst, lh, rh, start=first, stop=False, skip_group_check=True)
                mm(dst, lh, rl, start=False, stop=False, skip_group_check=True)
                return mm(dst, ll, rh, start=False, stop=last, skip_group_check=True)

            def wcols(w, s):
                return w[s][:, :].rearrange("p (k n) -> p k n", n=256)

            def in_stage(name, turns=None):
                B = BASE[name]

                def chunk(s, tok, tiles=(0, 1)):
                    for m in tiles:
                        for k in range(K):
                            c = slice(m * P, (m + 1) * P)
                            ins = mm3(PS[:, 2 * s + m, tok], wcols(WH, s)[:, k, c], wcols(WL, s)[:, k, c],
                                      hH[:, k, tok], hL[:, k, tok], k == 0, k == K - 1)
                    return ins

                if turns:
                    q, turn = turns
                    pe.wait_ge(h_ready, T * q + 2)
                    for s in range(2):
                        pe.wait_ge(w_split[s], B.split[s] + 1)
                        pe.wait_ge(pair_free[s], PF[name])
                        for m in range(2):
                            chunk(s, slice(0, S // 2), (m,))
                            if name == "cu" and s == 0 and m == 1:
                                turn(2)
                            if s == 1 and m == (name == "cu"):
                                if name != "cu":
                                    turn(2)
                                turn(3)
                    pe.wait_ge(h_ready, T * q + 4)
                    for s in range(2):
                        chunk(s, slice(S // 2, S)).then_inc(used[s], 1)
                with pe.Fori(1 if turns else 0, B.pairs) as i:
                    for s in range(2):
                        pe.wait_ge(w_split[s], B.split[s] + i + 1)
                        pe.wait_ge(pair_free[s], PF[name] + i)
                        ins = chunk(s, slice(0, S))
                        if name == "xb":
                            pe.wait_ge(v_left, 2)
                        if name in ADA_AT:
                            for m in range(2):
                                pe.wait_ge(ada_sum[m], i * 2 + (ADA_AT[name] + s + 1 + CREDIT))
                                ins = mm(PS[:, 4, 2 * s + m:2 * s + m + 1], ada_acc[m][:, :], one_col, start=True, stop=True)
                        ins.then_inc(used[s], 1)

            def out_stage(name, lh, ll, ready, bank_ready, first_depth=2, turn=None, order=(2, 3, 0, 1)):
                B = BASE[name]
                kt = 0
                pairs = B.pairs

                def tiles(kt, s, d, t, first, last):
                    for n in range(2):
                        c = slice(d * D + n * S, d * D + (n + 1) * S)
                        ins = mm3(PS[:, 2 * t + n, :], lh[:, kt, t * P:(t + 1) * P], ll[:, kt, t * P:(t + 1) * P],
                                  WH[s][:, c], WL[s][:, c], first, last)
                    return ins

                for j in range(pairs - 1):
                    depth = first_depth if j == 0 else 2
                    for s in range(2):
                        pe.wait_ge(w_split[s], B.split[s] + j + 1)
                        if kt == 0:
                            ready(depth - 1)
                            for t in order:
                                bank_ready(t)
                                for d in range(depth):
                                    ins = tiles(d, s, d, t, d == 0, False)
                        else:
                            for d in range(depth):
                                ready(kt + d)
                                for t in range(T):
                                    ins = tiles(kt + d, s, d, t, False, False)
                        kt += depth
                        ins.then_inc(used[s], 1)

                def part(s, t):
                    for d in range(2):
                        ins = tiles(kt + 2 * s + d, s, d, t, False, s == 1 and d == 1)
                    return ins

                pe.wait_ge(w_split[0], B.split[0] + pairs)
                ready(kt + 1)
                for t in range(2):
                    part(0, t)
                pe.wait_ge(w_split[1], B.split[1] + pairs)
                ready(kt + 3)
                for t in range(2):
                    part(1, t).then_inc(y_ready, 1)
                part(0, 2)
                part(0, 3).then_inc(used[0], 1)
                part(1, 2).then_inc(y_ready, 1)
                if turn and name != "oout":
                    turn(0)
                    turn(1)
                part(1, 3).then_inc(used[1], 1)
                if name == "oout":
                    turn(0)
                    turn(1)

            def turn_tile(q, t, src, ready, b=None):
                ready(t)
                for k in range(K):
                    ins = tr(two(2 * t if b is None else b)[:, k, :], src[:, k * P:(k + 1) * P], ident)
                ins.then_inc(tr_done, 1)

            pe.wait_ge(small_in, 16 * 3)
            tr(PS[:, 7, 0:N_FIRST], rows[0:N_FIRST, :], ident[0:N_FIRST, 0:N_FIRST]).then_inc(rows_tr, 1)
            for c in range(ADA_FIRST):
                pe.wait_ge(ada_first, K * (c + 1))
                for m in range(2):
                    for j in range(2):
                        ins = mm(PS[:, 7, 256 + 2 * c + m:257 + 2 * c + m], ada_part[c][:, j, m * P:(m + 1) * P], one_col, start=(j == 0), stop=(j == 1))
            ins.then_inc(ada_done, 1)
            for t in range(T):
                if t == T - 1:
                    pe.wait_ge(mod_ready, 1)
                turn_tile(0, t, x[:, t, :], lambda t: pe.wait_ge(x_in[t], 16))

            def left(name):
                return lambda t: pe.wait_ge(pair_free[t], PF[name]) if t < 2 else None

            def gate_rows(n, one, dg, b):
                pe.wait_ge(diag_ready, n)
                for k in range(K):
                    ins = mm(two(b)[:, k, :], one[:, :], dg[:, k, :], start=True, stop=True)
                ins.then_inc(gate_mm, 1)

            B = BASE["v"]
            for c in range(4):
                n, s = c // 2, c % 2
                if c == 2:
                    pe.wait_ge(rest_in, 16 * 8)
                    tr(PS[:, 7, 0:N_ROWS], rows[0:N_ROWS, :], ident[0:N_ROWS, 0:N_ROWS]).then_inc(rows_tr, 1)
                    for h in range(G_HEADS):
                        ins = tr(PS[:, 6, h * P:(h + 1) * P], ws_sb[:, h, :], ident)
                    ins.then_inc(ws_tr, 1)
                pe.wait_ge(w_split[s], B.split[s] + n + 1)
                for t in range(T):
                    if c == 0:
                        pe.wait_ge(h_ready, t + 1)
                    if c == 2 and t == 2:
                        pe.wait_ge(wT_ready, 1)
                    for k in range(4):
                        kt = 4 * s + k
                        w = slice(k * S, (k + 1) * S)
                        ins = mm3(PS[:, 4 * n + t, :], hH[:, kt, t * P:(t + 1) * P], hL[:, kt, t * P:(t + 1) * P],
                                  WH[s][:, w], WL[s][:, w], kt == 0, kt == K - 1)
                ins.then_inc(used[s], 1)
            pe.wait_ge(v_left, 1)
            in_stage("xb")
            pe.wait_ge(vn_ready, 2)
            pe.wait_ge(wT_ready, 1)
            pe.wait_ge(ada_col, ADA_AT["zu"])
            for f in range(K):
                if f == 4:
                    pe.wait_ge(pair_free[0], PF["zu"])
                if f >= 6:
                    pe.wait_ge(sv_ready, f - 4)
                for b in range(T):
                    ins = mm(PS[:, SIDE[f], b * P:(b + 1) * P], vn[:, b, f * P:(f + 1) * P], wT[:, f // 2, :], start=True, stop=True)
                ins.then_inc(sp_done, 1)
            pe.wait_ge(sv_ready, 6)
            in_stage("zu")
            B = BASE["pool"]
            pe.wait_ge(pool_low, 1)
            pe.wait_ge(ada_col, ADA_AT["zb"])
            for f in range(K):
                g, m, s = f // 2, f % 2, f // 4
                if f % 4 == 0:
                    pe.wait_ge(w_split[s], B.split[s] + 1)
                if f == 4:
                    pe.wait_ge(pair_free[0], PF["zb"])
                if f >= 6:
                    pe.wait_ge(yb_ready, f - 4)
                for k in range(2):
                    c = (2 * (g % 2) + k) * 256 + m * P
                    ins = mm3(PS[:, SIDE[f], :], WH[s][:, c:c + P], WL[s][:, c:c + P], poolH[:, 2 * g + k, :], poolL[:, 2 * g + k, :], k == 0, k == 1)
                ins.then_inc(used[s] if f % 4 == 3 else py_done, 1)
            pe.wait_ge(yb_ready, 6)
            in_stage("zb")
            pe.wait_ge(ada_col, ADA_END)
            gate_rows(1, ones, diag, 6)
            def turn_norm(t):
                turn_tile(TR["eout"], t, x[:, t, :], lambda t: pe.wait_ge(norm_ready, t + 1))

            out_stage("eout", mixH, mixL, lambda kt: pe.wait_ge(gate_low, 2 + kt + 1),
                      lambda t: pe.wait_ge(gate_ready, 1) if t == 3 else left("cu")(t), turn=turn_norm)

            B = BASE["lat"]

            def latents(t, s):
                if s == 0:
                    pe.wait_ge(h_ready, T + t + 1)
                pe.wait_ge(w_split[s], B.split[s] + 1)
                for k in range(4):
                    kt = 4 * s + k
                    w = slice(k * S, k * S + LATENT)
                    ins = mm3(PS[:, t, 0:LATENT], hH[:, kt, t * P:(t + 1) * P], hL[:, kt, t * P:(t + 1) * P],
                              WH[s][:, w], WL[s][:, w], kt == 0, kt == K - 1)
                return ins

            latents(0, 0)
            latents(1, 0)
            turn_norm(2)
            latents(0, 1).then_inc(lat_done, 1)
            latents(1, 1).then_inc(lat_done, 1)
            turn_norm(3)
            latents(2, 0)
            latents(2, 1).then_inc(lat_done, 1)
            latents(3, 0).then_inc(used[0], 1)
            latents(3, 1).then_inc(used[1], 1)
            pe.wait_ge(h_ready, 2 * T)
            for t in range(T):
                pe.wait_ge(latn_ready, t + 1)
                for j in range(4):
                    ins = tr(PS[:, 4 + j, t * P:(t + 1) * P], latn[:, t, j * P:(j + 1) * P], ident)
            ins.then_inc(lat_tr, 1)
            gate_rows(2, ones1, diag1, 2)
            pe.wait_ge(lat_ev, 3)
            pe.wait_ge(late_in, 32)
            mm(PS[:, 7, :], turn_m[:, :], kraw[:, :], start=True, stop=True).then_inc(kr_turn, 1)
            pe.wait_ge(lat_low, 1)

            B = BASE["mla"]

            def part(c, n, pattern, **sizes):
                return [w[1][:, c:c + n].rearrange(pattern, **sizes) if pattern else w[1][:, c:c + n] for w in (WH, WL)]

            wnH, wnL = part(0, 512, "p (k h e) -> p k h e", k=2, h=2)
            wrH, wrL = part(512, 256, "p (k m) -> p k m", k=2)
            wkH, wkL = part(768, 256, "p (h e) -> p h e", h=2)
            wvH, wvL = part(1024, 256, None)
            with pe.Fori(0, 8) as i:
                pe.wait_ge(w_split[1], B.split[1] + i + 1)
                pe.wait_ge(sz_ready, i + CREDIT)
                for h in range(2):
                    for k in range(2):
                        ins = mm3(PS[:, h, :], wnH[:, k, h, :], wnL[:, k, h, :], qcH[:, k, :], qcL[:, k, :], k == 0, k == 1)
                ins.then_inc(proj_done, 1)
                pe.wait_ge(gate_ready, 2)
                for k in range(2):
                    ins = mm3(PS[:, 2, :], wrH[:, k, :], wrL[:, k, :], qcH[:, k, :], qcL[:, k, :], k == 0, k == 1)
                ins.then_inc(proj_done, 1)
                pe.wait_ge(lat_low, 2)
                for h in range(2):
                    ins = mm3(PS[:, 4 + h, :], wkH[:, h, :], wkL[:, h, :], kvH[:, :], kvL[:, :], True, True)
                ins.then_inc(proj_done, 1)
                pe.wait_ge(qa_ready, i * 2 + 2)
                pe.wait_ge(kr_ready, 1)
                mm(PS[:, 3, :], turn_m[:, :], qraw[:, :], start=True, stop=True).then_inc(q_turn, 1)
                pe.wait_ge(oz_ready, i * 2 + CREDIT)
                for t in range(T):
                    ins = mm3(PS[:, 6 + t // 2, (t % 2) * 256:(t % 2 + 1) * 256], kvH[:, t * P:(t + 1) * P], kvL[:, t * P:(t + 1) * P],
                              wvH, wvL, True, True)
                ins.then_inc(proj_done, 1)
                pe.wait_ge(proj_done, i * 4 + 4)
                pe.sem_inc(used[1], 1)
                pe.wait_ge(w_split[0], B.split[0] + i + 1)
                pe.wait_ge(qn_ready, i + 1)

                def z_parts(first, last):
                    for j in range(first, last):
                        m, k = j // K, j % K
                        c = slice(m * P, (m + 1) * P)
                        ins = mm3(PS[:, m, :], wcols(WH, 0)[:, k, c], wcols(WL, 0)[:, k, c], hH[:, k, :], hL[:, k, :],
                                  k == 0, k == K - 1)
                    if first < last == 2 * K:
                        ins.then_inc(used[0], 1)

                def score(u):
                    h, q = u // T, u % T
                    w = (q + 1) * P
                    if u >= 2:
                        pe.wait_ge(e_ready, i * 8 + u - 1)
                    rp = slice(h * ROPE, (h + 1) * ROPE)
                    mm3(PS[:, 2 + u % 2, 0:w], qnH[:, h, q * P:w], qnL[:, h, q * P:w], knH[:, h, 0:w], knL[:, h, 0:w], True, False)
                    mm3(PS[:, 2 + u % 2, 0:w], qrH[rp, q * P:w], qrL[rp, q * P:w], krH[rp, 0:w], krL[rp, 0:w], False, True).then_inc(s_done, 1)

                def turn(u):
                    q = u % T
                    if u >= 2:
                        pe.wait_ge(pT_ready, i * 8 + u - 1)
                    pe.wait_ge(p_ready, i * 8 + u + 1)
                    for k in range(q + 1):
                        ins = tr(PS[:, 4 + u % 2, k * P:(k + 1) * P], pm[u % 2][:, k * P:(k + 1) * P], ident)
                    ins.then_inc(t_done, 1)

                def weigh(h):
                    pe.wait_ge(kv_ready, i + 1)
                    pe.wait_ge(pT_ready, i * 8 + T * h + T)
                    for k in range(T):
                        ins = mm(PS[:, 6 + h, k * P:], vh[:, k, h * NOPE:(h + 1) * NOPE], pT[h][:, k, k * P:],
                                 start=(k == 0), stop=(k == T - 1), skip_group_check=True)
                    ins.then_inc(pv_done, 1)

                Z = (0, 4, 6, 8, 10, 12, 14, 15, 15, 16, 16)
                z_parts(0, Z[1])
                pe.wait_ge(qr_ready, i + 1)
                score(0)
                score(1)
                z_parts(Z[1], Z[2])
                for u in range(8):
                    turn(u)
                    if u + 2 < 8:
                        score(u + 2)
                    if u == 5:
                        weigh(0)
                    z_parts(Z[u + 2], Z[u + 3])
                weigh(1)

            def attended(t):
                if t == 0:
                    pe.wait_ge(sz_ready, 8 + CREDIT)
                if t == 3:
                    pe.wait_ge(oz_ready, HEADS + CREDIT)

            def turner(name, n, hats):
                q = TR[name]
                return lambda t: turn_tile(q, t, hats[t % 2], lambda t: pe.wait_ge(xhat_ready, n * T + t + 1))

            turn = turner("oout", 0, x_hat1)
            out_stage("oout", oH, oL, lambda kt: pe.wait_ge(ol_ready, kt + 1), attended, turn=turn, order=(2, 1, 0, 3))
            in_stage("cu", (TR["oout"], turn))
            in_stage("b")
            turn = turner("aout", 1, x_hat)
            out_stage("aout", yH, yL, lambda kt: pe.wait_ge(gate_low, 2 + GATED["b"] + kt + 1), left("gu0"), turn=turn)
            in_stage("gu0", (TR["aout"], turn))
            turn = turner("dn0", 2, x_hat)
            out_stage("dn0", fH, fL, lambda kt: pe.wait_ge(gate_low, 2 + GATED["gu0"] + kt + 1), left("gu1"), 1, turn=turn)

            B = BASE["kv"]

            def values(t):
                pe.wait_ge(h_ready, T * TR["q"] - T + t + 1)
                for k in range(K):
                    ins = mm3(PS[:, t // 2, (t % 2) * 256:(t % 2 + 1) * 256], hH[:, k, t * P:(t + 1) * P], hL[:, k, t * P:(t + 1) * P],
                              wcols(WH, 0)[:, k, :], wcols(WL, 0)[:, k, :], k == 0, k == K - 1)
                return ins

            def keys(tok, tiles=(0, 1)):
                for m in tiles:
                    for k in range(K):
                        c = slice(m * P, (m + 1) * P)
                        ins = mm3(PS[:, 2 + m, tok], wcols(WH, 1)[:, k, c], wcols(WL, 1)[:, k, c], hH[:, k, tok], hL[:, k, tok], k == 0, k == K - 1)
                return ins

            pe.wait_ge(w_split[0], B.split[0] + 1)
            values(0)
            values(1)
            pe.wait_ge(w_split[1], B.split[1] + 1)
            keys(slice(0, S // 2), (0,))
            turn(2)
            keys(slice(0, S // 2), (1,))
            turn(3)
            values(2)
            values(3).then_inc(used[0], 1)

            def turn_queries(t):
                if t >= 2:
                    pe.wait_ge(h_ready, T * TR["q"] + t - 1)
                turn_tile(TR["q"], t, x_hat[t % 2], lambda t: pe.wait_ge(xhat_ready, 3 * T + t + 1), 4 + 2 * (t % 2))

            turn_queries(0)
            turn_queries(1)
            keys(slice(S // 2, S)).then_inc(used[1], 1)
            turn_queries(2)
            turn_queries(3)
            pe.wait_ge(k2_raw, 1)
            pe.wait_ge(late_in, 48)
            for m in range(2):
                ins = mm(PS[:, 2 + m, :], turn_b, q2raw[:, m, :], start=True, stop=True)
            ins.then_inc(k2_turn, 1)

            B = BASE["q"]

            def queries(g, first, last, tok=slice(0, S)):
                s = g % 2
                if first == 0:
                    pe.wait_ge(w_split[s], B.split[s] + g // 2 + 1)
                    if g >= 2:
                        pe.wait_ge(q2_sin, g - 1)
                for j in range(first, last):
                    m, k = j // K, j % K
                    c = slice(m * P, (m + 1) * P)
                    ins = mm3(PS[:, m, tok], wcols(WH, s)[:, k, c], wcols(WL, s)[:, k, c], hH[:, k, tok], hL[:, k, tok], k == 0, k == K - 1)
                if last == 2 * K and tok.stop == S:
                    ins.then_inc(used[s], 1)

            def partners(g):
                pe.wait_ge(q2_raw, g + 1)
                for m in range(2):
                    ins = mm(PS[:, m if g else 6 + m, :], turn_b, q2raw[:, m, :], start=True, stop=True)
                ins.then_inc(q2_turn, 1)

            def score2(n):
                g, b = n // T, n % T
                if b == 0:
                    pe.wait_ge(q2_ready, g + 1)
                if n:
                    pe.wait_ge(m2_ready, n)
                lo = max(b - 1, 0) * P
                for h in range(GROUP):
                    r = slice((h % 2) * HD, (h % 2 + 1) * HD)
                    c = (h // 2) * 2 * P
                    ins = mm(PS[:, 2 + h % 2, c + (0 if b else P):c + 2 * P], q2[g % 2][r, h // 2, b * P:(b + 1) * P],
                             kdup[r, g, lo:(b + 1) * P], start=True, stop=True)
                ins.then_inc(s2_done, 1)

            def turn2(n):
                if n:
                    pe.wait_ge(p2T_ready, n)
                pe.wait_ge(p2_ready, n + 1)
                for h in range(GROUP):
                    for k in range(0 if n % T else 1, 2):
                        ins = tr(two(4)[:, 2 * h + k, :], p2[n % 3][:, h, k * P:(k + 1) * P], ident)
                ins.then_inc(t2_done, 1)

            def weigh2(n):
                g, b = n // T, n % T
                if b == 0 and g:
                    pe.wait_ge(o2_low, 2 * g)
                pe.wait_ge(p2T_ready, n + 1)
                for h in range(GROUP):
                    o, j = h // 2, h % 2
                    ks = range(0 if b else 1, 2)
                    for k in ks:
                        ins = mm(PS[o * HD:(o + 1) * HD, 6 + j, b * P:(b + 1) * P], vall[:, b - 1 + k, g * HD:(g + 1) * HD],
                                 p2T[n % 2][:, 2 * h + k, :], start=(k == ks[0]), stop=(k == 1), skip_group_check=True)
                ins.then_inc(pv2_done, 1)

            pe.wait_ge(v2_ready, 1)
            pe.wait_ge(h_ready, T * TR["q"] + 2)
            queries(0, 0, 2 * K, slice(0, S // 2))
            pe.wait_ge(h_ready, T * TR["q"] + 4)
            queries(0, 0, 2 * K, slice(S // 2, S))
            partners(0)
            queries(1, 0, 6)
            pe.wait_ge(kd_ready, 1)
            score2(0)
            queries(1, 6, 11)
            score2(1)
            queries(1, 11, 2 * K)
            for n in range(UNITS):
                g, b = n // T, n % T
                if n + 2 < UNITS:
                    score2(n + 2)
                if b == 0 and g + 1 < KVH:
                    partners(g + 1)
                if b == 1 and g + 2 < KVH:
                    queries(g + 2, 0, 5)
                turn2(n)
                if n:
                    weigh2(n - 1)
                if b >= 2 and g + 2 < KVH:
                    queries(g + 2, *((5, 10), (10, 2 * K))[b - 2])
            weigh2(UNITS - 1)
            turn = turner("wo", 4, x_hat)
            out_stage("wo", o2H, o2L, lambda kt: pe.wait_ge(o2_low, kt + 1),
                      lambda t: pe.wait_ge(o2_low, K) if t == 3 else None, turn=turn)
            in_stage("gu1", (TR["wo"], turn))
            out_stage("dn1", fH, fL, lambda kt: pe.wait_ge(gate_low, 2 + GATED["gu1"] + kt + 1), left("end"), 1)


_LAYOUT = [
    ("x", "x", (S, D)), ("c", "c", (1, D)), ("positions", "positions", (1, S)),
    ("ada_w", "ada_w", (DEPTH, D, 3 * D)), ("ada_b", "ada_b", (DEPTH, 3 * D)), ("ln_g", "ln_g", (DEPTH, D)), ("ln_b", "ln_b", (DEPTH, D)),
    ("e_w_in", "e_w_in", (D, 5 * D)), ("gmlp_norm_g", "gmlp_norm_g", (1, G_DIM)), ("gmlp_norm_b", "gmlp_norm_b", (1, G_DIM)),
    ("gmlp_ws", "gmlp_ws", (G_HEADS, P, P)), ("gmlp_bs", "gmlp_bs", (1, G_HEADS * P)), ("pool_w", "pool_w", (4, 256, 256)),
    ("pool_b", "pool_b", (1, D)), ("pool_scale", "pool_scale", (1, D)), ("e_w_out", "e_w_out", (2 * D, D)),
    ("o_w_in", "o_w_in", (D, LATENT + HEADS * NOPE)), ("mla_q_norm_g", "q_g", (1, QR)), ("mla_kv_norm_g", "kv_g", (1, KVR)),
    ("mla_w_uq", "mla_w_uq", (QR, HEADS, NOPE + ROPE)), ("mla_w_uk", "mla_w_uk", (KVR, HEADS, NOPE)),
    ("mla_w_uv", "mla_w_uv", (KVR, HEADS, NOPE)), ("o_w_out", "o_w_out", (2 * D, D)),
    ("a_pre_norm_2", "a_pre", (1, D)), ("a_w_in_2", "a_w_in", (D, 3 * D)), ("a_conv_w_2", "conv", (3, D)), ("a_w_out_2", "a_w_out", (D, D)),
    ("a_post_norm_2", "a_post", (1, D)), ("ffn_pre_norm_2", "f_pre", (DEPTH, D)), ("ffn_w_gate_up_2", "f_gate_up", (DEPTH, D, 2 * D_FF)),
    ("ffn_w_down_2", "f_down", (DEPTH, D_FF, D)), ("ffn_post_norm_2", "f_post", (DEPTH, D)), ("kv_norm_2", "kv_norm", (1, D)),
    ("w_kv_2", "w_kv", (D, 2 * KVH * HD)), ("b_pre_norm_2", "b_pre", (1, D)), ("b_w_q_2", "b_w_q", (D, D)), ("b_sinks_2", "b_sinks", (1, 16)),
    ("b_w_o_2", "b_w_o", (D, D)), ("b_post_norm_2", "b_post", (1, D)),
]


def kernel(**inputs):
    import numpy as _np
    import concourse.bacc as _bacc
    from concourse import mybir as _mybir
    from concourse.bass_utils import run_bass_kernel_spmd as _run

    nc = _bacc.Bacc("TRN2", target_bir_lowering=False, num_devices=1)
    arrays, args = {}, {}
    given = [(name, _np.ascontiguousarray(inputs[src]).reshape(shape)) for src, name, shape in _LAYOUT]
    for name, value in given + list(constants().items()):
        arrays[f"in_{name}"] = value
        args[name] = nc.dram_tensor(f"in_{name}", value.shape, _mybir.dt.from_np(value.dtype), kind="ExternalInput").ap()
    out = nc.dram_tensor("out_x", (S, D), F32, kind="ExternalOutput").ap()
    program(nc, args, out)
    r = _run(nc, [arrays], core_ids=[0])
    return r.results[0]["out_x"].reshape(1, S, D)
```
